# Optimizing a Trainium2 kernel written in Bass

```python
import math
import jax, jax.numpy as jnp
from jax import lax
import numpy as np

D_MODEL = 1024
BATCH = 1
SEQ = 512
DEPTH = 1

D_MIX = D_MODEL
NSA_HEADS = 8
NSA_KV_GROUPS = 2
NSA_HEAD_DIM = 64
NSA_HPG = NSA_HEADS // NSA_KV_GROUPS
CMP_BLOCK = 32
CMP_STRIDE = 16
CMP_HIDDEN = 256
SLC_BLOCK = 64
SLC_TOPK = 8
WINDOW = 512
FORCE_SCORE = 1e4
GLA_HEADS = 4
GLA_DK = 64
GLA_DV = 128
GLA_GATE_RANK = 16
GLA_TAU = 16.0
GLA_CHUNK = 64
ROPE_THETA = 500000.0
ROT_DIM = NSA_HEAD_DIM // 4
D_FF = 2816
CONV_W = 3
EPS = 1e-6
Q_BLOCK = 64
NEG = -1e30

NSA_Q_W = NSA_HEADS * NSA_HEAD_DIM
NSA_KV_W = NSA_KV_GROUPS * NSA_HEAD_DIM
GLA_QK_W = GLA_HEADS * GLA_DK
GLA_V_W = GLA_HEADS * GLA_DV
IN_SPLITS = [NSA_Q_W, 6 * NSA_KV_W, 3 * NSA_HEADS, GLA_QK_W, GLA_QK_W, GLA_V_W, GLA_GATE_RANK, GLA_V_W]
D_IN = sum(IN_SPLITS)


def rms_norm(x, g):
    xf = x.astype(jnp.float32)
    y = xf * lax.rsqrt(jnp.mean(xf * xf, axis=-1, keepdims=True) + EPS)
    return (y * g.astype(jnp.float32)).astype(x.dtype)

def partial_rope(x, pos):
    half = ROT_DIM // 2
    inv = ROPE_THETA ** (-jnp.arange(half, dtype=jnp.float32) / half)
    ang = pos.astype(jnp.float32)[:, None] * inv[None, :]
    cos = jnp.cos(ang)[:, None, :]
    sin = jnp.sin(ang)[:, None, :]
    xr = x[..., :ROT_DIM].astype(jnp.float32)
    x1, x2 = xr[..., :half], xr[..., half:]
    rot = jnp.concatenate([x1 * cos - x2 * sin, x2 * cos + x1 * sin], axis=-1).astype(x.dtype)
    return jnp.concatenate([rot, x[..., ROT_DIM:]], axis=-1)

def masked_softmax(s, mask):
    s = jnp.where(mask, s.astype(jnp.float32), NEG)
    return jax.nn.softmax(s, axis=-1) * mask

def nsa_mixer(q, kv, gate_logits, q_gain, k_gains, pe_k, pe_v, w1_k, w2_k, w1_v, w2_v):
    B, S = q.shape[0], q.shape[1]
    dt = q.dtype
    G, HPG, D = NSA_KV_GROUPS, NSA_HPG, NSA_HEAD_DIM
    scale = D ** -0.5
    pos = jnp.arange(S)
    kc, vc, ks, vs, kw, vw = [c.reshape(B, S, G, D) for c in jnp.split(kv, 6, axis=-1)]
    q = partial_rope(rms_norm(q.reshape(B, S, NSA_HEADS, D), q_gain), pos)
    q = q.reshape(B, S, G, HPG, D) * scale

    n_cmp = (S - CMP_BLOCK) // CMP_STRIDE + 1
    blk = np.arange(n_cmp)[:, None] * CMP_STRIDE + np.arange(CMP_BLOCK)[None, :]

    def compress(t, pe, w1, w2):
        tb = t[:, blk] + pe[:, None, :]
        tb = jnp.moveaxis(tb, 3, 2).reshape(B, n_cmp, G, CMP_BLOCK * D)
        return jax.nn.gelu(tb @ w1) @ w2

    cmp_end = jnp.arange(n_cmp) * CMP_STRIDE + CMP_BLOCK - 1
    k_cmp = partial_rope(rms_norm(compress(kc, pe_k, w1_k, w2_k), k_gains[0]), cmp_end)
    v_cmp = compress(vc, pe_v, w1_v, w2_v)
    s_cmp = jnp.einsum('bsghd,bngd->bghsn', q, k_cmp)
    p_cmp = masked_softmax(s_cmp, cmp_end[None, :] <= pos[:, None])
    o_cmp = jnp.einsum('bghsn,bngd->bsghd', p_cmp.astype(dt), v_cmp).reshape(B, S, NSA_HEADS, D)

    n_slc = S // SLC_BLOCK
    top_k = min(SLC_TOPK, n_slc)
    ci = np.arange(n_cmp)[:, None]
    sj = np.arange(n_slc)[None, :]
    overlap = ((ci * CMP_STRIDE < (sj + 1) * SLC_BLOCK) &
               (ci * CMP_STRIDE + CMP_BLOCK > sj * SLC_BLOCK)).astype(np.float32)
    p_slc = jnp.einsum('bghsn,nj->bgsj', p_cmp, jnp.asarray(overlap))
    j = jnp.arange(n_slc)[None, :]
    cur = (pos // SLC_BLOCK)[:, None]
    forced = (j == 0) | (j == cur) | (j == cur - 1)
    causal_blk = j * SLC_BLOCK <= pos[:, None]
    score = jnp.where(causal_blk, jnp.where(forced, FORCE_SCORE, p_slc), -jnp.inf)
    _, sel_idx = lax.top_k(score, top_k)

    ks = partial_rope(rms_norm(ks, k_gains[1]), pos)
    kw = partial_rope(rms_norm(kw, k_gains[2]), pos)
    ks_blk = jnp.moveaxis(ks.reshape(B, n_slc, SLC_BLOCK, G, D), 3, 1)
    vs_blk = jnp.moveaxis(vs.reshape(B, n_slc, SLC_BLOCK, G, D), 3, 1)
    pad = ((0, 0), (WINDOW, 0), (0, 0), (0, 0))
    kw_pad = jnp.pad(kw, pad)
    vw_pad = jnp.pad(vw, pad)
    n_qb = S // Q_BLOCK
    q_blocks = jnp.moveaxis(q.reshape(B, n_qb, Q_BLOCK, G, HPG, D), 1, 0)
    idx_blocks = jnp.moveaxis(sel_idx.reshape(B, G, n_qb, Q_BLOCK, top_k), 2, 0)
    bi = jnp.arange(B)[:, None, None, None]
    gi = jnp.arange(G)[None, :, None, None]

    def block_fn(args):
        i, qb, ib = args
        start = i * Q_BLOCK
        tq = start + jnp.arange(Q_BLOCK)
        k_sel = ks_blk[bi, gi, ib].reshape(B, G, Q_BLOCK, top_k * SLC_BLOCK, D)
        v_sel = vs_blk[bi, gi, ib].reshape(B, G, Q_BLOCK, top_k * SLC_BLOCK, D)
        kpos = (ib[..., None] * SLC_BLOCK + jnp.arange(SLC_BLOCK)).reshape(B, G, Q_BLOCK, top_k * SLC_BLOCK)
        m_sel = kpos <= tq[None, None, :, None]
        s = jnp.einsum('bqghd,bgqkd->bghqk', qb, k_sel)
        p = masked_softmax(s, m_sel[:, :, None])
        o_sel = jnp.einsum('bghqk,bgqkd->bqghd', p.astype(dt), v_sel)
        k_win = lax.dynamic_slice_in_dim(kw_pad, start, WINDOW + Q_BLOCK, axis=1)
        v_win = lax.dynamic_slice_in_dim(vw_pad, start, WINDOW + Q_BLOCK, axis=1)
        wpos = start - WINDOW + jnp.arange(WINDOW + Q_BLOCK)
        m_win = ((wpos[None, :] <= tq[:, None]) & (wpos[None, :] > tq[:, None] - WINDOW)
                 & (wpos[None, :] >= 0))
        s = jnp.einsum('bqghd,bkgd->bghqk', qb, k_win)
        p = masked_softmax(s, m_win)
        o_win = jnp.einsum('bghqk,bkgd->bqghd', p.astype(dt), v_win)
        return o_sel, o_win

    o_sel, o_win = lax.map(block_fn, (jnp.arange(n_qb), q_blocks, idx_blocks))
    o_sel = jnp.moveaxis(o_sel, 0, 1).reshape(B, S, NSA_HEADS, D)
    o_win = jnp.moveaxis(o_win, 0, 1).reshape(B, S, NSA_HEADS, D)

    g = jax.nn.sigmoid(gate_logits.reshape(B, S, NSA_HEADS, 3).astype(jnp.float32)).astype(dt)
    o = g[..., 0:1] * o_cmp + g[..., 1:2] * o_sel + g[..., 2:3] * o_win
    return o.reshape(B, S, NSA_Q_W)

def gla_mixer(q, k, v, g_lr, g_out, w_gate2, b_gate, out_gain):
    B, S = q.shape[0], q.shape[1]
    dt = q.dtype
    H, L = GLA_HEADS, GLA_CHUNK
    C = S // L

    def heads(t, d):
        return t.astype(jnp.float32).reshape(B, C, L, H, d).transpose(0, 3, 1, 2, 4)

    log_a = jax.nn.log_sigmoid((g_lr @ w_gate2 + b_gate).astype(jnp.float32)) / GLA_TAU
    qh = heads(q, GLA_DK) * (GLA_DK ** -0.5)
    kh = heads(k, GLA_DK)
    vh = heads(v, GLA_DV)
    b = jnp.cumsum(heads(log_a, GLA_DK), axis=3)
    b_last = b[:, :, :, -1:, :]
    q_t = qh * jnp.exp(b)
    k_t = kh * jnp.exp(-b)
    tril = jnp.tril(jnp.ones((L, L), dtype=bool))
    A = jnp.where(tril, jnp.einsum('bhcid,bhcjd->bhcij', q_t, k_t), 0.0)
    o_intra = jnp.einsum('bhcij,bhcjv->bhciv', A, vh)
    dS = jnp.einsum('bhcjd,bhcjv->bhcdv', kh * jnp.exp(b_last - b), vh)
    decay = jnp.exp(b_last[:, :, :, 0, :])

    def step(state, xs):
        dec, ds = xs
        return dec[..., None] * state + ds, state

    init = jnp.zeros((B, H, GLA_DK, GLA_DV), jnp.float32)
    _, s_prev = lax.scan(step, init, (jnp.moveaxis(decay, 2, 0), jnp.moveaxis(dS, 2, 0)))
    s_prev = jnp.moveaxis(s_prev, 0, 2)
    o = o_intra + jnp.einsum('bhcid,bhcdv->bhciv', q_t, s_prev)
    o = o.transpose(0, 2, 3, 1, 4).reshape(B, S, H, GLA_DV)
    o = rms_norm(o, out_gain) * jax.nn.silu(g_out.astype(jnp.float32).reshape(B, S, H, GLA_DV))
    return o.reshape(B, S, GLA_V_W).astype(dt)

def causal_dwconv(u, w, b):
    C = u.shape[-1]
    y = lax.conv_general_dilated(u, w[:, None, :].astype(u.dtype), window_strides=(1,),
                                 padding=[(CONV_W - 1, 0)],
                                 dimension_numbers=('NWC', 'WIO', 'NWC'),
                                 feature_group_count=C)
    return y + b

def first_inputs(seed: int = 0) -> dict:
    key = jax.random.key(seed)
    ks = jax.random.split(key, 24)
    L = DEPTH

    def nrm(k, shape, scale):
        return jax.random.normal(k, shape, jnp.float32) * scale

    def gain(k, shape):
        return 1.0 + 0.05 * jax.random.normal(k, shape, jnp.float32)

    cmp_in = CMP_BLOCK * NSA_HEAD_DIM
    return {
        'x': nrm(ks[0], (BATCH, SEQ, D_MODEL), 1.0),
        'attn_norm': gain(ks[1], (L, D_MODEL)),
        'w_in': nrm(ks[2], (L, D_MODEL, D_IN), D_MODEL ** -0.5),
        'nsa_q_norm': gain(ks[3], (L, NSA_HEAD_DIM)),
        'nsa_k_norm': gain(ks[4], (L, 3, NSA_HEAD_DIM)),
        'cmp_pos_k': nrm(ks[5], (L, CMP_BLOCK, NSA_HEAD_DIM), 0.1),
        'cmp_pos_v': nrm(ks[6], (L, CMP_BLOCK, NSA_HEAD_DIM), 0.1),
        'cmp_w1_k': nrm(ks[7], (L, cmp_in, CMP_HIDDEN), cmp_in ** -0.5),
        'cmp_w2_k': nrm(ks[8], (L, CMP_HIDDEN, NSA_HEAD_DIM), CMP_HIDDEN ** -0.5),
        'cmp_w1_v': nrm(ks[9], (L, cmp_in, CMP_HIDDEN), cmp_in ** -0.5),
        'cmp_w2_v': nrm(ks[10], (L, CMP_HIDDEN, NSA_HEAD_DIM), CMP_HIDDEN ** -0.5),
        'gla_w_gate2': nrm(ks[11], (L, GLA_GATE_RANK, GLA_QK_W), GLA_GATE_RANK ** -0.5),
        'gla_b_gate': nrm(ks[12], (L, GLA_QK_W), 0.1),
        'gla_out_norm': gain(ks[13], (L, GLA_DV)),
        'w_out': nrm(ks[14], (L, D_MIX, D_MODEL), D_MIX ** -0.5),
        'ffn_norm': gain(ks[15], (L, D_MODEL)),
        'w_up': nrm(ks[16], (L, D_MODEL, 2 * D_FF), D_MODEL ** -0.5),
        'conv_w': nrm(ks[17], (L, CONV_W, 2 * D_FF), CONV_W ** -0.5),
        'conv_b': nrm(ks[18], (L, 2 * D_FF), 0.02),
        'w_down': nrm(ks[19], (L, D_FF, D_MODEL), D_FF ** -0.5),
    }

def first_block(x, attn_norm, w_in, nsa_q_norm, nsa_k_norm, cmp_pos_k, cmp_pos_v, cmp_w1_k, cmp_w2_k,
              cmp_w1_v, cmp_w2_v, gla_w_gate2, gla_b_gate, gla_out_norm, w_out, ffn_norm, w_up,
              conv_w, conv_b, w_down):
    offs = [int(o) for o in np.cumsum(IN_SPLITS)[:-1]]
    h = x
    for l in range(DEPTH):
        z = rms_norm(h, attn_norm[l]) @ w_in[l]
        nq, nkv, ngate, gq, gk, gv, glr, gout = jnp.split(z, offs, axis=-1)
        o_nsa = nsa_mixer(nq, nkv, ngate, nsa_q_norm[l], nsa_k_norm[l], cmp_pos_k[l], cmp_pos_v[l],
                          cmp_w1_k[l], cmp_w2_k[l], cmp_w1_v[l], cmp_w2_v[l])
        o_gla = gla_mixer(gq, gk, gv, glr, gout, gla_w_gate2[l], gla_b_gate[l], gla_out_norm[l])
        h = h + jnp.concatenate([o_nsa, o_gla], axis=-1) @ w_out[l]
        u = causal_dwconv(rms_norm(h, ffn_norm[l]) @ w_up[l], conv_w[l], conv_b[l])
        gate, up = jnp.split(u, 2, axis=-1)
        h = h + (jax.nn.silu(gate) * up) @ w_down[l]
    return h


CHUNK = 64
N_META = 16
DN_HEADS = 8
DN_DK = 128
DN_DV = 256
DN_CONV = 4
DN_QK = DN_HEADS * DN_DK
DN_V = DN_HEADS * DN_DV
SB_HEADS = 8
SB_DH = 128
SB_W = SB_HEADS * SB_DH
SB_BLOCK = 128
D_FF_2 = -(-8 * D_MODEL // (3 * 256)) * 256
PROJ_WIDTH = 2 * DN_QK + 2 * DN_V + 2 * DN_HEADS + 3 * SB_W + 2 * D_MODEL
RMS_EPS = 1e-6
L2_EPS = 1e-6


def _split_points():
    widths = (DN_QK, DN_QK, DN_V, DN_V, DN_HEADS, DN_HEADS, SB_W, SB_W, SB_W, D_MODEL, D_MODEL)
    return [int(s) for s in np.cumsum(widths)[:-1]]

def rmsnorm(x, gain):
    xf = x.astype(jnp.float32)
    y = xf * lax.rsqrt(jnp.mean(xf * xf, axis=-1, keepdims=True) + RMS_EPS)
    return (y * gain.astype(jnp.float32)).astype(x.dtype)

def l2norm(x):
    xf = x.astype(jnp.float32)
    return xf * lax.rsqrt(jnp.sum(xf * xf, axis=-1, keepdims=True) + L2_EPS)

def causal_depthwise_conv(x, w):
    K, C = w.shape
    return lax.conv_general_dilated(
        x, w[:, None, :].astype(x.dtype), window_strides=(1,), padding=[(K - 1, 0)],
        dimension_numbers=('NWC', 'WIO', 'NWC'), feature_group_count=C)

def gated_delta_rule(q, k, v, g, beta):
    B, T, H, DK = q.shape
    DV = v.shape[-1]
    N = T // CHUNK
    f32 = jnp.float32

    def to_chunks(a):
        a = a.astype(f32).reshape((B, N, CHUNK, H) + a.shape[3:])
        return jnp.moveaxis(a, (1, 3), (0, 2))

    q = to_chunks(q) * (DK ** -0.5)
    k = to_chunks(k)
    v = to_chunks(v)
    beta = to_chunks(beta)
    g = jnp.cumsum(to_chunks(g), axis=-1)
    idx = jnp.arange(CHUNK)
    incl = idx[:, None] >= idx[None, :]
    strict = idx[:, None] > idx[None, :]
    decay = jnp.exp(jnp.where(incl, g[..., :, None] - g[..., None, :], -jnp.inf))
    kb = k * beta[..., None]
    lower = jnp.where(strict, jnp.einsum('nbhid,nbhjd->nbhij', kb, k) * decay, 0.0)
    eye = jnp.eye(CHUNK, dtype=f32)
    rhs = jnp.concatenate([v * beta[..., None], kb * jnp.exp(g)[..., None]], axis=-1)
    sol = lax.linalg.triangular_solve(eye + lower, rhs, left_side=True, lower=True)
    u, w = sol[..., :DV], sol[..., DV:]
    attn = jnp.einsum('nbhid,nbhjd->nbhij', q, k) * decay
    q_dec = q * jnp.exp(g)[..., None]
    k_dec = k * jnp.exp(g[..., -1:] - g)[..., None]
    g_last = jnp.exp(g[..., -1])

    def step(S, xs):
        u_c, w_c, attn_c, qd_c, kd_c, gl_c = xs
        v_new = u_c - jnp.einsum('bhcd,bhde->bhce', w_c, S)
        o = jnp.einsum('bhcd,bhde->bhce', qd_c, S) + jnp.einsum('bhij,bhje->bhie', attn_c, v_new)
        S = S * gl_c[..., None, None] + jnp.einsum('bhcd,bhce->bhde', kd_c, v_new)
        return S, o

    S0 = jnp.zeros((B, H, DK, DV), f32)
    _, o = lax.scan(step, S0, (u, w, attn, q_dec, k_dec, g_last))
    return jnp.moveaxis(o, (0, 2), (1, 3)).reshape(B, T, H, DV)

def stick_breaking_attention(q, k, v):
    B, T, H, D = q.shape
    nq = -(-T // SB_BLOCK)
    Tp = nq * SB_BLOCK
    pad = ((0, 0), (0, Tp - T), (0, 0), (0, 0))
    f32 = jnp.float32
    qh = jnp.pad(q.astype(f32), pad).reshape(B, nq, SB_BLOCK, H, D).transpose(1, 0, 3, 2, 4)
    kh = jnp.pad(k.astype(f32), pad).transpose(0, 2, 1, 3)
    vh = jnp.pad(v.astype(f32), pad).transpose(0, 2, 1, 3)
    key_pos = jnp.arange(Tp)
    scale = D ** -0.5

    def block(args):
        q_blk, start = args
        z = jnp.einsum('bhqd,bhkd->bhqk', q_blk, kh) * scale
        q_pos = start + jnp.arange(SB_BLOCK)
        visible = key_pos[None, :] < q_pos[:, None]
        log_keep = jnp.where(visible, jax.nn.log_sigmoid(-z), 0.0)
        log_w = jax.nn.log_sigmoid(z) + lax.cumsum(log_keep, axis=3, reverse=True) - log_keep
        w = jnp.where(visible, jnp.exp(log_w), 0.0)
        return jnp.einsum('bhqk,bhkd->bhqd', w, vh)

    o = lax.map(block, (qh, jnp.arange(nq) * SB_BLOCK))
    return o.transpose(1, 0, 3, 2, 4).reshape(B, Tp, H, D)[:, :T]

def hybrid_mixer(hn, w_in, conv_q, conv_k, conv_v, a_log, dt_bias, dn_gain, sbq_gain, sbk_gain,
                 w_branch_dn, w_branch_sb, w_out):
    B, T, _ = hn.shape
    proj = hn @ w_in
    (dq, dk, dv, dz, da, db, sq, sk, sv, gate_dn, gate_sb) = jnp.split(proj, _split_points(), axis=-1)

    def heads(a, d):
        return a.reshape(B, T, -1, d)

    q = l2norm(heads(jax.nn.silu(causal_depthwise_conv(dq, conv_q)), DN_DK))
    k = l2norm(heads(jax.nn.silu(causal_depthwise_conv(dk, conv_k)), DN_DK))
    v = heads(jax.nn.silu(causal_depthwise_conv(dv, conv_v)), DN_DV)
    g = -jnp.exp(a_log.astype(jnp.float32)) * jax.nn.softplus(da.astype(jnp.float32) + dt_bias.astype(jnp.float32))
    beta = jax.nn.sigmoid(db.astype(jnp.float32))
    pad_l = (-N_META) % CHUNK
    pad_r = (-(T + pad_l)) % CHUNK

    def chunk_pad(a):
        return jnp.pad(a, ((0, 0), (pad_l, pad_r)) + ((0, 0),) * (a.ndim - 2))

    o_dn = gated_delta_rule(chunk_pad(q), chunk_pad(k), chunk_pad(v), chunk_pad(g), chunk_pad(beta))
    o_dn = o_dn[:, pad_l:pad_l + T]
    o_dn = rmsnorm(o_dn, dn_gain) * jax.nn.silu(heads(dz, DN_DV).astype(jnp.float32))
    o_dn = o_dn.astype(hn.dtype).reshape(B, T, DN_V)

    qs = rmsnorm(heads(sq, SB_DH), sbq_gain)
    ks = rmsnorm(heads(sk, SB_DH), sbk_gain)
    o_sb = stick_breaking_attention(qs, ks, heads(sv, SB_DH)).astype(hn.dtype).reshape(B, T, SB_W)

    merged = jax.nn.sigmoid(gate_dn) * (o_dn @ w_branch_dn) + jax.nn.sigmoid(gate_sb) * (o_sb @ w_branch_sb)
    return merged @ w_out

def swiglu(hn, w_ffn_in, w_ffn_out):
    gate, up = jnp.split(hn @ w_ffn_in, 2, axis=-1)
    return (jax.nn.silu(gate) * up) @ w_ffn_out

def second_inputs(seed: int = 0) -> dict:
    key = jax.random.key(seed)
    ks = jax.random.split(key, 20)
    f32 = jnp.float32

    def nrm(k, shape, fan_in):
        return jax.random.normal(k, shape, f32) * (fan_in ** -0.5)

    def gain(k, n):
        return 1.0 + 0.02 * jax.random.normal(k, (DEPTH, n), f32)

    dt = jnp.exp(jax.random.uniform(ks[7], (DEPTH, DN_HEADS), f32) * (math.log(0.1) - math.log(1e-3)) + math.log(1e-3))
    return {
        'x': jax.random.normal(ks[0], (BATCH, SEQ, D_MODEL), f32),
        'meta_tokens': jax.random.normal(ks[1], (N_META, D_MODEL), f32),
        'norm_mix_gain': gain(ks[2], D_MODEL),
        'w_in': nrm(ks[3], (DEPTH, D_MODEL, PROJ_WIDTH), D_MODEL),
        'conv_q': nrm(ks[4], (DEPTH, DN_CONV, DN_QK), DN_CONV),
        'conv_k': nrm(ks[5], (DEPTH, DN_CONV, DN_QK), DN_CONV),
        'conv_v': nrm(ks[6], (DEPTH, DN_CONV, DN_V), DN_CONV),
        'dn_a_log': jnp.log(jax.random.uniform(ks[8], (DEPTH, DN_HEADS), f32, 1.0, 16.0)),
        'dn_dt_bias': dt + jnp.log(-jnp.expm1(-dt)),
        'dn_out_norm_gain': gain(ks[9], DN_DV),
        'sb_q_norm_gain': gain(ks[10], SB_DH),
        'sb_k_norm_gain': gain(ks[11], SB_DH),
        'w_branch_dn': nrm(ks[12], (DEPTH, DN_V, D_MODEL), DN_V),
        'w_branch_sb': nrm(ks[13], (DEPTH, SB_W, D_MODEL), SB_W),
        'w_out': nrm(ks[14], (DEPTH, D_MODEL, D_MODEL), D_MODEL),
        'norm_ffn_gain': gain(ks[15], D_MODEL),
        'w_ffn_in': nrm(ks[16], (DEPTH, D_MODEL, 2 * D_FF_2), D_MODEL),
        'w_ffn_out': nrm(ks[17], (DEPTH, D_FF_2, D_MODEL), D_FF_2),
    }

def second_block(x, meta_tokens, norm_mix_gain, w_in, conv_q, conv_k, conv_v, dn_a_log, dn_dt_bias,
              dn_out_norm_gain, sb_q_norm_gain, sb_k_norm_gain, w_branch_dn, w_branch_sb, w_out,
              norm_ffn_gain, w_ffn_in, w_ffn_out):
    B = x.shape[0]
    meta = jnp.broadcast_to(meta_tokens[None].astype(x.dtype), (B, N_META, D_MODEL))
    h = jnp.concatenate([meta, x], axis=1)
    for l in range(DEPTH):
        h = h + hybrid_mixer(rmsnorm(h, norm_mix_gain[l]), w_in[l], conv_q[l], conv_k[l], conv_v[l],
                             dn_a_log[l], dn_dt_bias[l], dn_out_norm_gain[l], sb_q_norm_gain[l],
                             sb_k_norm_gain[l], w_branch_dn[l], w_branch_sb[l], w_out[l])
        h = h + swiglu(rmsnorm(h, norm_ffn_gain[l]), w_ffn_in[l], w_ffn_out[l])
    return h[:, N_META:]


def setup_inputs(seed=0):
    out = dict(first_inputs(seed))
    for name, value in second_inputs(seed + 1).items():
        if name != "x":
            out[name + "_2"] = value
    return out


def reference(
    x, attn_norm, w_in, nsa_q_norm, nsa_k_norm, cmp_pos_k, cmp_pos_v, cmp_w1_k, cmp_w2_k,
    cmp_w1_v, cmp_w2_v, gla_w_gate2, gla_b_gate, gla_out_norm, w_out, ffn_norm, w_up, conv_w,
    conv_b, w_down, meta_tokens_2, norm_mix_gain_2, w_in_2, conv_q_2, conv_k_2, conv_v_2,
    dn_a_log_2, dn_dt_bias_2, dn_out_norm_gain_2, sb_q_norm_gain_2, sb_k_norm_gain_2,
    w_branch_dn_2, w_branch_sb_2, w_out_2, norm_ffn_gain_2, w_ffn_in_2, w_ffn_out_2,
):
    x = first_block(
        x, attn_norm, w_in, nsa_q_norm, nsa_k_norm, cmp_pos_k, cmp_pos_v, cmp_w1_k, cmp_w2_k,
        cmp_w1_v, cmp_w2_v, gla_w_gate2, gla_b_gate, gla_out_norm, w_out, ffn_norm, w_up,
        conv_w, conv_b, w_down,
    )
    return second_block(
        x, meta_tokens_2, norm_mix_gain_2, w_in_2, conv_q_2, conv_k_2, conv_v_2, dn_a_log_2,
        dn_dt_bias_2, dn_out_norm_gain_2, sb_q_norm_gain_2, sb_k_norm_gain_2, w_branch_dn_2,
        w_branch_sb_2, w_out_2, norm_ffn_gain_2, w_ffn_in_2, w_ffn_out_2,
    )


_drawn_inputs = setup_inputs


def setup_inputs(seed=0):
    import zlib

    import numpy as np

    out = dict(_drawn_inputs(seed))
    spreads = {}
    factors = {'nsa_q_norm': 8.0,
     'nsa_k_norm': 8.0,
     'cmp_pos_k': 8.0,
     'conv_b': 3.583,
     'norm_mix_gain_2': 5.141,
     'dn_out_norm_gain_2': 8.0,
     'sb_q_norm_gain_2': 27.957,
     'sb_k_norm_gain_2': 26.829,
     'norm_ffn_gain_2': 14.685}
    for name, (base, spread) in spreads.items():
        noise = np.random.default_rng([zlib.crc32(name.encode()), seed]).standard_normal(out[name].shape)
        drawn = base * np.exp(spread * noise) if base else spread * noise
        out[name] = __import__('jax').numpy.asarray(drawn.astype(out[name].dtype))
    for name, factor in factors.items():
        out[name] = (out[name] * factor).astype(out[name].dtype)
    return out
```

```python
from contextlib import ExitStack

import numpy as np

import concourse.bass as bass
from concourse import mybir

F32 = mybir.dt.float32
F32R = mybir.dt.float32r
ACT = mybir.ActivationFunctionType
ALU = mybir.AluOpType
AX = mybir.AxisListType
ds = bass.ds

P = 128
SEQ = 512
D = 1024
KT = D // P
TT = SEQ // P
META = 16
T2 = SEQ + META
HALF = T2 // 2
EPS = 1e-6
NEG = -1e30
D_FF = 2816
FT = D_FF // P

NSA_H, NSA_G, NSA_D = 8, 2, 64
N_CMP = 31
CMP_J = 16
GLA_H = 4
CH = 64

DN_H, DN_V = 8, 256
HG = 4
SB_H = 8

RAW = 4
HL = 2


CONST_COLS = {}


def const_array():
    r = np.arange(P)
    row, col = r[:, None], r[None, :]
    same = (row // CH) == (col // CH)
    parts = {}
    parts["ident"] = np.eye(P)
    parts["causal"] = np.where(col <= row, 0.0, NEG)
    parts["tri_incl"] = (same & (row <= col)) * 1.0
    parts["tri_after"] = (same & (row > col)) * 1.0
    parts["chunk_ones"] = np.concatenate([(row < CH) * np.ones((1, P)), (row >= CH) * np.ones((1, P))], 1)
    parts["cap_incl"] = np.where(same & (row <= col), 0.0, NEG)
    parts["cap_strict"] = np.where(same & (col < row), 0.0, NEG)
    parts["same16"] = ((row // 16) == (col // 16)) * 1.0
    parts["sb_mask"] = np.where(row < col, 0.0, NEG)
    parts["neg_from"] = -((row >= col) * 1.0)
    parts["neg_ones"] = -np.ones((P, P))
    parts["ones"] = np.ones((P, P))
    half = 8
    inv = (np.float32(500000.0) ** (-np.arange(half, dtype=np.float32) / np.float32(half))).astype(np.float32)
    pos = np.arange(SEQ, dtype=np.float32).reshape(TT, P)
    ang = (pos[:, :, None] * inv).astype(np.float32)
    parts["cos"] = np.cos(ang).transpose(1, 0, 2).reshape(P, TT * half)
    parts["sin"] = np.sin(ang).transpose(1, 0, 2).reshape(P, TT * half)
    end = np.zeros(32, np.float32)
    end[:N_CMP] = np.arange(N_CMP) * 16 + 31
    angc = (np.tile(end, 4)[:, None] * inv).astype(np.float32)
    parts["cos_cmp"], parts["sin_cmp"] = np.cos(angc), np.sin(angc)
    t = np.arange(SEQ).reshape(TT, P)
    keep = np.zeros((P, TT, NSA_G, NSA_G, 32))
    for g in range(NSA_G):
        for n in range(N_CMP):
            keep[:, :, g, g, n] = (n * 16 + 31 <= t).T
    parts["cmp_keep"] = keep.reshape(P, -1)
    parts["cmp_bias"] = np.where(keep > 0, 0.0, NEG).reshape(P, -1)
    at, out = 0, []
    for name, a in parts.items():
        CONST_COLS[name] = (at, a.shape[1])
        at += a.shape[1]
        out.append(a.astype(np.float32))
    return np.ascontiguousarray(np.concatenate(out, 1))


const_array()


PARAM_COLS = {}
PARAM_SHAPES = [
    ("q_gain", 64), ("k_gain0", 64), ("k_gain1", 64), ("k_gain2", 64), ("b_gate", 256),
    ("gla_gain", 128), ("pe_k", CMP_J), ("pe_v", CMP_J),
    ("conv1_w", 44 * 3), ("conv1_b", 44),
    ("conv2", 2 * 16 * 4),
    ("a_log", 8), ("dt_bias", 8), ("dn_gain", 256), ("sbq_gain", 1), ("sbk_gain", 1),
    ("cmp_w2_k", 128), ("cmp_w2_v", 128), ("w_gate2", 256),
]
_at = 0
for _n, _w in PARAM_SHAPES:
    PARAM_COLS[_n] = (_at, _w)
    _at += _w
PARAM_N = _at


def param_array(v):
    def rows(a):
        return np.broadcast_to(a.reshape(1, -1), (P, a.size))

    def tiles(a):
        taps, n = a.shape
        return a.reshape(taps, n // P, P).transpose(2, 1, 0).reshape(P, -1)

    def pairs(pe):
        return pe.reshape(CMP_J, P).T

    def ktiles(w):
        return w.reshape(2, P, -1).transpose(1, 0, 2).reshape(P, -1)

    wg = np.zeros((P, 256), np.float32)
    wg[:16] = v["gla_w_gate2"][0]
    c1 = v["conv_w"][0]
    parts = dict(
        q_gain=rows(v["nsa_q_norm"][0]), k_gain0=rows(v["nsa_k_norm"][0, 0]), k_gain1=rows(v["nsa_k_norm"][0, 1]),
        k_gain2=rows(v["nsa_k_norm"][0, 2]), b_gate=rows(v["gla_b_gate"][0]), gla_gain=rows(v["gla_out_norm"][0]),
        pe_k=pairs(v["cmp_pos_k"][0]), pe_v=pairs(v["cmp_pos_v"][0]),
        conv1_w=tiles(c1), conv1_b=v["conv_b"][0].reshape(44, P).T,
        conv2=np.concatenate([tiles(a) for g in range(2) for a in (
            v["conv_q_2"][0][:, 512 * g:512 * g + 512], v["conv_k_2"][0][:, 512 * g:512 * g + 512],
            v["conv_v_2"][0][:, 1024 * g:1024 * g + 1024])], 1),
        a_log=rows(v["dn_a_log_2"][0]), dt_bias=rows(v["dn_dt_bias_2"][0]), dn_gain=rows(v["dn_out_norm_gain_2"][0]),
        sbq_gain=v["sb_q_norm_gain_2"][0].reshape(P, 1), sbk_gain=v["sb_k_norm_gain_2"][0].reshape(P, 1),
        cmp_w2_k=ktiles(v["cmp_w2_k"][0]), cmp_w2_v=ktiles(v["cmp_w2_v"][0]), w_gate2=wg,
    )
    return np.ascontiguousarray(np.concatenate([parts[n] for n, _ in PARAM_SHAPES], 1))



def chunks_cols(w, c0, n, rows=slice(0, D)):
    a = w[rows, c0:c0 + n * P].reshape(KT, P, n, P)
    return a.transpose(2, 1, 0, 3).reshape(n, P, 1024)


def chunks_rows512(w, c0, groups=1):
    a = w[:, c0:c0 + groups * 512].reshape(4, 2, P, groups, 512)
    return a.transpose(3, 0, 2, 1, 4).reshape(groups * 4, P, 1024)


def chunks_rows(w):
    return w.reshape(-1, P, 1024)


def interleave(a, b):
    return np.stack([a, b], 1).reshape(-1, P, 1024)


def stream1(v):
    w, up = v["w_in"][0], v["w_up"][0]
    return [
        chunks_rows512(w, 0), chunks_rows512(w, 768), chunks_rows512(w, 1816), chunks_rows512(w, 2344),
        chunks_cols(w, 512, 2), chunks_cols(w, 1280, 1), chunks_cols(w, 1304, 4), chunks_cols(w, 2328, 1),
        chunks_rows(v["w_out"][0]),
        interleave(chunks_cols(up, 0, FT), chunks_cols(up, D_FF, FT)),
        chunks_rows(v["w_down"][0]),
    ]


def stream2(v):
    w, up = v["w_in_2"][0], v["w_ffn_in_2"][0]
    bdn, bsb = v["w_branch_dn_2"][0], v["w_branch_sb_2"][0]
    out = [chunks_cols(w, 6144, 1)]
    for g in range(2):
        out += [chunks_cols(w, 512 * g, 4), chunks_cols(w, 1024 + 512 * g, 4), chunks_cols(w, 2048 + 1024 * g, 8),
                chunks_rows512(w, 4096 + 1024 * g, 2)]
        branch = chunks_cols(bdn, 0, 8, rows=slice(1024 * g, 1024 * g + 1024))
        out.append(branch if g == 0 else interleave(chunks_cols(w, 9232, 8), branch))
    out += [chunks_cols(w, 6160, 8), chunks_cols(w, 7184, 8), chunks_cols(w, 8208, 8),
            interleave(chunks_cols(w, 10256, 8), chunks_cols(bsb, 0, 8)),
            chunks_rows(v["w_out_2"][0]),
            interleave(chunks_cols(up, 0, FT), chunks_cols(up, D_FF, FT)),
            chunks_rows(v["w_ffn_out_2"][0])]
    return out


N_STREAM1 = 24 + 8 + 44 + 22
N_STREAM2 = 1 + 2 * (16 + 8) + 8 + 16 + 24 + 16 + 8 + 44 + 22



class Core:
    pass


class Chain:

    def __init__(self, sem):
        self.sem, self.count, self.turn, self.k = sem, 0, None, 0

    def loop(self, i, per):
        self.turn, self.per, self.k = i, per, 0

    def end(self, turns):
        assert self.k == self.per, (self.k, self.per)
        self.count += self.per * turns
        self.turn = None

    def link(self, eng, ins):
        ins.then_inc(self.sem, 1)
        if self.turn is None:
            self.count += 1
            eng.wait_ge(self.sem, self.count)
        else:
            self.k += 1
            eng.wait_ge(self.sem, self.turn * self.per + (self.count + self.k))


def over_chunks(eng, first, n, step, unroll=4, chain=None, links=0):
    turns = n // unroll
    if turns:
        with eng.Fori(0, turns) as i:
            if chain is not None:
                chain.loop(i, links * unroll)
            for u in range(unroll):
                step(i * unroll + u, first + u, i * (unroll // RAW))
            if chain is not None:
                chain.end(turns)
    for c in range(turns * unroll, n):
        step(c, first + c, 0)


def load_chunks(K, sp, first, n):
    n = min(n, K.n_stream - RAW - first)
    if n <= 0:
        return

    def step(c, s, turn):
        sp.wait_ge(K.s_lo, c + (first + 1))
        sp.dma_start(K.raw[:, s % RAW], K.stream[ds(c + (first + RAW), 1)][0]
                     ).then_inc(K.s_raw[s % RAW], 16)
    over_chunks(sp, first, n, step)


def split_hi(K, act, c, s, turn, first):
    act.wait_ge(K.s_used, c + (first + 1))
    n = s + HL
    act.wait_ge(K.s_raw[n % RAW], turn * 16 + 16 * (n // RAW + 1))
    act.activation(K.whi[:, n % HL], K.raw[:, n % RAW], ACT.Copy).then_inc(K.s_hi, 1)


def split_lo(K, dve, c, s, turn, first):
    n = s + HL
    dve.wait_ge(K.s_hi, c + (first + HL + 1))
    dve.tensor_tensor(K.wlo[:, n % HL], K.raw[:, n % RAW], K.whi[:, n % HL].bitcast(F32),
                      ALU.subtract).then_inc(K.s_lo, 1)


def guarded(K, first, step):
    def run(eng, c, s, turn):
        if isinstance(c, int) and first + c + HL >= K.n_stream:
            return
        step(K, eng, c, s, turn, first)
    return run


def three(pe, out, whi, wlo, xhi, xlo, start, stop, skip=False):
    pe.matmul(out, whi, xhi, start=start, stop=False, skip_group_check=skip)
    pe.matmul(out, whi, xlo, start=False, stop=False, skip_group_check=skip)
    return pe.matmul(out, wlo, xhi, start=False, stop=stop, skip_group_check=skip)


def sems(K, *names):
    for s in K.cleared:
        K.nc.release_semaphore(s)
    for s in K.live:
        K.nc.gpsimd.sem_clear(s)
    K.cleared = K.live
    K.stage += 1
    K.live = [K.nc.alloc_semaphore(f"{n}_{K.stage}") for n in names]
    return K.live


def cst(K, name, rows=P):
    a, n = CONST_COLS[name]
    return K.const[0:rows, a:a + n]


def par(K, name, rows=P):
    a, n = PARAM_COLS[name]
    return K.param[0:rows, a:a + n]


def bc(ap, shape, axis):
    return ap.unsqueeze(axis).to_broadcast(shape)



def product_cols(K, first, n, x_hi, x_lo, ranges, evac, unroll=4, act_links=0, dve_links=0):
    s_free, *more = sems(K, "banks_free", *evac.get("sems", ()))
    evac["signals"] = more

    with K.nc.Block() as block:
        @block.sync
        def _(sp):
            load_chunks(K, sp, first, n)

        @block.tensor
        def _(pe):
            def step(c, s, turn):
                u = s - first
                xh, xl, rng = ranges[u % len(ranges)]
                pe.wait_ge(K.s_lo, c + (first + 1))
                pe.wait_ge(s_free, c + 1)
                for h, (a, e) in enumerate(rng):
                    for k in range(KT):
                        mm = three(pe, K.ps[:, 2 * (u % 2) + h, 0:e - a],
                                   K.whi[:, s % HL, k * P:(k + 1) * P], K.wlo[:, s % HL, k * P:(k + 1) * P],
                                   xh[:, k, a:e], xl[:, k, a:e], k == 0, k == KT - 1)
                mm.then_inc(K.s_used, 1)
            over_chunks(pe, first, n, step, unroll)

        @block.scalar
        def _(act):
            if evac["frees"] == "act":
                act.nop().then_inc(s_free, 2)

            def step(c, s, turn):
                guarded(K, first, split_hi)(act, c, s, turn)
                if "act" in evac:
                    act.wait_ge(K.s_used, c + (first + 1))
                    evac["act"](act, c, s - first, turn, 2 * ((s - first) % 2), s_free)
            over_chunks(act, first, n, step, unroll, K.act_chain, act_links)

        @block.vector
        def _(dve):
            if evac["frees"] == "dve":
                dve.nop().then_inc(s_free, 2)
            if "head_dve" in evac:
                evac["head_dve"](dve)

            def step(c, s, turn):
                guarded(K, first, split_lo)(dve, c, s, turn)
                if "dve" in evac:
                    dve.wait_ge(K.s_used, c + (first + 1))
                    evac["dve"](dve, c, s - first, turn, 2 * ((s - first) % 2), s_free)
            over_chunks(dve, first, n, step, unroll, K.dve_chain, dve_links)


def product_rows512(K, first, groups, x_hi, x_lo, tok0, evac, unroll=8):
    s_free, = sems(K, "banks_free")
    n = 4 * groups

    with K.nc.Block() as block:
        @block.sync
        def _(sp):
            load_chunks(K, sp, first, n)

        @block.tensor
        def _(pe):
            def step(c, s, turn):
                u = s - first
                pe.wait_ge(K.s_lo, c + (first + 1))
                if u % 4 == 0:
                    pe.wait_ge(s_free, c + 4)
                for t in range(TT):
                    for k2 in range(2):
                        k = 2 * (u % 4) + k2
                        w = slice(k2 * 512, k2 * 512 + 512)
                        a = tok0 + t * P
                        out = K.ps[:, 4 * (u // 4 % 2) + t, :]
                        pe.matmul(out, x_hi[:, k, a:a + P], K.whi[:, s % HL, w], start=k == 0, stop=False)
                        pe.matmul(out, x_lo[:, k, a:a + P], K.whi[:, s % HL, w], start=False, stop=False)
                        mm = pe.matmul(out, x_hi[:, k, a:a + P], K.wlo[:, s % HL, w], start=False, stop=k == KT - 1)
                mm.then_inc(K.s_used, 1)
            over_chunks(pe, first, n, step, unroll)

        @block.scalar
        def _(act):
            act.nop().then_inc(s_free, 8)

            def step(c, s, turn):
                u = s - first
                guarded(K, first, split_hi)(act, c, s, turn)
                if u % 4 == 3:
                    act.wait_ge(K.s_used, c + (first + 1))
                    evac(act, c, u, K.ps[:, 4 * (u // 4 % 2):4 * (u // 4 % 2) + 4, :]).then_inc(s_free, 4)
            over_chunks(act, first, n, step, unroll)

        @block.vector
        def _(dve):
            def step(c, s, turn):
                guarded(K, first, split_lo)(dve, c, s, turn)
            over_chunks(dve, first, n, step, unroll)


def product_rows(K, first, n, x_hi, x_lo, finish, unroll=2):
    s_added, = sems(K, "rows_added")

    with K.nc.Block() as block:
        @block.tensor
        def _(pe):
            for c in range(n):
                pe.wait_ge(K.s_lo, first + c + 1)
                w = (first + c) % HL
                for t in range(TT):
                    for half in range(2):
                        out = K.ps[:, 2 * t + half, :]
                        wc = slice(half * 512, half * 512 + 512)
                        xh, xl = x_hi[:, c, t * P:(t + 1) * P], x_lo[:, c, t * P:(t + 1) * P]
                        pe.matmul(out, xh, K.whi[:, w, wc], start=c == 0, stop=False)
                        pe.matmul(out, xl, K.whi[:, w, wc], start=False, stop=False)
                        mm = pe.matmul(out, xh, K.wlo[:, w, wc], start=False, stop=c == n - 1)
                mm.then_inc(K.s_used, 1)

        @block.scalar
        def _(act):
            over_chunks(act, first, n, lambda c, s, turn: guarded(K, first, split_hi)(act, c, s, turn))

        @block.vector
        def _(dve):
            over_chunks(dve, first, n, lambda c, s, turn: guarded(K, first, split_lo)(dve, c, s, turn))
            dve.wait_ge(K.s_used, first + n)
            for t in range(TT):
                dve.tensor_tensor(K.h[:, t, :], K.h[:, t, :],
                                  K.ps[:, 2 * t:2 * t + 2, :].rearrange("p a b -> p (a b)"), ALU.add).then_inc(s_added, 1)

        @block.sync
        def _(sp):
            load_chunks(K, sp, first, n)
            if finish:
                finish(sp, s_added)



def norm_rows(K, gain, meta):
    meta_in, meta = meta, 0 if meta is None else 1
    ss, rs, xn, gb = K.t_ss, K.t_rs, K.t_xn, K.t_gain
    s_gain, s_sum, s_xn, s_tr, s_hi, s_ev, s_mt = sems(
        K, "gain_in", "sums", "xn", "transposed", "hi", "evacuated", "meta")
    tiles = [(K.h[:, t, :], P, META * meta + t * P) for t in range(TT)]
    if meta:
        tiles.append((K.hm[0:META, :], META, 0))
    nt = len(tiles)

    with K.nc.Block() as block:
        @block.sync
        def _(sp):
            if meta:
                sp.dma_start(K.hm[:], meta_in).then_inc(s_mt, 16)
            sp.dma_start(gb[:], gain).then_inc(s_gain, 16)

        @block.scalar
        def _(act):
            ch = K.act_chain
            for t, (h, rows, _) in enumerate(tiles):
                if t == TT:
                    act.wait_ge(s_mt, 16)
                act.activation(xn[0:rows, t, :], h, ACT.Square, accum_out=ss[0:rows, t:t + 1]).then_inc(s_sum, 1)
            act.wait_ge(s_sum, nt + 1)
            act.activation(rs[:, 0:nt], ss[:, 0:nt], ACT.Sqrt).then_inc(s_sum, 1)
            for k in range(KT):
                act.wait_ge(s_tr, k + 1)
                act.activation(K.nx_hi[:, k, META * meta:META * meta + SEQ], K.ps[:, k, :], ACT.Copy).then_inc(s_hi, 1)

        @block.vector
        def _(dve):
            ch = K.dve_chain
            dve.wait_ge(s_sum, nt)
            dve.tensor_scalar(ss[:, 0:nt], ss[:, 0:nt], 1.0 / D, EPS, ALU.mult, ALU.add).then_inc(s_sum, 1)
            dve.wait_ge(s_sum, nt + 2)
            ch.link(dve, dve.reciprocal(rs[:, 0:nt], rs[:, 0:nt]))
            dve.wait_ge(s_gain, 16)
            for t, (h, rows, _) in enumerate(tiles):
                dve.scalar_tensor_tensor(xn[0:rows, t, :], h, rs[0:rows, t:t + 1], gb[0:rows, :],
                                         ALU.mult, ALU.mult).then_inc(s_xn, 1)
            for k in range(KT):
                dve.wait_ge(s_hi, k + 1)
                dve.tensor_tensor(K.nx_lo[:, k, META * meta:META * meta + SEQ], K.ps[:, k, :],
                                  K.nx_hi[:, k, META * meta:META * meta + SEQ].bitcast(F32), ALU.subtract).then_inc(s_ev, 1)
            if meta:
                dve.wait_ge(s_mt, 17)
                pm = K.ps[:, 0, 0:KT * META].rearrange("p (k m) -> p k m", m=META)
                ch.link(dve, dve.tensor_copy(K.nx_hi[:, :, 0:META], pm))
                dve.tensor_tensor(K.nx_lo[:, :, 0:META], pm, K.nx_hi[:, :, 0:META].bitcast(F32), ALU.subtract)

        @block.tensor
        def _(pe):
            for k in range(KT):
                for t in range(TT):
                    if k == 0:
                        pe.wait_ge(s_xn, t + 1)
                    tr = pe.transpose(K.ps[:, k, t * P:(t + 1) * P], xn[:, t, k * P:(k + 1) * P], cst(K, "ident"))
                tr.then_inc(s_tr, 1)
            if meta:
                pe.wait_ge(s_xn, nt)
                pe.wait_ge(s_ev, 1)
                for k in range(KT):
                    tr = pe.transpose(K.ps[:, 0, k * META:(k + 1) * META], xn[0:META, TT, k * P:(k + 1) * P],
                                      cst(K, "ident", META)[:, 0:META])
                tr.then_inc(s_mt, 1)



def start(K, v, wait_x=True):
    s_in, = sems(K, "inputs_in")
    with K.nc.Block() as block:
        @block.sync
        def _(sp):
            sp.dma_start(K.h[:], v["x"].rearrange("b (t p) d -> p (b t) d", p=P)).then_inc(s_in, 16)
            for g in range(RAW):
                sp.dma_start(K.raw[:, g], K.stream[g]).then_inc(K.s_raw[g], 16)
            sp.dma_start(K.const[:], v["const"]).then_inc(s_in, 16)
            sp.dma_start(K.param[:], v["param"]).then_inc(s_in, 16)
            sp.wait_ge(s_in, 48)

        @block.scalar
        def _(act):
            for g in range(HL):
                act.wait_ge(K.s_raw[g], 16)
                act.activation(K.whi[:, g], K.raw[:, g], ACT.Copy).then_inc(K.s_hi, 1)

        @block.vector
        def _(dve):
            dve.memset(K.t_ss[:], 1.0)
            for g in range(HL):
                dve.wait_ge(K.s_hi, g + 1)
                dve.tensor_tensor(K.wlo[:, g], K.raw[:, g], K.whi[:, g].bitcast(F32), ALU.subtract).then_inc(K.s_lo, 1)



def project1(K, R):
    product_rows512(K, K.at, 4, K.nx_hi, K.nx_lo, 0,
                    lambda act, c, u, banks: act.activation(
                        R.rows[:, ds(c * 512 - 3 * 512, 2048)], banks.rearrange("p a b -> p (a b)"), ACT.Copy))
    K.at += 16
    product_cols(K, K.at, 8, None, None, [(K.nx_hi, K.nx_lo, [(0, SEQ)])], {
        "frees": "act",
        "act": lambda act, c, u, turn, b, s_free: act.activation(
            R.cols[:, ds(c * 512, 512)], K.ps[:, b, :], ACT.Copy).then_inc(s_free, 1)})
    K.at += 8



def rope(K, dve, x, cos, sin, t):
    ch = K.dve_chain
    x1, x2 = x
    dve.tensor_tensor(t[0], x1, cos, ALU.mult)
    dve.tensor_tensor(t[1], x2, sin, ALU.mult)
    dve.tensor_tensor(t[2], x2, cos, ALU.mult)
    ch.link(dve, dve.tensor_tensor(t[3], x1, sin, ALU.mult))
    dve.tensor_tensor(x1, t[0], t[1], ALU.subtract)
    ch.link(dve, dve.tensor_tensor(x2, t[2], t[3], ALU.add))


def nsa_prepare(K, R, v):
    s_ss, s_rt, s_q, s_kd, s_tr, s_ev, s_x2, s_w1, s_w1b, s_wu, s_tb, s_g, s_gt, s_gc, s_o2, s_kt, s_gate = sems(
        K, "square_sums", "roots", "q_rows", "k_rows", "transposed", "evacuated", "pairs_in", "w1_even_in",
        "w1_odd_in", "w1_used", "blocks", "gelu", "gelu_t", "gelu_tc", "cmp_out", "cmp_k_t", "gates_t")
    rows = R.rows.rearrange("p (g t c) -> p g t c", g=4, t=TT)
    cols = R.cols.rearrange("p (f t) -> p f t", f=8)
    q = rows[:, 0].rearrange("p t (h d) -> p (t h) d", d=64)
    ks = [rows[:, 1, :, b * 256:b * 256 + 128].rearrange("p t (g d) -> p t g d", d=64) for b in range(2)]
    with ExitStack() as c:
        ss = scratch(K, c, "ss", [P, 48])
        rt = scratch(K, c, "rt", [P, 48])
        tmp = scratch(K, c, "rope_t", [P, 4, 256])
        kd = scratch(K, c, "k_dup", [P, TT, 4, 2, 64])
        x2 = scratch(K, c, "x_pairs", [P, 4, SEQ])
        tb = scratch(K, c, "x_blocks", [P, 2, CMP_J, 64])
        sq = tb.rearrange("p a b c -> p (a b c)")
        w1 = scratch(K, c, "cmp_w1", [P, 2, 4, 256])
        gl = scratch(K, c, "gelu", [64, 2, 256])
        glt = scratch(K, c, "gelu_t", [P, 2, 2, 64])
        kc = scratch(K, c, "k_cmp", [64, 2, 64])
        s64 = scratch(K, c, "s64", [64, 4])
        t64 = scratch(K, c, "t64", [64, 64 + 32])
        n_ss = 3

        with K.nc.Block() as block:
            @block.sync
            def _(sp):
                for kind in range(2):
                    for g in range(NSA_G):
                        src = cols[g * 64:g * 64 + 64, kind]
                        sp.dma_start(x2[0:64, 2 * kind + g, :], src).then_inc(s_x2, 16)
                        sp.dma_start(x2[64:128, 2 * kind + g, 0:SEQ - 1], src[:, 1:SEQ]).then_inc(s_x2, 16)
                for i in range(8):
                    w = (v["cmp_w1_k"], v["cmp_w1_v"])[i // 4].rearrange("(j p) n -> p j n", p=P)
                    if i >= 2:
                        sp.wait_ge(s_wu, i - 1)
                    sp.dma_start(w1[:, i % 2], w[:, 4 * (i % 4):4 * (i % 4) + 4]).then_inc((s_w1, s_w1b)[i % 2], 16)

            @block.vector
            def _(dve):
                ch = K.dve_chain
                eps_q = 64 * EPS
                ch.link(dve, dve.tensor_tensor(sq[:], rows[:, 0].rearrange("p t c -> p (t c)"),
                                               rows[:, 0].rearrange("p t c -> p (t c)"), ALU.mult))
                ch.link(dve, dve.tensor_reduce(ss[:, 0:32], sq.rearrange("p (a d) -> p a d", d=64), AX.X, ALU.add))
                ch.link(dve, dve.tensor_scalar(ss[:, 0:32], ss[:, 0:32], eps_q, None, ALU.add))
                for b in range(2):
                    sqk = sq[:, 0:512].rearrange("p (t g d) -> p t g d", t=TT, g=2)
                    ch.link(dve, dve.tensor_tensor(sqk, ks[b], ks[b], ALU.mult))
                    ch.link(dve, dve.tensor_reduce(ss[:, 32 + 8 * b:40 + 8 * b],
                                                   sq[:, 0:512].rearrange("p (a d) -> p a d", d=64), AX.X, ALU.add))
                dve.tensor_scalar(ss[:, 32:48], ss[:, 32:48], 1.0 / 64, EPS, ALU.mult, ALU.add).then_inc(s_ss, 1)
                dve.wait_ge(s_rt, 1)
                ch.link(dve, dve.reciprocal(rt[:], rt[:]))
                ch.link(dve, dve.tensor_tensor(q, q, bc(rt[:, 0:32], [P, 32, 64], 2), ALU.mult))
                ch.link(dve, dve.tensor_tensor(q, q, bc(par(K, "q_gain"), [P, 32, 64], 1), ALU.mult))
                cos = cst(K, "cos").rearrange("p (t d) -> p t d", d=8)
                sin = cst(K, "sin").rearrange("p (t d) -> p t d", d=8)
                q4 = rows[:, 0].rearrange("p t (h d) -> p t h d", d=64)
                tq = [tmp[:, i].rearrange("p (t h d) -> p t h d", t=TT, h=8) for i in range(4)]
                rope(K, dve, (q4[:, :, :, 0:8], q4[:, :, :, 8:16]), bc(cos, [P, TT, 8, 8], 2),
                     bc(sin, [P, TT, 8, 8], 2), tq)
                dve.nop().then_inc(s_q, 1)
                for b in range(2):
                    r = rt[:, 32 + 8 * b:40 + 8 * b].rearrange("p (t g) -> p t g", t=TT)
                    ch.link(dve, dve.tensor_tensor(ks[b], ks[b], bc(r, [P, TT, 2, 64], 3), ALU.mult))
                    gain = par(K, f"k_gain{b + 1}").unsqueeze(1).unsqueeze(1).to_broadcast([P, TT, 2, 64])
                    ch.link(dve, dve.tensor_tensor(ks[b], ks[b], gain, ALU.mult))
                    tk = [tmp[:, i, 0:64].rearrange("p (t g d) -> p t g d", t=TT, g=2) for i in range(4)]
                    rope(K, dve, (ks[b][:, :, :, 0:8], ks[b][:, :, :, 8:16]), bc(cos, [P, TT, 2, 8], 2),
                         bc(sin, [P, TT, 2, 8], 2), tk)
                    for copy in range(2):
                        dve.tensor_copy(kd[:, :, 2 * b:2 * b + 2, copy, :], ks[b]).then_inc(s_kd, 1)
                ch.link(dve, dve.memset(tb[:], 0.0))
                dve.wait_ge(s_x2, 16 * 8)
                for kind in range(2):
                    pe_ = par(K, ("pe_k", "pe_v")[kind])
                    for g in range(NSA_G):
                        xs = x2[:, 2 * kind + g, :].rearrange("p (n s) -> p s n", s=16)
                        for hf in range(2):
                            dst = tb[:, kind, 8 * hf:8 * hf + 8, 32 * g:32 * g + N_CMP]
                            dve.tensor_tensor(dst, xs[:, 0:16:2, hf:hf + N_CMP],
                                              bc(pe_[:, 8 * hf:8 * hf + 8], [P, 8, N_CMP], 2), ALU.add).then_inc(s_tb, 1)
                dve.wait_ge(s_gt, 1)
                dve.tensor_copy(glt.rearrange("p a b c -> p (a b c)"), K.ps[:, 2, 0:256]).then_inc(s_gc, 1)
                dve.wait_ge(s_o2, 1)
                dve.tensor_copy(R.vcmp[:], K.ps[0:64, 3, 64:128])
                ch.link(dve, dve.tensor_copy(kc[:, 0], K.ps[0:64, 3, 0:64]))
                ch.link(dve, dve.tensor_tensor(t64[:, 0:64], kc[:, 0], kc[:, 0], ALU.mult))
                ch.link(dve, dve.tensor_reduce(s64[:, 0:1], t64[:, 0:64], AX.X, ALU.add))
                dve.tensor_scalar(s64[:, 1:2], s64[:, 0:1], 1.0 / 64, EPS, ALU.mult, ALU.add).then_inc(s_ss, 1)
                dve.wait_ge(s_rt, 2)
                ch.link(dve, dve.reciprocal(s64[:, 2:3], s64[:, 2:3]))
                ch.link(dve, dve.scalar_tensor_tensor(kc[:, 0], kc[:, 0], s64[:, 2:3], par(K, "k_gain0", 64), ALU.mult, ALU.mult))
                rope(K, dve, (kc[:, 0, 0:8], kc[:, 0, 8:16]), cst(K, "cos_cmp", 64), cst(K, "sin_cmp", 64),
                     [t64[:, 64 + 8 * i:72 + 8 * i] for i in range(4)])
                dve.tensor_copy(kc[:, 1], kc[:, 0]).then_inc(s_kt, 1)
                dve.wait_ge(s_kt, 2)
                dve.tensor_copy(R.kcT[:], K.ps[:, 3, 128:192])

            @block.scalar
            def _(act):
                act.wait_ge(s_ss, 1)
                act.activation(rt[:], ss[:], ACT.Sqrt).then_inc(s_rt, 1)
                for i in range(8):
                    act.wait_ge(s_tr, i + 1)
                    dst = R.qT[:, i, :] if i < 4 else R.kT[:, i - 4, :]
                    act.activation(dst, K.ps[:, 4 + i % 4, :], ACT.Copy).then_inc(s_ev, 1)
                act.wait_ge(s_gate, 1)
                act.activation(R.gates[:], K.ps[:, 2, 0:96], ACT.Sigmoid)
                for kind in range(2):
                    act.wait_ge(s_wu, 4 * kind + 4)
                    act.activation(gl[:, kind], K.ps[0:64, kind, 0:256], ACT.Gelu_apprx_tanh).then_inc(s_g, 1)
                act.wait_ge(s_ss, 2)
                act.activation(s64[:, 2:3], s64[:, 1:2], ACT.Sqrt).then_inc(s_rt, 1)

            @block.tensor
            def _(pe):
                ident = cst(K, "ident")
                for t in range(TT):
                    tr = pe.transpose(K.ps[:, 2, 24 * t:24 * t + 24], cols[0:24, 2, t * P:(t + 1) * P],
                                      cst(K, "ident", 24)[:, 0:24])
                tr.then_inc(s_gate, 1)
                pe.wait_ge(s_q, 1)
                for i in range(4):
                    for t in range(TT):
                        tr = pe.transpose(K.ps[:, 4 + i, t * P:(t + 1) * P], rows[:, 0, t, i * P:(i + 1) * P], ident)
                    tr.then_inc(s_tr, 1)
                pe.wait_ge(s_kd, 4)
                for i in range(4):
                    pe.wait_ge(s_ev, i + 1)
                    for t in range(TT):
                        tr = pe.transpose(K.ps[:, 4 + i, t * P:(t + 1) * P],
                                          kd[:, t, i].rearrange("p c d -> p (c d)"), ident)
                    tr.then_inc(s_tr, 1)
                for kind in range(2):
                    pe.wait_ge(s_tb, 4 * kind + 4)
                    for j in range(CMP_J):
                        i = 4 * kind + j // 4
                        if j % 4 == 0:
                            pe.wait_ge((s_w1, s_w1b)[i % 2], 16 * (i // 2 + 1))
                        mm = pe.matmul(K.ps[0:64, kind, 0:256], tb[:, kind, j], w1[:, i % 2, j % 4], start=j == 0, stop=j == CMP_J - 1)
                        if j % 4 == 3:
                            mm.then_inc(s_wu, 1)
                for kind in range(2):
                    pe.wait_ge(s_g, kind + 1)
                    for f in range(2):
                        tr = pe.transpose(K.ps[:, 2, (2 * kind + f) * 64:(2 * kind + f + 1) * 64],
                                          gl[:, kind, f * P:(f + 1) * P], cst(K, "ident", 64)[:, 0:64])
                tr.then_inc(s_gt, 1)
                pe.wait_ge(s_gc, 1)
                for kind in range(2):
                    w2 = par(K, ("cmp_w2_k", "cmp_w2_v")[kind])
                    for f in range(2):
                        mm = pe.matmul(K.ps[0:64, 3, 64 * kind:64 * kind + 64], glt[:, kind, f], w2[:, f * 64:f * 64 + 64],
                                       start=f == 0, stop=f == 1)
                mm.then_inc(s_o2, 1)
                pe.wait_ge(s_kt, 1)
                pe.transpose(K.ps[:, 3, 128:192], kc.rearrange("p c d -> p (c d)"), cst(K, "ident", 64)[:, 0:64]).then_inc(s_kt, 1)


def nsa_attend(K, R):
    s_sc, s_mx, s_ex, s_w, s_trs, s_pt, s_ptc, s_pv, s_oc, s_oh = sems(
        K, "scores", "maxima", "probs", "weighted", "transposed", "probs_t", "probs_tc", "pv", "o_copied", "o_hi")
    rows = R.rows.rearrange("p (g t c) -> p g t c", g=4, t=TT)
    keep = cst(K, "cmp_keep").rearrange("p (t g n) -> p t g n", t=TT, g=2)
    cbias = cst(K, "cmp_bias").rearrange("p (t g n) -> p t g n", t=TT, g=2)
    units = [(h, t) for h in range(NSA_H) for t in range(TT)]
    NU = len(units)
    with ExitStack() as c:
        pr = scratch(K, c, "probs", [P, 2, 2, SEQ])
        pc = scratch(K, c, "probs_c", [P, 2, 64])
        pt = scratch(K, c, "probs_t", [P, 2, 2, SEQ])
        ptc = scratch(K, c, "probs_tc", [64, 2, P])
        mx = scratch(K, c, "max", [P, 2, 3])
        sm = scratch(K, c, "sum", [P, 2, 3])
        fc = scratch(K, c, "factor", [P, 2, 3])
        CB = lambda u: K.ps[:, 3 * (u % 2) + 2, 0:64]
        CT = lambda u: K.ps[0:64, 3 * (u % 2) + 2, 256:384]

        with K.nc.Block() as block:
            @block.tensor
            def _(pe):
                ident, causal = cst(K, "ident"), cst(K, "causal")

                def scores(u):
                    h, t = units[u]
                    g, b0 = h // 4, 64 * (h % 2)
                    qt = R.qT[b0:b0 + 64, h // 2, t * P:(t + 1) * P]
                    ext = (t + 1) * P
                    if u >= 2:
                        pe.wait_ge(s_ex, 3 * (u - 1))
                    for b in range(2):
                        out = K.ps[:, 3 * (u % 2) + b, 0:ext]
                        pe.matmul(out, qt, R.kT[b0:b0 + 64, 2 * b + g, 0:ext], start=True, stop=False, skip_group_check=True)
                        pe.matmul(out[:, t * P:ext], ident, causal, start=False, stop=True, skip_group_check=True)
                    pe.matmul(CB(u), qt, R.kcT[b0:b0 + 64, :], start=True, stop=False, skip_group_check=True)
                    pe.matmul(CB(u), ident, cbias[:, t, g, :], start=False, stop=True,
                              skip_group_check=True).then_inc(s_sc, 1)

                def values(u):
                    h, t = units[u]
                    g, b0 = h // 4, 64 * (h % 2)
                    out = K.ps[b0:b0 + 64, 7, t * P:(t + 1) * P]

                    def transposed(b):
                        for kt in range(t + 1):
                            tr = pe.transpose(K.ps[:, 6, kt * P:(kt + 1) * P], pr[:, u % 2, b, kt * P:(kt + 1) * P], ident)
                        tr.then_inc(s_trs, 1)

                    def summed(b):
                        for kt in range(t + 1):
                            vv = rows[:, 1, kt, 256 * b + 128 + g * 64:256 * b + 192 + g * 64]
                            mm = pe.matmul(out, vv, pt[:, u % 2, b, kt * P:(kt + 1) * P], start=b == 0 and kt == 0,
                                           stop=b == 1 and kt == t, skip_group_check=True)
                        return mm
                    pe.wait_ge(s_w, 3 * u + 1)
                    transposed(0)
                    pe.wait_ge(s_w, 3 * u + 2)
                    pe.transpose(CT(u), pc[:, u % 2, :], ident).then_inc(s_trs, 1)
                    pe.wait_ge(s_w, 3 * u + 3)
                    pe.wait_ge(s_pt, u + 1)
                    transposed(1)
                    if h % 2 == 0 and t == 0 and h >= 2:
                        pe.wait_ge(s_oc, h // 2)
                    summed(0)
                    pe.wait_ge(s_ptc, 2 * u + 1)
                    pe.matmul(out, R.vcmp[:], ptc[:, u % 2, :], start=False, stop=False, skip_group_check=True)
                    pe.wait_ge(s_ptc, 2 * u + 2)
                    summed(1).then_inc(s_pv, 1)
                scores(0)
                for u in range(NU):
                    if u + 1 < NU:
                        scores(u + 1)
                    values(u)

            @block.vector
            def _(dve):
                ch = K.dve_chain
                def maxima(u):
                    h, t = units[u]
                    dve.wait_ge(s_sc, u + 1)
                    for b in range(2):
                        dve.tensor_reduce(mx[:, u % 2, b + 1:b + 2], K.ps[:, 3 * (u % 2) + b, 0:(t + 1) * P], AX.X, ALU.max, negate=True)
                    dve.tensor_reduce(mx[:, u % 2, 0:1], CB(u), AX.X, ALU.max, negate=True).then_inc(s_mx, 1)

                def weights(u):
                    h, t = units[u]
                    g = h // 4
                    dve.wait_ge(s_ex, 3 * u + 3)
                    ch.link(dve, dve.reciprocal(fc[:, u % 2, :], sm[:, u % 2, :]))
                    ch.link(dve, dve.tensor_tensor(fc[:, u % 2, :], fc[:, u % 2, :],
                                                   R.gates[:, t * 24 + h * 3:t * 24 + h * 3 + 3], ALU.mult))
                    for b in range(2):
                        p = pr[:, u % 2, b, 0:(t + 1) * P]
                        dve.tensor_scalar(p, p, fc[:, u % 2, b + 1:b + 2], None, ALU.mult).then_inc(s_w, 1)
                        if b == 0:
                            dve.scalar_tensor_tensor(pc[:, u % 2, :], pc[:, u % 2, :], fc[:, u % 2, 0:1],
                                                     keep[:, t, g, :], ALU.mult, ALU.mult).then_inc(s_w, 1)

                def copies(u):
                    h, t = units[u]
                    dve.wait_ge(s_trs, 3 * u + 2)
                    if u >= 2:
                        dve.wait_ge(s_pv, u - 1)
                    dve.tensor_copy(ptc[:, u % 2, :], CT(u)).then_inc(s_ptc, 1)
                    dve.wait_ge(s_trs, 3 * u + 3)
                    dve.tensor_copy(pt[:, u % 2, 1, 0:(t + 1) * P], K.ps[:, 6, 0:(t + 1) * P]).then_inc(s_ptc, 1)
                    if h % 2 == 1 and t == TT - 1:
                        i = h // 2
                        dve.wait_ge(s_oh, i + 1)
                        dve.tensor_tensor(K.nx_lo[:, i, 0:SEQ], K.ps[:, 7, :], K.nx_hi[:, i, 0:SEQ].bitcast(F32),
                                          ALU.subtract).then_inc(s_oc, 1)
                maxima(0)
                for u in range(NU):
                    weights(u)
                    if u + 1 < NU:
                        maxima(u + 1)
                    copies(u)

            @block.scalar
            def _(act):
                def exps(u):
                    h, t = units[u]
                    act.wait_ge(s_mx, u + 1)
                    if u >= 2:
                        act.wait_ge(s_trs, 3 * (u - 2) + 3)
                    for b in range(2):
                        act.activation(pr[:, u % 2, b, 0:(t + 1) * P], K.ps[:, 3 * (u % 2) + b, 0:(t + 1) * P], ACT.Exp,
                                       bias=mx[:, u % 2, b + 1:b + 2], accum_out=sm[:, u % 2, b + 1:b + 2]).then_inc(s_ex, 1)
                    act.activation(pc[:, u % 2, :], CB(u), ACT.Exp, bias=mx[:, u % 2, 0:1],
                                   accum_out=sm[:, u % 2, 0:1]).then_inc(s_ex, 1)

                def copies(u):
                    h, t = units[u]
                    if u >= 2:
                        act.wait_ge(s_pv, u - 1)
                    act.wait_ge(s_trs, 3 * u + 1)
                    act.activation(pt[:, u % 2, 0, 0:(t + 1) * P], K.ps[:, 6, 0:(t + 1) * P], ACT.Copy).then_inc(s_pt, 1)
                    if h % 2 == 1 and t == TT - 1:
                        i = h // 2
                        act.wait_ge(s_pv, u + 1)
                        act.activation(K.nx_hi[:, i, 0:SEQ], K.ps[:, 7, :], ACT.Copy).then_inc(s_oh, 1)
                for u in range(NU):
                    exps(u)
                    if u >= 1:
                        copies(u - 1)
                copies(NU - 1)



def gla(K, R):
    (s_x, s_xb, s_ab, s_la, s_b, s_eb, s_bl, s_kd, s_kt, s_kc, s_at, s_am, s_ds, s_st, s_o, s_of, s_ss, s_rt,
     s_on, s_tr, s_hi, s_lo) = sems(
        K, "gate_logits", "biased", "log_parts", "log_a", "cum", "exps", "last", "k_decayed", "kd_t", "kd_rows",
        "scores_t", "masked_t", "states_in", "states", "o_sums", "o_free", "squares", "roots", "normed", "o_t", "o_hi", "o_lo")
    rows = R.rows.rearrange("p (g t c) -> p g t c", g=4, t=TT)
    cols = R.cols.rearrange("p (f t) -> p f t", f=8)
    gv, gout, glr = rows[:, 2], rows[:, 3], cols[0:16, 7]
    with ExitStack() as c:
        la = scratch(K, c, "log_a", [P, TT, 256])
        e1 = scratch(K, c, "exp1", [P, TT, 256])
        eb = scratch(K, c, "exp_b", [P, 2, SEQ])
        enb = scratch(K, c, "exp_nb", [P, 2, SEQ])
        ekd = scratch(K, c, "exp_kd", [P, 2, SEQ])
        bl = scratch(K, c, "b_last", [P, 2, 8])
        dec = scratch(K, c, "decay", [P, 2, 8])
        kd = scratch(K, c, "kd_rows", [P, TT, 256])
        am = scratch(K, c, "scores_m", [P, 2, GLA_H, P])
        st = scratch(K, c, "states", [P, 8, 2, P])
        o, sil = rows[:, 0], gout
        sq = scratch(K, c, "sq", [P, 512])
        ss = scratch(K, c, "ss", [P, 32])
        qt, kt, kdt = eb, enb, ekd

        with K.nc.Block() as block:
            @block.tensor
            def _(pe):
                ident, tri = cst(K, "ident"), cst(K, "tri_incl")
                for t in range(TT):
                    mm = pe.matmul(K.ps[:, t // 2, 256 * (t % 2):256 * (t % 2) + 256], glr[:, t * P:(t + 1) * P],
                                   par(K, "w_gate2", 16), start=True, stop=True)
                mm.then_inc(s_x, 1)
                pe.wait_ge(s_la, 1)
                for f in range(2):
                    for t in range(TT):
                        mm = pe.matmul(K.ps[:, 2 + f, t * P:(t + 1) * P], la[:, t, f * P:(f + 1) * P], tri, start=True, stop=True)
                mm.then_inc(s_b, 1)
                pe.wait_ge(s_kd, 1)
                for f in range(2):
                    for t in range(TT):
                        tr = pe.transpose(K.ps[:, 4 + t // 2, 256 * (t % 2) + f * P:256 * (t % 2) + (f + 1) * P],
                                          kdt[:, f, t * P:(t + 1) * P], ident)
                tr.then_inc(s_kt, 1)
                pe.wait_ge(s_kc, 1)
                for ck in range(8):
                    t, r0 = ck // 2, CH * (ck % 2)
                    for hh in range(GLA_H):
                        b0, at = 64 * (hh % 2), 256 * (ck // 2 % 2) + P * (hh // 2)
                        mm = pe.matmul(K.ps[b0:b0 + 64, 2 * (ck % 2) + ck // 4, at:at + P],
                                       kd[r0:r0 + 64, t, hh * 64:hh * 64 + 64], gv[r0:r0 + 64, t, hh * P:(hh + 1) * P],
                                       start=True, stop=True, skip_group_check=True)
                    mm.then_inc(s_ds, 1)

                def scores(t):
                    if t >= 1:
                        pe.wait_ge(s_am, t)
                    for hh in range(GLA_H):
                        b0, f = 64 * (hh % 2), hh // 2
                        mm = pe.matmul(K.ps[:, 4 + hh % 2, f * P:(f + 1) * P], kt[b0:b0 + 64, f, t * P:(t + 1) * P],
                                       qt[b0:b0 + 64, f, t * P:(t + 1) * P], start=True, stop=True)
                    mm.then_inc(s_at, 1)
                scores(0)
                for t in range(TT):
                    if t + 1 < TT:
                        scores(t + 1)
                    pe.wait_ge(s_am, t + 1)
                    pe.wait_ge(s_st, min(2 * t + 1, 7))
                    if t >= 1:
                        pe.wait_ge(s_of, t)
                    for hh in range(GLA_H):
                        b0, f = 64 * (hh % 2), hh // 2
                        pe.matmul(K.ps[:, 6 + hh % 2, f * P:(f + 1) * P], am[:, t % 2, hh], gv[:, t, hh * P:(hh + 1) * P],
                                  start=True, stop=False, skip_group_check=True)
                        for c2 in range(2):
                            mm = pe.matmul(K.ps[64 * c2:64 * c2 + 64, 6 + hh % 2, f * P:(f + 1) * P],
                                           qt[b0:b0 + 64, f, t * P + 64 * c2:t * P + 64 * c2 + 64],
                                           st[b0:b0 + 64, 2 * t + c2, f], start=False, stop=c2 == 1, skip_group_check=True)
                    mm.then_inc(s_o, 1)
                pe.wait_ge(s_on, 1)
                for hh in range(GLA_H):
                    for t in range(TT):
                        tr = pe.transpose(K.ps[:, hh, t * P:(t + 1) * P], o[:, t, hh * P:(hh + 1) * P], ident)
                    tr.then_inc(s_tr, 1)

            @block.vector
            def _(dve):
                ch = K.dve_chain
                dve.wait_ge(s_x, 1)
                x4 = K.ps[:, 0:2, :].rearrange("p a (b c) -> p (a b) c", b=2)
                dve.tensor_tensor(la[:], x4, bc(par(K, "b_gate"), [P, TT, 256], 1), ALU.add).then_inc(s_xb, 1)
                dve.wait_ge(s_ab, 1)
                dve.scalar_tensor_tensor(la.rearrange("p t c -> p (t c)"), la.rearrange("p t c -> p (t c)"), 0.0,
                                         e1.rearrange("p t c -> p (t c)"), ALU.min, ALU.subtract).then_inc(s_la, 1)
                dve.wait_ge(s_b, 1)
                for f in range(2):
                    last = dve.tensor_scalar(bl[:, f, :], K.ps[:, 2 + f, CH - 1::CH], 1.0 / 16, None, ALU.mult)
                last.then_inc(s_bl, 1)
                dve.wait_ge(s_eb, 1)
                for f in range(2):
                    last = dve.tensor_tensor(kdt[:, f], kdt[:, f], cols[:, 5 + f], ALU.mult)
                last.then_inc(s_kd, 1)
                for f in range(2):
                    dve.scalar_tensor_tensor(qt[:, f], qt[:, f], GLA_SCALE, cols[:, 3 + f], ALU.mult, ALU.mult)
                    last = dve.tensor_tensor(kt[:, f], kt[:, f], cols[:, 5 + f], ALU.mult)
                last.then_inc(s_kd, 1)
                dve.wait_ge(s_kt, 1)
                dve.tensor_copy(kd.rearrange("p t c -> p (t c)"), K.ps[:, 4:6, :].rearrange("p a b -> p (a b)")).then_inc(s_kc, 1)

                def mask(t):
                    dve.wait_ge(s_at, t + 1)
                    if t >= 2:
                        dve.wait_ge(s_o, t - 1)
                    dve.tensor_tensor(am[:, t % 2].rearrange("p (f b) c -> p b f c", b=2),
                                      K.ps[:, 4:6, 0:256].rearrange("p b (f c) -> p b f c", f=2),
                                      cst(K, "tri_incl").unsqueeze(1).unsqueeze(1).to_broadcast([P, 2, 2, P]),
                                      ALU.mult).then_inc(s_am, 1)

                def evac(t):
                    dve.wait_ge(s_o, t + 1)
                    dve.tensor_copy(o[:, t, :].rearrange("p (f b c) -> p b f c", f=2, b=2),
                                    K.ps[:, 6:8, 0:256].rearrange("p b (f c) -> p b f c", f=2)).then_inc(s_of, 1)
                mask(0)
                ch.link(dve, dve.memset(st[:, 0], 0.0))
                for ck in range(7):
                    dve.wait_ge(s_ds, 4 * (ck // 4) + 4)
                    at = 256 * (ck // 2 % 2)
                    for f in range(2):
                        last = dve.scalar_tensor_tensor(st[:, ck + 1, f], st[:, ck, f], dec[:, f, ck:ck + 1],
                                                        K.ps[:, 2 * (ck % 2) + ck // 4, at + f * P:at + (f + 1) * P],
                                                        ALU.mult, ALU.add)
                    last.then_inc(s_st, 1)
                    dve.wait_ge(s_st, ck + 1)
                for t in range(1, TT):
                    mask(t)
                    evac(t - 1)
                evac(TT - 1)
                for t in range(TT):
                    dve.wait_ge(s_of, t + 1)
                    ch.link(dve, dve.tensor_tensor(sq[:], o[:, t], o[:, t], ALU.mult))
                    ch.link(dve, dve.tensor_reduce(ss[:, 4 * t:4 * t + 4], sq.rearrange("p (h c) -> p h c", h=4), AX.X, ALU.add))
                dve.tensor_scalar(ss[:, 0:16], ss[:, 0:16], 1.0 / P, EPS, ALU.mult, ALU.add).then_inc(s_ss, 1)
                dve.wait_ge(s_rt, 1)
                ch.link(dve, dve.reciprocal(ss[:, 16:32], ss[:, 16:32]))
                o16 = o.rearrange("p t (h c) -> p (t h) c", h=4)
                ch.link(dve, dve.tensor_tensor(o16, o16, bc(ss[:, 16:32], [P, 16, P], 2), ALU.mult))
                ch.link(dve, dve.tensor_tensor(o16, o16, bc(par(K, "gla_gain"), [P, 16, P], 1), ALU.mult))
                dve.tensor_tensor(o, o, sil, ALU.mult).then_inc(s_on, 1)
                for hh in range(GLA_H):
                    dve.wait_ge(s_hi, hh + 1)
                    dve.tensor_tensor(K.nx_lo[:, 4 + hh, 0:SEQ], K.ps[:, hh, :], K.nx_hi[:, 4 + hh, 0:SEQ].bitcast(F32), ALU.subtract)

            @block.scalar
            def _(act):
                ch = K.act_chain
                act.wait_ge(s_xb, 1)
                ch.link(act, act.activation(e1[:], la[:], ACT.Abs))
                ch.link(act, act.activation(e1[:], e1[:], ACT.Exp, scale=-1.0))
                act.activation(e1[:], e1[:], ACT.Ln, bias=1.0).then_inc(s_ab, 1)
                act.wait_ge(s_bl, 1)
                act.activation(eb[:], K.ps[:, 2:4, :], ACT.Exp, scale=1.0 / 16)
                act.activation(enb[:], K.ps[:, 2:4, :], ACT.Exp, scale=-1.0 / 16)
                act.activation(dec[:], bl[:], ACT.Exp)
                for f in range(2):
                    for ck in range(8):
                        last = act.activation(ekd[:, f, ck * CH:(ck + 1) * CH], K.ps[:, 2 + f, ck * CH:(ck + 1) * CH], ACT.Exp,
                                              bias=bl[:, f, ck:ck + 1], scale=-1.0 / 16)
                last.then_inc(s_eb, 1)
                act.activation(sil, gout, ACT.Silu)
                act.wait_ge(s_ss, 1)
                act.activation(ss[:, 16:32], ss[:, 0:16], ACT.Sqrt).then_inc(s_rt, 1)
                for hh in range(GLA_H):
                    act.wait_ge(s_tr, hh + 1)
                    act.activation(K.nx_hi[:, 4 + hh, 0:SEQ], K.ps[:, hh, :], ACT.Copy).then_inc(s_hi, 1)


GLA_SCALE = 64 ** -0.5



def ffn_up(K, act_hi, act_lo, conv, tok0):
    with ExitStack() as c:
        g = scratch(K, c, "gate", [P, 2, SEQ])
        up = scratch(K, c, "up", [P, 2, SEQ])
        w1 = par(K, "conv1_w").rearrange("p (k f t) -> p k f t", k=2, t=3)
        b1 = par(K, "conv1_b").rearrange("p (k f) -> p k f", k=2)

        def evac_act(act, ch, u, turn, b, s_free):
            s_first, s_silu, s_full, s_hi = evac["signals"]
            kind, pb, pair = u % 2, u // 2 % 2, turn * 2 + u // 2
            if conv:
                act.activation((g, up)[kind][:, pb], K.ps[:, b, :], ACT.Identity,
                               scale=w1[:, kind, ds(pair, 1), 2], bias=b1[:, kind, ds(pair, 1)]).then_inc(s_first, 1)
                if kind == 1:
                    act.wait_ge(s_free, ch + 2)
                    act.activation(g[:, pb], g[:, pb], ACT.Silu).then_inc(s_silu, 1)
            elif kind == 0:
                act.activation(g[:, pb], K.ps[:, b, :], ACT.Silu).then_inc(s_silu, 1)
            if kind == 1:
                act.wait_ge(s_full, pair + 1)
                act.activation(act_hi[:, ds(pair, 1), :], up[:, pb].unsqueeze(1), ACT.Copy).then_inc(s_hi, 1)

        def evac_dve(dve, ch, u, turn, b, s_free):
            s_first, s_silu, s_full, s_hi = evac["signals"]
            kind, pb, pair = u % 2, u // 2 % 2, turn * 2 + u // 2
            y = (g, up)[kind][:, pb]
            if conv:
                dve.wait_ge(s_first, ch + 1)
                K.dve_chain.link(dve, dve.scalar_tensor_tensor(
                    y[:, 1:SEQ], K.ps[:, b, 0:SEQ - 1], w1[:, kind, ds(pair, 1), 1], y[:, 1:SEQ], ALU.mult, ALU.add))
                dve.scalar_tensor_tensor(y[:, 2:SEQ], K.ps[:, b, 0:SEQ - 2], w1[:, kind, ds(pair, 1), 0], y[:, 2:SEQ],
                                         ALU.mult, ALU.add).then_inc(s_free, 1)
                if kind == 1:
                    dve.wait_ge(s_free, ch + 3)
            elif kind == 0:
                dve.wait_ge(s_silu, pair + 1)
                dve.nop().then_inc(s_free, 1)
            if kind == 1:
                dve.wait_ge(s_silu, pair + 1)
                if conv:
                    dve.tensor_tensor(y, y, g[:, pb], ALU.mult).then_inc(s_full, 1)
                else:
                    dve.tensor_tensor(y, K.ps[:, b, :], g[:, pb], ALU.mult).then_inc(s_full, 1)
                    dve.wait_ge(s_full, pair + 1)
                    dve.nop().then_inc(s_free, 1)
                dve.wait_ge(s_hi, pair + 1)
                dve.tensor_tensor(act_lo[:, ds(pair, 1), :], up[:, pb].unsqueeze(1),
                                  act_hi[:, ds(pair, 1), :].bitcast(F32), ALU.subtract)
        evac = {"frees": "dve", "act": evac_act, "dve": evac_dve,
                "sems": ("first_tap", "silu", "act_full", "act_hi")}
        product_cols(K, K.at, 2 * FT, None, None, [(K.nx_hi, K.nx_lo, [(tok0, tok0 + SEQ)])], evac,
                     dve_links=1 if conv else 0)
    K.at += 2 * FT


def block1(K, v):
    norm_stage(K, v["attn_gain"], None)
    with ExitStack() as c:
        R = Core()
        R.rows, R.cols = scratch(K, c, "rows", [P, 4 * 2048]), scratch(K, c, "cols", [P, 8 * 512])
        project1(K, R)
        with ExitStack() as c2:
            R.qT, R.kT = scratch(K, c2, "qT", [P, 4, SEQ]), scratch(K, c2, "kT", [P, 4, SEQ])
            R.kcT, R.vcmp = scratch(K, c2, "kcT", [P, 64]), scratch(K, c2, "vcmp", [64, 64])
            R.gates = scratch(K, c2, "gates", [P, TT * 24])
            nsa_prepare(K, R, v)
            nsa_attend(K, R)
        gla(K, R)
    product_rows(K, K.at, KT, K.nx_hi, K.nx_lo, None)
    K.at += KT
    norm_stage(K, v["ffn_gain"], None)
    with ExitStack() as c:
        act_hi, act_lo = scratch(K, c, "act_hi", [P, FT, SEQ], F32R), scratch(K, c, "act_lo", [P, FT, SEQ], F32R)
        ffn_up(K, act_hi, act_lo, True, 0)
        product_rows(K, K.at, FT, act_hi, act_lo, None)
        K.at += FT



FULL = [(0, HALF), (HALF, T2)]


def norm_cols(K, tiles):
    s_sq, s_ss, s_rt, s_out = sems(K, "squares", "sums", "roots", "normed")
    n = len(tiles)
    with ExitStack() as c:
        sq, rt = scratch(K, c, "sq", [P, 2, T2]), scratch(K, c, "rt", [P, 2, T2])
        with K.nc.Block() as block:
            @block.tensor
            def _(pe):
                for i in range(n):
                    pe.wait_ge(s_sq, i + 1)
                    if i >= 2:
                        pe.wait_ge(s_rt, i - 1)
                    for h, (a, e) in enumerate(FULL):
                        mm = pe.matmul(K.ps[:, 2 * (i % 2) + h, 0:HALF], cst(K, "ones"), sq[:, i % 2, a:e], start=True, stop=True)
                    mm.then_inc(s_ss, 1)

            @block.scalar
            def _(act):
                for i in range(n + 1):
                    if i < n:
                        if i >= 2:
                            act.wait_ge(s_ss, i - 1)
                        act.activation(sq[:, i % 2], tiles[i][0], ACT.Square).then_inc(s_sq, 1)
                    if i >= 1:
                        j = i - 1
                        act.wait_ge(s_ss, j + 1)
                        if j >= 2:
                            act.wait_ge(s_out, j - 1)
                        act.activation(rt[:, j % 2].rearrange("p (a b) -> p a b", a=2), K.ps[:, 2 * (j % 2):2 * (j % 2) + 2, 0:HALF],
                                       ACT.Sqrt, scale=tiles[j][1], bias=tiles[j][2]).then_inc(s_rt, 1)

            @block.vector
            def _(dve):
                for i, (x, _, _, gain) in enumerate(tiles):
                    dve.wait_ge(s_rt, i + 1)
                    K.dve_chain.link(dve, dve.reciprocal(rt[:, i % 2], rt[:, i % 2]))
                    if gain is None:
                        dve.tensor_tensor(x, x, rt[:, i % 2], ALU.mult).then_inc(s_out, 1)
                    else:
                        dve.scalar_tensor_tensor(x, x, gain, rt[:, i % 2], ALU.mult, ALU.mult).then_inc(s_out, 1)


def transpose_units(K, units):
    s_tr, s_act, s_dve = sems(K, "transposed", "even_copied", "odd_copied")
    with K.nc.Block() as block:
        @block.tensor
        def _(pe):
            for u, (dst, srcs) in enumerate(units):
                if u >= 8:
                    pe.wait_ge((s_act, s_dve)[u % 2], (u - 8) // 2 + 1)
                for j, src in enumerate(srcs):
                    k, m = src.shape
                    tr = pe.transpose(K.ps[0:m, u % 8, j * k:(j + 1) * k], src, cst(K, "ident", k)[:, 0:k])
                tr.then_inc(s_tr, 1)

        @block.scalar
        def _(act):
            for u, (dst, srcs) in enumerate(units):
                if u % 2 == 0:
                    act.wait_ge(s_tr, u + 1)
                    act.activation(dst, K.ps[0:dst.shape[0], u % 8, 0:dst.shape[1]], ACT.Copy).then_inc(s_act, 1)

        @block.vector
        def _(dve):
            for u, (dst, srcs) in enumerate(units):
                if u % 2 == 1:
                    dve.wait_ge(s_tr, u + 1)
                    dve.tensor_copy(dst, K.ps[0:dst.shape[0], u % 8, 0:dst.shape[1]]).then_inc(s_dve, 1)


def token_ranges():
    return [(t, P, META + t * P) for t in range(TT)] + [(TT, META, 0)]


def project_conv(K, dst, taps):
    with ExitStack() as c:
        z = scratch(K, c, "z", [P, 2, T2 + 3])
        y = scratch(K, c, "y", [P, 2, T2])

        def head(dve):
            K.dve_chain.link(dve, dve.memset(z[:, :, 0:3], 0.0))

        def evac_act(act, ch, u, turn, b, s_free):
            s_conv, = evac["signals"]
            act.activation(z[:, u % 2, 3:].rearrange("p (a b) -> p a b", a=2), K.ps[:, b:b + 2, 0:HALF], ACT.Copy).then_inc(s_free, 1)
            act.wait_ge(s_conv, ch + 1)
            act.activation(dst[:, ds(ch, 1), :], y[:, u % 2].unsqueeze(1), ACT.Silu)

        def evac_dve(dve, ch, u, turn, b, s_free):
            s_conv, = evac["signals"]
            dve.wait_ge(s_free, ch + 3)
            yy, zz = y[:, u % 2], z[:, u % 2]
            K.dve_chain.link(dve, dve.tensor_scalar(yy, zz[:, 3:], taps[:, ds(ch, 1), 3], None, ALU.mult))
            for j in (2, 1):
                K.dve_chain.link(dve, dve.scalar_tensor_tensor(yy, zz[:, j:j + T2], taps[:, ds(ch, 1), j], yy, ALU.mult, ALU.add))
            dve.scalar_tensor_tensor(yy, zz[:, 0:T2], taps[:, ds(ch, 1), 0], yy, ALU.mult, ALU.add).then_inc(s_conv, 1)
        evac = {"frees": "act", "act": evac_act, "dve": evac_dve, "sems": ("convolved",), "head_dve": head}
        product_cols(K, K.at, 8, None, None, [(K.nx_hi, K.nx_lo, FULL)], evac, dve_links=3)
    K.at += 8


def project_plain(K, n, dst):
    def evac_act(act, ch, u, turn, b, s_free):
        act.activation(dst[:, ds(ch, 1), :].rearrange("p o (a b) -> p (o a) b", a=2), K.ps[:, b:b + 2, 0:HALF],
                       ACT.Copy).then_inc(s_free, 1)
    product_cols(K, K.at, n, None, None, [(K.nx_hi, K.nx_lo, FULL)], {"frees": "act", "act": evac_act})
    K.at += n



def delta_gates(K, S):
    with ExitStack() as c:
        abT = scratch(K, c, "ab_cols", [P, 1, T2])
        ab = scratch(K, c, "ab_rows", [P, 5, 16])
        xa = scratch(K, c, "xa", [P, 5, 8])
        e1 = scratch(K, c, "e1", [P, 5, 8])
        ea = scratch(K, c, "exp_a_log", [P, 8])
        project_plain(K, 1, abT)
        s_tr, s_x, s_ln, s_ea, s_g, s_cum, s_e = sems(K, "transposed", "logits", "ln", "betas", "g", "cums", "exps")
        with K.nc.Block() as block:
            @block.tensor
            def _(pe):
                for t, rows, a in token_ranges():
                    tr = pe.transpose(K.ps[0:rows, 0, 16 * t:16 * t + 16], abT[0:16, 0, a:a + rows], cst(K, "ident", 16)[:, 0:16])
                tr.then_inc(s_tr, 1)
                pe.wait_ge(s_g, 1)
                for t, rows, a in token_ranges():
                    g = S.g[0:rows, t, :]
                    pe.matmul(K.ps[0:rows, 1, 8 * t:8 * t + 8], cst(K, "tri_incl", rows)[:, 0:rows], g, start=True, stop=True)
                    pe.matmul(K.ps[0:rows, 2, 8 * t:8 * t + 8], cst(K, "tri_after", rows)[:, 0:rows], g, start=True, stop=True)
                    for ck in range(2 if rows == P else 1):
                        mm = pe.matmul(K.ps[:, 3, 16 * t + 8 * ck:16 * t + 8 * ck + 8],
                                       cst(K, "chunk_ones", rows)[:, P * ck:P * ck + P], g, start=True, stop=True)
                mm.then_inc(s_cum, 1)

            @block.vector
            def _(dve):
                ch = K.dve_chain
                ch.link(dve, dve.memset(ab[:], 0.0))
                dve.memset(S.eg[:], 0.0)
                dve.memset(S.beg[:], 0.0)
                ch.link(dve, dve.memset(S.g_cum[:], 0.0))
                dve.wait_ge(s_tr, 1)
                dve.tensor_copy(ab[:, 0:4].rearrange("p a b -> p (a b)"), K.ps[:, 0, 0:64])
                ch.link(dve, dve.tensor_copy(ab[0:META, 4], K.ps[0:META, 0, 64:80]))
                dve.tensor_tensor(xa[:], ab[:, :, 0:8], bc(par(K, "dt_bias"), [P, 5, 8], 1), ALU.add).then_inc(s_x, 1)
                dve.wait_ge(s_ln, 1)
                ch.link(dve, dve.scalar_tensor_tensor(xa.rearrange("p a b -> p (a b)"), xa.rearrange("p a b -> p (a b)"), 0.0,
                                                      e1.rearrange("p a b -> p (a b)"), ALU.max, ALU.add))
                dve.scalar_tensor_tensor(S.g[:], xa[:], -1.0, bc(ea[:], [P, 5, 8], 1), ALU.mult, ALU.mult).then_inc(s_g, 1)
                dve.wait_ge(s_cum, 1)
                dve.tensor_copy(S.g_cum[:, 0:4].rearrange("p a b -> p (a b)"), K.ps[:, 1, 0:32])
                dve.tensor_copy(S.g_cum[0:META, 4], K.ps[0:META, 1, 32:40]).then_inc(s_x, 1)
                dve.wait_ge(s_e, 1)
                dve.tensor_tensor(S.beg[:], S.eg[:], S.beta[:], ALU.mult)

            @block.scalar
            def _(act):
                ch = K.act_chain
                act.wait_ge(s_x, 1)
                ch.link(act, act.activation(e1[:], xa[:], ACT.Abs))
                ch.link(act, act.activation(e1[:], e1[:], ACT.Exp, scale=-1.0))
                act.activation(e1[:], e1[:], ACT.Ln, bias=1.0)
                act.activation(ea[:], par(K, "a_log"), ACT.Exp).then_inc(s_ln, 1)
                act.activation(S.beta[:], ab[:, :, 8:16], ACT.Sigmoid)
                act.wait_ge(s_x, 2)
                act.activation(S.eg[:], S.g_cum[:], ACT.Exp)
                act.activation(S.ea[:, 0:4].rearrange("p a b -> p (a b)"), K.ps[:, 2, 0:32], ACT.Exp)
                act.activation(S.ea[0:META, 4], K.ps[0:META, 2, 32:40], ACT.Exp)
                act.activation(S.egl[:, 0:4].rearrange("p a b c -> p (a b c)"), K.ps[:, 3, 0:64], ACT.Exp)
                act.activation(S.egl[:, 4, 0], K.ps[:, 3, 64:72], ACT.Exp).then_inc(s_e, 1)


def delta_rule(K, S, grp):
    names = ("tile_done", "ug", "gb", "kk", "caps", "exps", "lower", "pooled", "a_t", "a_sb", "r1", "p2", "a2_sb", "x2_sb",
             "p4", "a4_sb", "x4_sb", "p8", "x8_sb", "r3", "p16", "r_sb", "k_t", "k_sb", "kt_sb", "k2", "k2_sb", "y_t", "y_sb",
             "w", "w_sb", "u", "u_sb", "nw", "vs", "vn", "ds", "state", "o", "o_sb")
    z = dict(zip(names, sems(K, *names)))
    tiles = [token_ranges()[-1]] + token_ranges()[:-1]
    H4 = range(HG)
    hd = slice(HG * grp, HG * grp + HG)
    with ExitStack() as c:
        def buf(name, n=P):
            return scratch(K, c, name, [P, HG, n])
        ug, dt, qd, lw, x1, a1, rr, x2, a2, x4, a4, at, kd, kb, nw = [buf(n) for n in (
            "ug", "decay_t", "q_dec", "lower", "x1", "a1", "r", "x2", "a2", "x4", "a4", "attn_t", "k_dec", "k_beta", "neg_w")]
        vb, uu = buf("v_beta", DN_V), buf("u", DN_V)
        st = S.state

        def bank(b, rows, n):
            return K.ps[0:rows, b, 0:HG * n].rearrange("p (h c) -> p h c", h=HG)

        def wide(b, p0, p1):
            return K.ps[p0:p1, b:b + 2, :].rearrange("p a (h c) -> p (a h) c", h=2)

        def tb(ap, rows, n):
            return bc(ap, [rows, HG, n], 2)

        with K.nc.Block() as block:
            @block.tensor
            def _(pe):
                for n, (t, r, a) in enumerate(tiles):
                    x = n - 1
                    s = slice(0, r)

                    def four(b, lhs, rhs, w=r, **kw):
                        for h in H4:
                            mm = pe.matmul(bank(b, w, r)[:, h], lhs(h), rhs(h), start=True, stop=True)
                        return mm
                    pe.wait_ge(z["ug"], n + 1)
                    pe.matmul(K.ps[:, 0, 0:HG * r], cst(K, "ones", r), ug[s, :, 0:r], start=True, stop=True).then_inc(z["gb"], 1)
                    q, k = (lambda h: S.qk[:, h, a:a + r]), (lambda h: S.qk[:, HG + h, a:a + r])
                    mm = four(1, k, k)
                    if x >= 0:
                        mm = four(2, k, q)
                    mm.then_inc(z["kk"], 1)
                    pe.wait_ge(z["lower"], n + 1)
                    for h in H4:
                        mm = pe.transpose(bank(3, r, r)[:, h], x1[s, h, 0:r], cst(K, "ident", r)[:, 0:r])
                    mm.then_inc(z["a_t"], 1)
                    A, X, A2, X2, A4, X4, R = [(lambda h, v=v: v[s, h, 0:r]) for v in (a1, x1, a2, x2, a4, x4, rr)]
                    pe.wait_ge(z["a_sb"], n + 1)
                    four(4, X, A)
                    four(5, A, X).then_inc(z["p2"], 1)
                    pe.wait_ge(z["a2_sb"], n + 1)
                    pe.wait_ge(z["x2_sb"], n + 1)
                    four(6, X2, A2)
                    four(7, A2, X2)
                    pe.wait_ge(z["r1"], n + 1)
                    four(3, X2, R).then_inc(z["p4"], 1)
                    pe.wait_ge(z["a4_sb"], n + 1)
                    pe.wait_ge(z["x4_sb"], n + 1)
                    four(4, A4, X4)
                    four(5, X4, R).then_inc(z["p8"], 1)
                    pe.wait_ge(z["x8_sb"], n + 1)
                    pe.wait_ge(z["r3"], n + 1)
                    four(6, A, R).then_inc(z["p16"], 1)
                    pe.wait_ge(z["r_sb"], n + 1)
                    W = R
                    if x >= 0:
                        N = lambda h: lw[s, h, 0:r]
                        four(7, R, N)
                        four(3, N, R)
                        for h in H4:
                            mm = pe.transpose(bank(4, r, r)[:, h], R(h), cst(K, "ident", r)[:, 0:r])
                        mm.then_inc(z["k_t"], 1)
                        pe.wait_ge(z["k_sb"], x + 1)
                        pe.wait_ge(z["kt_sb"], x + 1)
                        four(5, X2, A2).then_inc(z["k2"], 1)
                        pe.wait_ge(z["k2_sb"], x + 1)
                        four(6, A4, X4).then_inc(z["y_t"], 1)
                        pe.wait_ge(z["y_sb"], x + 1)
                        four(7, X, X4).then_inc(z["w"], 1)
                        pe.wait_ge(z["w_sb"], x + 1)
                        W = A
                    pe.wait_ge(z["pooled"], n + 1)
                    for h in H4:
                        mm = pe.matmul(wide(0, 0, r)[:, h], W(h), vb[s, h], start=True, stop=True)
                    if x >= 0:
                        mm = four(2, lambda h: kb[s, h], W, w=P)
                    mm.then_inc(z["u"], 1)
                    pe.wait_ge(z["u_sb"], n + 1)
                    if x < 0:
                        for h in H4:
                            mm = pe.matmul(wide(3, 0, P)[:, h], kd[s, h], uu[s, h], start=True, stop=True)
                        mm.then_inc(z["ds"], 1)
                        continue
                    pe.wait_ge(z["nw"], x + 1)
                    for ck in range(2):
                        m, r0 = 2 * x + ck, CH * ck
                        c0 = slice(r0, r0 + CH)
                        pe.wait_ge(z["state"], m + 1)
                        for h in H4:
                            mm = pe.matmul(wide(3, r0, r0 + CH)[:, h], nw[:, h, c0], st[:, h], start=True, stop=True)
                        mm.then_inc(z["vs"], 1)
                        if m >= 1:
                            pe.wait_ge(z["o_sb"], m)
                        for h in H4:
                            pe.matmul(wide(5, r0, r0 + CH)[:, h], qd[:, h, c0], st[:, h], start=h % 2 == 0, stop=False,
                                      skip_group_check=True)
                        pe.wait_ge(z["vn"], m + 1)
                        for h in H4:
                            b = (7, 7, 0, 0)[h]
                            mm = pe.matmul(K.ps[:, b, 256 * (h % 2):256 * (h % 2) + 256], kd[c0, h], uu[c0, h], start=True, stop=True)
                        mm.then_inc(z["ds"], 1)
                        for h in H4:
                            mm = pe.matmul(wide(5, r0, r0 + CH)[:, h], at[c0, h, c0], uu[c0, h], start=False, stop=True,
                                           skip_group_check=True)
                        mm.then_inc(z["o"], 1)

            @block.vector
            def _(dve):
                ch = K.dve_chain
                for n, (t, r, a) in enumerate(tiles):
                    x, s = n - 1, slice(0, r)
                    ident4 = bc(cst(K, "ident", r)[:, 0:r], [r, HG, r], 1)

                    def v4(b):
                        return b[s, :, 0:r]
                    if x >= 1:
                        dve.wait_ge(z["o"], 2 * x)
                    tri = bc(cst(K, "tri_incl", r)[:, 0:r], [r, HG, r], 1)
                    dve.tensor_tensor(v4(ug), tri, tb(S.g[s, t, hd], r, r), ALU.mult).then_inc(z["ug"], 1)
                    dve.wait_ge(z["gb"], n + 1)
                    ch.link(dve, dve.tensor_tensor(v4(ug), bank(0, r, r), tb(S.g_cum[s, t, hd], r, r), ALU.subtract))
                    cap = bc(cst(K, "cap_incl", r)[:, 0:r], [r, HG, r], 1)
                    ch.link(dve, dve.tensor_tensor(v4(dt), v4(ug), cap, ALU.min))
                    cap = bc(cst(K, "cap_strict", r)[:, 0:r], [r, HG, r], 1)
                    dve.scalar_tensor_tensor(v4(ug), v4(ug), -1.0, cap, ALU.mult, ALU.min).then_inc(z["caps"], 1)
                    dve.wait_ge(z["exps"], n + 1)
                    dve.wait_ge(z["kk"], n + 1)
                    for h in H4:
                        hh = HG * grp + h
                        last = dve.scalar_tensor_tensor(lw[s, h, 0:r], bank(1, r, r)[:, h], S.beta[s, t, hh:hh + 1], ug[s, h, 0:r],
                                                        ALU.mult, ALU.mult)
                    ch.link(dve, last)
                    same = bc(cst(K, "same16", r)[:, 0:r], [r, HG, r], 1)
                    dve.tensor_tensor(v4(x1), v4(lw), same, ALU.mult).then_inc(z["lower"], 1)
                    if x >= 0:
                        dve.wait_ge(z["lower"], n + 1)
                        dve.tensor_tensor(v4(lw), v4(lw), v4(x1), ALU.subtract)
                        dve.tensor_tensor(v4(at), bank(2, r, r), v4(dt), ALU.mult)
                    dve.wait_ge(z["a_sb"], n + 1)
                    dve.scalar_tensor_tensor(v4(rr), v4(a1), -1.0, ident4, ALU.mult, ALU.add).then_inc(z["r1"], 1)
                    dve.wait_ge(z["p2"], n + 1)
                    dve.tensor_copy(v4(x2), bank(5, r, r)).then_inc(z["x2_sb"], 1)
                    dve.wait_ge(z["p4"], n + 1)
                    dve.tensor_tensor(v4(rr), v4(rr), bank(3, r, r), ALU.add)
                    dve.tensor_copy(v4(x4), bank(7, r, r)).then_inc(z["x4_sb"], 1)
                    dve.wait_ge(z["p8"], n + 1)
                    dve.tensor_tensor(v4(rr), v4(rr), bank(5, r, r), ALU.add).then_inc(z["r3"], 1)
                    dve.wait_ge(z["p16"], n + 1)
                    dve.tensor_tensor(v4(rr), v4(rr), bank(6, r, r), ALU.add).then_inc(z["r_sb"], 1)
                    if x >= 0:
                        dve.wait_ge(z["k_t"], x + 1)
                        ch.link(dve, dve.tensor_copy(v4(x2), bank(3, r, r)))
                        dve.scalar_tensor_tensor(v4(x4), v4(x2), -1.0, ident4, ALU.mult, ALU.add).then_inc(z["kt_sb"], 1)
                        dve.wait_ge(z["y_t"], x + 1)
                        dve.tensor_tensor(v4(x4), v4(x4), bank(6, r, r), ALU.add).then_inc(z["y_sb"], 1)
                        dve.wait_ge(z["u"], n + 1)
                        dve.tensor_scalar(nw[:], bank(2, P, r), -1.0, None, ALU.mult).then_inc(z["nw"], 1)
                        for ck in range(2):
                            m, r0 = 2 * x + ck, CH * ck
                            c0 = slice(r0, r0 + CH)
                            dve.wait_ge(z["vs"], m + 1)
                            dve.wait_ge(z["u_sb"], n + 1)
                            dve.tensor_tensor(uu[c0], wide(3, r0, r0 + CH), uu[c0], ALU.add).then_inc(z["vn"], 1)
                            dve.wait_ge(z["ds"], m + 2)
                            for h in H4:
                                hh, b = HG * grp + h, (7, 7, 0, 0)[h]
                                last = dve.scalar_tensor_tensor(st[:, h], st[:, h], S.egl[:, t, ck, hh:hh + 1],
                                                                K.ps[:, b, 256 * (h % 2):256 * (h % 2) + 256], ALU.mult, ALU.add)
                            last.then_inc(z["state"], 1)
                            dve.wait_ge(z["state"], m + 2)
                    else:
                        dve.wait_ge(z["ds"], 1)
                        dve.tensor_copy(st[:], wide(3, 0, P)).then_inc(z["state"], 1)
                        dve.wait_ge(z["state"], 1)

            @block.scalar
            def _(act):
                for n, (t, r, a) in enumerate(tiles):
                    x, s = n - 1, slice(0, r)

                    def v4(b):
                        return b[s, :, 0:r]
                    act.wait_ge(z["caps"], n + 1)
                    act.activation(v4(dt), v4(dt), ACT.Exp)
                    act.activation(qd[:, :, 0:r], bank(0, P, r), ACT.Exp)
                    act.activation(v4(ug), v4(ug), ACT.Exp).then_inc(z["exps"], 1)
                    for sig, dst, b, done in (("a_t", a1, 3, "a_sb"), ("p2", a2, 4, "a2_sb"), ("p4", a4, 6, "a4_sb"),
                                              ("p8", a1, 4, "x8_sb")):
                        act.wait_ge(z[sig], n + 1)
                        act.activation(v4(dst), bank(b, r, r), ACT.Copy).then_inc(z[done], 1)
                    if x >= 0:
                        act.wait_ge(z["k_t"], x + 1)
                        act.activation(v4(a2), bank(7, r, r), ACT.Copy)
                        act.activation(v4(x1), bank(4, r, r), ACT.Copy).then_inc(z["k_sb"], 1)
                        act.wait_ge(z["k2"], x + 1)
                        act.activation(v4(a4), bank(5, r, r), ACT.Copy).then_inc(z["k2_sb"], 1)
                        act.wait_ge(z["w"], x + 1)
                        act.activation(v4(a1), bank(7, r, r), ACT.Copy).then_inc(z["w_sb"], 1)
                    act.wait_ge(z["u"], n + 1)
                    act.activation(uu[s], wide(0, 0, r), ACT.Copy).then_inc(z["u_sb"], 1)
                    if x >= 0:
                        for ck in range(2):
                            m, c0 = 2 * x + ck, slice(CH * ck, CH * ck + CH)
                            act.wait_ge(z["o"], m + 1)
                            act.activation(S.v[c0, t].rearrange("p (h c) -> p h c", h=HG), wide(5, CH * ck, CH * ck + CH),
                                           ACT.Copy).then_inc(z["o_sb"], 1)

            @block.gpsimd
            def _(pool):
                for n, (t, r, a) in enumerate(tiles):
                    x, s = n - 1, slice(0, r)
                    if x == 0:
                        pool.wait_ge(z["ds"], 1)
                    if x >= 1:
                        pool.wait_ge(z["o"], 2 * x)
                    k4 = S.k[s, t].rearrange("p (h c) -> p h c", h=HG)
                    v4_ = S.v[s, t].rearrange("p (h c) -> p h c", h=HG)
                    pool.tensor_tensor(kd[s], k4, tb(S.ea[s, t, hd], r, P), ALU.mult)
                    pool.tensor_tensor(kb[s], k4, tb(S.beg[s, t, hd], r, P), ALU.mult)
                    last = pool.tensor_tensor(vb[s], v4_, tb(S.beta[s, t, hd], r, DN_V), ALU.mult)
                    if x >= 0:
                        pool.wait_ge(z["exps"], n + 1)
                        last = pool.tensor_tensor(qd[:], qd[:], S.qk[:, 0:HG, a:a + r], ALU.mult)
                    last.then_inc(z["pooled"], 1)


def delta_output(K, S, o_hi, o_lo):
    s_ss, s_rt, s_on, s_tr, s_hi, s_lo = sems(K, "sums", "roots", "gated", "transposed", "hi", "lo")
    o = S.v
    with ExitStack() as c:
        sq = scratch(K, c, "sq", [P, TT, 1024])
        ss = scratch(K, c, "ss", [P, 32])
        with K.nc.Block() as block:
            @block.vector
            def _(dve):
                ch = K.dve_chain
                o16 = o[:, 0:TT].rearrange("p t (h c) -> p (t h) c", c=DN_V)
                ch.link(dve, dve.tensor_tensor(sq[:], o[:, 0:TT], o[:, 0:TT], ALU.mult))
                ch.link(dve, dve.tensor_reduce(ss[:, 0:16], sq.rearrange("p t (h c) -> p (t h) c", c=DN_V), AX.X, ALU.add))
                dve.tensor_scalar(ss[:, 0:16], ss[:, 0:16], 1.0 / DN_V, EPS, ALU.mult, ALU.add).then_inc(s_ss, 1)
                dve.wait_ge(s_rt, 1)
                ch.link(dve, dve.reciprocal(ss[:, 16:32], ss[:, 16:32]))
                ch.link(dve, dve.tensor_tensor(o16, o16, bc(ss[:, 16:32], [P, 16, DN_V], 2), ALU.mult))
                ch.link(dve, dve.tensor_tensor(o16, o16, bc(par(K, "dn_gain"), [P, 16, DN_V], 1), ALU.mult))
                for t in range(TT):
                    ot = o[:, t].rearrange("p (g c) -> p g c", g=2)
                    dve.tensor_tensor(ot, ot, S.dz.rearrange("p (g t c) -> p g t c", g=2, t=TT)[:, :, t], ALU.mult).then_inc(s_on, 1)
                for f in range(8):
                    dve.wait_ge(s_hi, f + 1)
                    dve.tensor_tensor(o_lo[:, f], K.ps[:, f], o_hi[:, f].bitcast(F32), ALU.subtract)

            @block.scalar
            def _(act):
                act.wait_ge(s_ss, 1)
                act.activation(ss[:, 16:32], ss[:, 0:16], ACT.Sqrt).then_inc(s_rt, 1)
                for f in range(8):
                    act.wait_ge(s_tr, f + 1)
                    act.activation(o_hi[:, f], K.ps[:, f], ACT.Copy).then_inc(s_hi, 1)

            @block.tensor
            def _(pe):
                for f in range(8):
                    for t in range(TT):
                        if f == 0:
                            pe.wait_ge(s_on, t + 1)
                        tr = pe.transpose(K.ps[:, f, t * P:(t + 1) * P], o[:, t, f * P:(f + 1) * P], cst(K, "ident"))
                    tr.then_inc(s_tr, 1)



def merge_pairs(K, o_hi, o_lo, pre, out_hi=None, out_lo=None):
    with ExitStack() as c:
        g = scratch(K, c, "gate", [P, 2, SEQ])
        y = scratch(K, c, "y", [P, 2, SEQ])

        def evac_act(act, ch, u, turn, b, s_free):
            s_sig, s_sum, s_hi = evac["signals"]
            kind, pb, pair = u % 2, u // 2 % 2, turn * 2 + u // 2
            if kind == 0:
                act.activation(g[:, pb], K.ps[:, b, :], ACT.Sigmoid).then_inc(s_sig, 1)
            elif out_hi is not None:
                act.wait_ge(s_sum, pair + 1)
                act.activation(out_hi[:, ds(pair, 1), :], y[:, pb].unsqueeze(1), ACT.Copy).then_inc(s_hi, 1)

        def evac_dve(dve, ch, u, turn, b, s_free):
            s_sig, s_sum, s_hi = evac["signals"]
            kind, pb, pair = u % 2, u // 2 % 2, turn * 2 + u // 2
            yy, p1 = y[:, pb].unsqueeze(1), pre[:, ds(pair, 1), :]
            if kind == 0:
                dve.wait_ge(s_sig, pair + 1)
                dve.nop().then_inc(s_free, 1)
                return
            ps = K.ps[:, b:b + 1, :]
            if out_hi is None:
                dve.tensor_tensor(yy, ps, p1, ALU.add).then_inc(s_free, 1)
                dve.wait_ge(s_free, ch + 3)
                dve.tensor_tensor(p1, yy, g[:, pb].unsqueeze(1), ALU.mult).then_inc(s_sum, 1)
            else:
                dve.tensor_tensor(yy, ps, g[:, pb].unsqueeze(1), ALU.mult).then_inc(s_free, 1)
                dve.wait_ge(s_free, ch + 3)
                dve.tensor_tensor(yy, yy, p1, ALU.add).then_inc(s_sum, 1)
                dve.wait_ge(s_hi, pair + 1)
                dve.tensor_tensor(out_lo[:, ds(pair, 1), :], yy, out_hi[:, ds(pair, 1), :].bitcast(F32), ALU.subtract)
        evac = {"frees": "dve", "act": evac_act, "dve": evac_dve, "sems": ("sigmoid", "summed", "hi")}
        product_cols(K, K.at, 16, None, None, [(K.nx_hi, K.nx_lo, [(META, T2)]), (o_hi, o_lo, [(0, SEQ)])], evac)
    K.at += 16



def stick_breaking(K, qT, kT, v):
    s_z, s_ln, s_sp, s_r, s_c, s_w, s_pv, s_o = sems(
        K, "z", "ln", "softplus", "later", "log_w", "w", "pv", "o")
    units = [(h, a) for h in range(SB_H) for a in (3, 2, 1, 0, 4)]
    NU = len(units)

    def geo(u):
        h, a = units[u]
        return (h, a, P, a * P, META + a * P, SEQ - a * P) if a < TT else (h, a, META, 0, 0, SEQ)
    with ExitStack() as c:
        az, sp, w = [scratch(K, c, n, [P, 3, SEQ]) for n in ("abs_z", "softplus", "w")]
        rs = scratch(K, c, "later_sum", [P, 2, SEQ])
        with K.nc.Block() as block:
            @block.tensor
            def _(pe):
                def z_product(u):
                    h, a, r, q0, k0, n = geo(u)
                    if u >= 6:
                        pe.wait_ge(s_w, u - 5)
                    out = K.ps[0:r, u % 6, 0:n]
                    if a == 3 and h >= 1:
                        pass
                    mm = pe.matmul(out, kT[:, h, k0:k0 + r], qT[:, h, META + q0:T2], start=True, stop=a == TT, skip_group_check=True)
                    if a < TT:
                        mm = pe.matmul(out[:, 0:P], cst(K, "ident"), cst(K, "sb_mask"), start=False, stop=True, skip_group_check=True)
                    mm.then_inc(s_z, 1)

                def later_sums(u):
                    h, a, r, q0, k0, n = geo(u)
                    pe.wait_ge(s_sp, u + 1)
                    mm = pe.matmul(K.ps[0:r, u % 6, 0:n], cst(K, "neg_from", r)[:, 0:r], sp[0:r, u % 3, 0:n],
                                   start=False, stop=a == 3, skip_group_check=True)
                    if a != 3:
                        pe.wait_ge(s_r, u - u // 5)
                        off = P if a < TT else 0
                        mm = pe.matmul(K.ps[0:r, u % 6, off:n], cst(K, "neg_ones")[:, 0:r], rs[:, u % 5 % 2, q0 + off:SEQ],
                                       start=False, stop=True, skip_group_check=True)
                    mm.then_inc(s_c, 1)

                def values(u):
                    h, a, r, q0, k0, n = geo(u)
                    pe.wait_ge(s_w, u + 1)
                    if a == 3 and h >= 2:
                        pe.wait_ge(s_o, h - 1)
                    pe.matmul(K.ps[:, 6 + h % 2, q0:SEQ], v[0:r, a, h * P:(h + 1) * P], w[0:r, u % 3, 0:n], start=a == 3,
                              stop=a == TT, skip_group_check=True).then_inc(s_pv, 1)
                for u in range(3):
                    z_product(u)
                for u in range(NU):
                    if u + 3 < NU:
                        z_product(u + 3)
                    later_sums(u)
                    if u >= 1:
                        values(u - 1)
                values(NU - 1)

            @block.vector
            def _(dve):
                def softplus(u):
                    h, a, r, q0, k0, n = geo(u)
                    dve.wait_ge(s_ln, u + 1)
                    if u >= 3:
                        dve.wait_ge(s_c, u - 2)
                        k = u - 3
                        dve.wait_ge(s_r, (k // 5) * 4 + min(k % 5, 3) + 1)
                    dve.scalar_tensor_tensor(sp[0:r, u % 3, 0:n], K.ps[0:r, u % 6, 0:n], 0.0, az[0:r, u % 3, 0:n],
                                             ALU.max, ALU.add).then_inc(s_sp, 1)
                for u in range(NU):
                    softplus(u)

            @block.scalar
            def _(act):
                def logs(u):
                    h, a, r, q0, k0, n = geo(u)
                    act.wait_ge(s_z, u + 1)
                    if u >= 3:
                        act.wait_ge(s_sp, u - 2)
                    b = az[0:r, u % 3, 0:n]
                    K.act_chain.link(act, act.activation(b, K.ps[0:r, u % 6, 0:n], ACT.Abs))
                    K.act_chain.link(act, act.activation(b, b, ACT.Exp, scale=-1.0))
                    act.activation(b, b, ACT.Ln, bias=1.0).then_inc(s_ln, 1)

                def weights(u):
                    h, a, r, q0, k0, n = geo(u)
                    act.wait_ge(s_c, u + 1)
                    if u >= 3:
                        act.wait_ge(s_pv, u - 2)
                    act.activation(w[0:r, u % 3, 0:n], K.ps[0:r, u % 6, 0:n], ACT.Exp).then_inc(s_w, 1)

                def copy_out(h):
                    act.wait_ge(s_pv, 5 * h + 5)
                    act.activation(qT[:, h, 0:SEQ], K.ps[:, 6 + h % 2, :], ACT.Copy).then_inc(s_o, 1)
                logs(0)
                for u in range(NU):
                    if u + 1 < NU:
                        logs(u + 1)
                    weights(u)
                    if u >= 6 and u % 5 == 1:
                        copy_out(u // 5 - 1)
                copy_out(SB_H - 1)

            @block.gpsimd
            def _(pool):
                for u in range(NU):
                    h, a, r, q0, k0, n = geo(u)
                    if a == TT:
                        continue
                    i = u % 5
                    pool.wait_ge(s_sp, u + 1)
                    if u >= 1:
                        pool.wait_ge(s_c, u if i else u)
                    last = pool.tensor_copy(rs[:, (i + 1) % 2, q0:q0 + P], sp[:, u % 3, 0:P])
                    if a < 3:
                        last = pool.tensor_tensor(rs[:, (i + 1) % 2, q0 + P:SEQ], rs[:, i % 2, q0 + P:SEQ], sp[:, u % 3, P:n], ALU.add)
                    last.then_inc(s_r, 1)
                    pool.wait_ge(s_r, u - u // 5 + 1)


def split_stage(K, src, hi, lo, n):
    s_hi, = sems(K, "hi")
    with K.nc.Block() as block:
        @block.scalar
        def _(act):
            for i in range(n):
                act.activation(hi[:, i], src[:, i, 0:SEQ], ACT.Copy).then_inc(s_hi, 1)

        @block.vector
        def _(dve):
            for i in range(n):
                dve.wait_ge(s_hi, i + 1)
                dve.tensor_tensor(lo[:, i], src[:, i, 0:SEQ], hi[:, i].bitcast(F32), ALU.subtract)


def block2(K, v):
    norm_stage(K, v["mix_gain"], v["meta"])
    with ExitStack() as c:
        pre = scratch(K, c, "merged", [P, 8, SEQ])
        with ExitStack() as c2:
            S = Core()
            S.g, S.g_cum, S.eg, S.beg, S.ea, S.beta = [
                scratch(K, c2, n, [P, 5, 8]) for n in ("g", "g_cum", "exp_g", "beta_exp_g", "exp_after", "beta")]
            S.egl = scratch(K, c2, "egl", [P, 5, 2, 8])
            delta_gates(K, S)
            taps = par(K, "conv2").rearrange("p (g f t) -> p g f t", g=2, t=4)
            for grp in range(2):
                with ExitStack() as c3:
                    S.v = scratch(K, c3, "v_rows", [P, 5, 1024])
                    with ExitStack() as c4:
                        S.k = scratch(K, c4, "k_rows", [P, 5, 512])
                        S.qk = scratch(K, c4, "qk_cols", [P, 8, T2])
                        S.state = scratch(K, c4, "state", [P, HG, DN_V])
                        project_conv(K, S.qk, taps[:, grp, 0:8])
                        with ExitStack() as c5:
                            vT = scratch(K, c5, "v_cols", [P, 8, T2])
                            project_conv(K, vT, taps[:, grp, 8:16])
                            norm_cols(K, [(S.qk[:, i], 128.0, 128.0 * EPS, None) for i in range(4)]
                                      + [(S.qk[:, i], 1.0, EPS, None) for i in range(4, 8)])
                            units = []
                            for t, r, a in token_ranges():
                                for f in range(2):
                                    units.append((S.v[0:r, t, 512 * f:512 * f + 512], [vT[:, 4 * f + j, a:a + r] for j in range(4)]))
                                units.append((S.k[0:r, t, :], [S.qk[:, 4 + j, a:a + r] for j in range(4)]))
                            transpose_units(K, units)
                        delta_rule(K, S, grp)
                    with ExitStack() as c4:
                        o_hi, o_lo = [scratch(K, c4, n, [P, 8, SEQ], F32R) for n in ("o_hi", "o_lo")]
                        with ExitStack() as c5:
                            S.dz = scratch(K, c5, "dz", [P, 2 * 2048])
                            product_rows512(K, K.at, 2, K.nx_hi, K.nx_lo, META, lambda act, ch, u, banks: act.activation(
                                S.dz[:, ds(ch * 512 - 3 * 512, 2048)], banks.rearrange("p a b -> p (a b)"), ACT.Silu))
                            K.at += 8
                            delta_output(K, S, o_hi, o_lo)
                        if grp == 0:
                            product_cols(K, K.at, 8, None, None, [(o_hi, o_lo, [(0, SEQ)])], {
                                "frees": "act",
                                "act": lambda act, ch, u, turn, b, s_free: act.activation(
                                    pre[:, ds(ch, 1), :], K.ps[:, b:b + 1, :], ACT.Copy).then_inc(s_free, 1)})
                            K.at += 8
                        else:
                            merge_pairs(K, o_hi, o_lo, pre)
        with ExitStack() as c2:
            qT = scratch(K, c2, "sb_q", [P, SB_H, T2])
            with ExitStack() as c3:
                kT = scratch(K, c3, "sb_k", [P, SB_H, T2])
                v_rows = scratch(K, c3, "sb_v", [P, 5, 1024])
                project_plain(K, 8, qT)
                project_plain(K, 8, kT)
                with ExitStack() as c4:
                    vT = scratch(K, c4, "sb_vT", [P, SB_H, T2])
                    project_plain(K, 8, vT)
                    transpose_units(K, [(v_rows[0:r, t, 512 * f:512 * f + 512], [vT[:, 4 * f + j, a:a + r] for j in range(4)])
                                        for t, r, a in token_ranges() for f in range(2)])
                norm_cols(K, [(qT[:, i], 1.0, 128.0 * EPS, par(K, "sbq_gain")) for i in range(8)]
                          + [(kT[:, i], 1.0 / 128, EPS, par(K, "sbk_gain")) for i in range(8)])
                stick_breaking(K, qT, kT, v_rows)
            o_hi, o_lo = [scratch(K, c2, n, [P, 8, SEQ], F32R) for n in ("o_hi", "o_lo")]
            split_stage(K, qT, o_hi, o_lo, 8)
            with ExitStack() as c3:
                m_hi, m_lo = [scratch(K, c3, n, [P, 8, SEQ], F32R) for n in ("m_hi", "m_lo")]
                merge_pairs(K, o_hi, o_lo, pre, m_hi, m_lo)
                product_rows(K, K.at, KT, m_hi, m_lo, None)
                K.at += KT
    norm_stage(K, v["ffn_gain_2"], None)
    with ExitStack() as c:
        act_hi, act_lo = scratch(K, c, "act_hi", [P, FT, SEQ], F32R), scratch(K, c, "act_lo", [P, FT, SEQ], F32R)
        ffn_up(K, act_hi, act_lo, False, 0)

        def finish(sp, s_added):
            out = v["out"].rearrange("b (t p) d -> p (b t) d", p=P)
            for t in range(TT):
                sp.wait_ge(s_added, t + 1)
                sp.dma_start(out[:, t], K.h[:, t]).then_inc(K.s_out, 16)
            sp.wait_ge(K.s_out, 16 * TT)
        product_rows(K, K.at, FT, act_hi, act_lo, finish)
        K.at += FT



def core_setup(nc, ctx, v, n_stream):
    K = Core()
    K.live, K.cleared, K.uid = [], [], 0
    K.nc, K.stage, K.at, K.stream, K.n_stream = nc, 0, 0, v["stream"], n_stream

    def sb(name, shape, dt=F32):
        return ctx.enter_context(nc.sbuf_tensor(name, shape, dt))

    K.ps = ctx.enter_context(nc.psum_tensor("ps", [P, 8, 512], F32))
    K.raw = sb("raw", [P, RAW, 1024])
    K.whi, K.wlo = sb("whi", [P, HL, 1024], F32R), sb("wlo", [P, HL, 1024], F32R)
    K.h = sb("h_sb", [P, TT, D])
    K.const, K.param = sb("const_sb", [P, v["const"].shape[1]]), sb("param_sb", [P, PARAM_N])
    K.nx_hi, K.nx_lo = sb("nx_hi", [P, KT, T2], F32R), sb("nx_lo", [P, KT, T2], F32R)
    K.s_out = ctx.enter_context(nc.semaphore("out_written"))
    K.t_ss, K.t_rs = sb("t_ss", [P, 8]), sb("t_rs", [P, 8])
    K.s_raw = [ctx.enter_context(nc.semaphore(f"raw_in_{i}")) for i in range(RAW)]
    K.s_hi, K.s_lo, K.s_used = [ctx.enter_context(nc.semaphore(n)) for n in ("hi_made", "lo_made", "chunk_used")]
    K.act_chain = Chain(ctx.enter_context(nc.semaphore("act_step")))
    K.dve_chain = Chain(ctx.enter_context(nc.semaphore("dve_step")))
    K.pool_chain = Chain(ctx.enter_context(nc.semaphore("pool_step")))
    return K


def scratch(K, ctx, name, shape, dt=F32):
    K.uid += 1
    return ctx.enter_context(K.nc.sbuf_tensor(f"{name}_{K.uid}", shape, dt))


def norm_stage(K, gain, meta):
    with ExitStack() as c:
        K.t_xn = scratch(K, c, "xn", [P, TT + 1, D])
        K.t_gain = scratch(K, c, "gain", [P, D])
        if meta is not None:
            K.hm = scratch(K, c, "h_meta", [META, D])
        norm_rows(K, gain, meta)


def program(nc, v):
    with ExitStack() as ctx:
        K = core_setup(nc, ctx, v, N_STREAM1 + N_STREAM2)
        start(K, v)
        block1(K, v)
        block2(K, v)



def kernel(**inputs):
    import concourse.bacc as bacc
    from concourse.bass_utils import run_bass_kernel_spmd

    v = {n: np.asarray(a) for n, a in inputs.items()}

    def rows(a):
        return np.ascontiguousarray(np.broadcast_to(a.reshape(1, -1), (P, a.size)))

    arrays = dict(
        x=v["x"], meta=v["meta_tokens_2"], stream=np.concatenate(stream1(v) + stream2(v)),
        const=const_array(), param=param_array(v),
        attn_gain=rows(v["attn_norm"][0]), ffn_gain=rows(v["ffn_norm"][0]),
        mix_gain=rows(v["norm_mix_gain_2"][0]), ffn_gain_2=rows(v["norm_ffn_gain_2"][0]),
        cmp_w1_k=v["cmp_w1_k"][0], cmp_w1_v=v["cmp_w1_v"][0],
    )
    arrays = {f"{n}_dram": np.ascontiguousarray(a) for n, a in arrays.items()}
    nc = bacc.Bacc("TRN2", target_bir_lowering=False, num_devices=1)
    args = {n.removesuffix("_dram"): nc.dram_tensor(n, a.shape, mybir.dt.from_np(a.dtype), kind="ExternalInput").ap()
            for n, a in arrays.items()}
    args["out"] = nc.dram_tensor("out_dram", (1, SEQ, D), F32, kind="ExternalOutput").ap()
    program(nc, args)
    result = run_bass_kernel_spmd(nc, [arrays], core_ids=[0])
    return result.results[0]["out_dram"]
```

```python
from contextlib import ExitStack

import numpy as np

import concourse.bass as bass
from concourse import mybir

F32 = mybir.dt.float32
F32R = mybir.dt.float32r
ACT = mybir.ActivationFunctionType
ALU = mybir.AluOpType
AX = mybir.AxisListType
ds = bass.ds

P = 128
SEQ = 512
D = 1024
KT = D // P
TT = SEQ // P
META = 16
T2 = SEQ + META
HALF = T2 // 2
EPS = 1e-6
NEG = -1e30
D_FF = 2816
FT = D_FF // P

NSA_H, NSA_G, NSA_D = 8, 2, 64
N_CMP = 31
CMP_J = 16
GLA_H = 4
CH = 64

DN_H, DN_V = 8, 256
HG = 4
SB_H = 8

RAW = 4
HL = 2


CONST_COLS = {}


def const_array():
    r = np.arange(P)
    row, col = r[:, None], r[None, :]
    same = (row // CH) == (col // CH)
    parts = {}
    parts["ident"] = np.eye(P)
    parts["tri_incl"] = (same & (row <= col)) * 1.0
    parts["tri_after"] = (same & (row > col)) * 1.0
    parts["chunk_ones"] = np.concatenate([(row < CH) * np.ones((1, P)), (row >= CH) * np.ones((1, P))], 1)
    parts["cap_incl"] = np.where(same & (row <= col), 0.0, NEG)
    parts["cap_strict"] = np.where(same & (col < row), 0.0, NEG)
    parts["same16"] = ((row // 16) == (col // 16)) * 1.0
    parts["sb_mask"] = np.where(row < col, 0.0, NEG)
    parts["neg_from"] = -((row >= col) * 1.0)
    parts["neg_ones"] = -np.ones((P, P))
    parts["ones"] = np.ones((P, P))
    parts["pick"] = (np.arange(31)[None, :] == 15) * np.ones((P, 1))
    parts["dn_scales"] = np.where(row < 4, 128.0 ** -0.5, 1.0)
    parts["sb_scales"] = np.where(row < 8, 1.0, 128.0 ** 0.5)
    CONST_COLS["of block 1"] = (sum(a.shape[1] for a in parts.values()), 0)
    parts["causal"] = np.where(col <= row, 0.0, NEG)
    half = 8
    inv = (np.float32(500000.0) ** (-np.arange(half, dtype=np.float32) / np.float32(half))).astype(np.float32)
    pos = np.arange(SEQ, dtype=np.float32).reshape(TT, P)
    ang = (pos[:, :, None] * inv).astype(np.float32)
    parts["cos"] = np.cos(ang).transpose(1, 0, 2).reshape(P, TT * half)
    parts["sin"] = np.sin(ang).transpose(1, 0, 2).reshape(P, TT * half)
    end = np.zeros(32, np.float32)
    end[:N_CMP] = np.arange(N_CMP) * 16 + 31
    angc = (np.tile(end, 4)[:, None] * inv).astype(np.float32)
    parts["cos_cmp"], parts["sin_cmp"] = np.cos(angc), np.sin(angc)
    t = np.arange(SEQ).reshape(TT, P)
    keep = np.zeros((P, TT, NSA_G, NSA_G, 32))
    for g in range(NSA_G):
        for n in range(N_CMP):
            keep[:, :, g, g, n] = (n * 16 + 31 <= t).T
    parts["cmp_keep"] = keep.reshape(P, -1)
    parts["cmp_bias"] = np.where(keep > 0, 0.0, NEG).reshape(P, -1)
    at, out = 0, []
    for name, a in parts.items():
        CONST_COLS[name] = (at, a.shape[1])
        at += a.shape[1]
        out.append(a.astype(np.float32))
    return np.ascontiguousarray(np.concatenate(out, 1))


const_array()


PARAM_COLS = {}
PARAM_SHAPES = [
    ("q_gain", 64), ("k_gain0", 64), ("k_gain1", 64), ("k_gain2", 64), ("b_gate", 256),
    ("gla_gain", 128), ("pe_k", CMP_J), ("pe_v", CMP_J),
    ("conv1_w", 44 * 3), ("conv1_b", 44),
    ("conv2", 2 * 16 * 4),
    ("a_log", 8), ("dt_bias", 8), ("dn_gain", 2), ("sbq_gain", 1), ("sbk_gain", 1),
    ("cmp_w2_k", 128), ("cmp_w2_v", 128), ("w_gate2", 256),
]
_at = 0
for _n, _w in PARAM_SHAPES:
    PARAM_COLS[_n] = (_at, _w)
    _at += _w
PARAM_N = _at


def param_array(v):
    def rows(a):
        return np.broadcast_to(a.reshape(1, -1), (P, a.size))

    def tiles(a):
        taps, n = a.shape
        return a.reshape(taps, n // P, P).transpose(2, 1, 0).reshape(P, -1)

    def pairs(pe):
        return pe.reshape(CMP_J, P).T

    def ktiles(w):
        return w.reshape(2, P, -1).transpose(1, 0, 2).reshape(P, -1)

    wg = np.zeros((P, 256), np.float32)
    wg[:16] = v["gla_w_gate2"][0]
    c1 = v["conv_w"][0]
    parts = dict(
        q_gain=rows(v["nsa_q_norm"][0]), k_gain0=rows(v["nsa_k_norm"][0, 0]), k_gain1=rows(v["nsa_k_norm"][0, 1]),
        k_gain2=rows(v["nsa_k_norm"][0, 2]), b_gate=rows(v["gla_b_gate"][0]), gla_gain=rows(v["gla_out_norm"][0]),
        pe_k=pairs(v["cmp_pos_k"][0]), pe_v=pairs(v["cmp_pos_v"][0]),
        conv1_w=tiles(c1), conv1_b=v["conv_b"][0].reshape(44, P).T,
        conv2=np.concatenate([tiles(a) for g in range(2) for a in (
            v["conv_q_2"][0][:, 512 * g:512 * g + 512], v["conv_k_2"][0][:, 512 * g:512 * g + 512],
            v["conv_v_2"][0][:, 1024 * g:1024 * g + 1024])], 1),
        a_log=rows(v["dn_a_log_2"][0]), dt_bias=rows(v["dn_dt_bias_2"][0]), dn_gain=v["dn_out_norm_gain_2"][0].reshape(2, P).T,
        sbq_gain=v["sb_q_norm_gain_2"][0].reshape(P, 1), sbk_gain=v["sb_k_norm_gain_2"][0].reshape(P, 1),
        cmp_w2_k=ktiles(v["cmp_w2_k"][0]), cmp_w2_v=ktiles(v["cmp_w2_v"][0]), w_gate2=wg,
    )
    return np.ascontiguousarray(np.concatenate([parts[n] for n, _ in PARAM_SHAPES], 1))



def chunks_cols(w, c0, n, rows=slice(0, D)):
    a = w[rows, c0:c0 + n * P].reshape(KT, P, n, P)
    return a.transpose(2, 1, 0, 3).reshape(n, P, 1024)


def chunks_rows512(w, c0, groups=1):
    a = w[:, c0:c0 + groups * 512].reshape(4, 2, P, groups, 512)
    return a.transpose(3, 0, 2, 1, 4).reshape(groups * 4, P, 1024)


def chunks_rows(w):
    return w.reshape(-1, P, 1024)


def interleave(a, b):
    return np.stack([a, b], 1).reshape(-1, P, 1024)


def stream1(v):
    w, up = v["w_in"][0], v["w_up"][0]
    return [
        chunks_rows512(w, 0), chunks_rows512(w, 768), chunks_rows512(w, 1816), chunks_rows512(w, 2344),
        chunks_cols(w, 512, 2), chunks_cols(w, 1280, 1), chunks_cols(w, 1304, 4), chunks_cols(w, 2328, 1),
        chunks_rows(v["w_out"][0]),
        interleave(chunks_cols(up, 0, FT), chunks_cols(up, D_FF, FT)),
        chunks_rows(v["w_down"][0]),
    ]


def stream2(v):
    w, up = v["w_in_2"][0], v["w_ffn_in_2"][0]
    bdn, bsb = v["w_branch_dn_2"][0], v["w_branch_sb_2"][0]
    out = [chunks_cols(w, 6144, 1)]
    for g in range(2):
        out += [chunks_cols(w, 512 * g, 4), chunks_cols(w, 1024 + 512 * g, 4), chunks_cols(w, 2048 + 1024 * g, 8),
                chunks_cols(w, 4096 + 1024 * g, 8)]
        branch = chunks_cols(bdn, 0, 8, rows=slice(1024 * g, 1024 * g + 1024))
        out.append(branch if g == 0 else interleave(chunks_cols(w, 9232, 8), branch))
    out += [chunks_cols(w, 6160, 8), chunks_cols(w, 7184, 8), chunks_cols(w, 8208, 8),
            interleave(chunks_cols(w, 10256, 8), chunks_cols(bsb, 0, 8)),
            chunks_rows(v["w_out_2"][0]),
            interleave(chunks_cols(up, 0, FT), chunks_cols(up, D_FF, FT)),
            chunks_rows(v["w_ffn_out_2"][0])]
    return out


N_STREAM1 = 24 + 8 + 44 + 22
N_STREAM2 = 1 + 2 * (16 + 8) + 8 + 16 + 24 + 16 + 8 + 44 + 22



class Core:
    pass


class Chain:

    def __init__(self, sem):
        self.sem, self.count, self.turn, self.k = sem, 0, None, 0

    def loop(self, i, per):
        self.turn, self.per, self.k = i, per, 0

    def end(self, turns):
        assert self.k == self.per, (self.k, self.per)
        self.count += self.per * turns
        self.turn = None

    def link(self, eng, ins):
        ins.then_inc(self.sem, 1)
        if self.turn is None:
            self.count += 1
            eng.wait_ge(self.sem, self.count)
        else:
            self.k += 1
            eng.wait_ge(self.sem, self.turn * self.per + (self.count + self.k))


def over_chunks(eng, first, n, step, unroll=4, chain=None, links=0):
    turns = n // unroll
    if turns:
        with eng.Fori(0, turns) as i:
            if chain is not None:
                chain.loop(i, links * unroll)
            for u in range(unroll):
                step(i * unroll + u, first + u, i * (unroll // RAW))
            if chain is not None:
                chain.end(turns)
    for c in range(turns * unroll, n):
        step(c, first + c, 0)


def load_chunks(K, sp, first, n):
    n = min(n, K.n_stream - RAW - first)
    if n <= 0:
        return

    def step(c, s, turn):
        sp.wait_ge(K.s_lo, c + (first + 1))
        sp.dma_start(K.raw[:, s % RAW], K.stream[ds(c + (first + RAW), 1)][0]
                     ).then_inc(K.s_raw[s % RAW], 16)
    over_chunks(sp, first, n, step)


def split_hi(K, act, c, s, turn, first):
    act.wait_ge(K.s_used, c + (first + 1))
    n = s + HL
    act.wait_ge(K.s_raw[n % RAW], turn * 16 + 16 * (n // RAW + 1))
    act.activation(K.whi[:, n % HL], K.raw[:, n % RAW], ACT.Copy).then_inc(K.s_hi, 1)


def split_lo(K, dve, c, s, turn, first):
    n = s + HL
    dve.wait_ge(K.s_hi, c + (first + HL + 1))
    dve.tensor_tensor(K.wlo[:, n % HL], K.raw[:, n % RAW], K.whi[:, n % HL].bitcast(F32),
                      ALU.subtract).then_inc(K.s_lo, 1)


def guarded(K, first, step):
    def run(eng, c, s, turn):
        if isinstance(c, int) and first + c + HL >= K.n_stream:
            return
        step(K, eng, c, s, turn, first)
    return run


def three(pe, out, whi, wlo, xhi, xlo, start, stop, skip=False):
    pe.matmul(out, whi, xhi, start=start, stop=False, skip_group_check=skip)
    pe.matmul(out, whi, xlo, start=False, stop=False, skip_group_check=skip)
    return pe.matmul(out, wlo, xhi, start=False, stop=stop, skip_group_check=skip)


def sems(K, *names):
    for s in K.cleared:
        K.nc.release_semaphore(s)
    for s in K.live:
        K.nc.gpsimd.sem_clear(s)
    K.cleared = K.live
    K.stage += 1
    K.live = [K.nc.alloc_semaphore(f"{n}_{K.stage}") for n in names]
    return K.live


def cst(K, name, rows=P):
    a, n = CONST_COLS[name]
    a1 = CONST_COLS["of block 1"][0]
    return K.const1[0:rows, a - a1:a - a1 + n] if a >= a1 else K.const[0:rows, a:a + n]


def par(K, name, rows=P):
    a, n = PARAM_COLS[name]
    return K.param[0:rows, a:a + n]


def bc(ap, shape, axis):
    return ap.unsqueeze(axis).to_broadcast(shape)



def product_cols(K, first, n, x_hi, x_lo, ranges, evac, unroll=4, act_links=0, dve_links=0):
    s_free, *more = sems(K, "banks_free", *evac.get("sems", ()))
    evac["signals"] = more

    with K.nc.Block() as block:
        @block.sync
        def _(sp):
            load_chunks(K, sp, first, n)

        @block.tensor
        def _(pe):
            def step(c, s, turn):
                u = s - first
                xh, xl, rng = ranges[u % len(ranges)]
                pe.wait_ge(K.s_lo, c + (first + 1))
                pe.wait_ge(s_free, c + 1)
                for h, (a, e) in enumerate(rng):
                    for k in range(KT):
                        mm = three(pe, K.ps[:, 2 * (u % 2) + h, 0:e - a],
                                   K.whi[:, s % HL, k * P:(k + 1) * P], K.wlo[:, s % HL, k * P:(k + 1) * P],
                                   xh[:, k, a:e], xl[:, k, a:e], k == 0, k == KT - 1)
                mm.then_inc(K.s_used, 1)
            over_chunks(pe, first, n, step, unroll)

        @block.scalar
        def _(act):
            if "table" in evac:
                act.preload_act_table(evac["table"])
            if evac["frees"] == "act":
                act.nop().then_inc(s_free, 2)

            def step(c, s, turn):
                guarded(K, first, split_hi)(act, c, s, turn)
                if "act" in evac:
                    act.wait_ge(K.s_used, c + (first + 1))
                    evac["act"](act, c, s - first, turn, 2 * ((s - first) % 2), s_free)
            over_chunks(act, first, n, step, unroll, K.act_chain, act_links)

        @block.vector
        def _(dve):
            if evac["frees"] == "dve":
                dve.nop().then_inc(s_free, 2)
            if "head_dve" in evac:
                evac["head_dve"](dve)

            def step(c, s, turn):
                guarded(K, first, split_lo)(dve, c, s, turn)
                if "dve" in evac:
                    dve.wait_ge(K.s_used, c + (first + 1))
                    evac["dve"](dve, c, s - first, turn, 2 * ((s - first) % 2), s_free)
            over_chunks(dve, first, n, step, unroll, K.dve_chain, dve_links)


def product_rows512(K, first, groups, x_hi, x_lo, tok0, evac, unroll=8, load=None):
    s_free, s_load = sems(K, "banks_free", "loaded")
    n = 4 * groups

    with K.nc.Block() as block:
        @block.sync
        def _(sp):
            if load:
                sp.dma_start(*load).then_inc(s_load, 16)
            load_chunks(K, sp, first, n)
            if load:
                sp.wait_ge(s_load, 16)

        @block.tensor
        def _(pe):
            def step(c, s, turn):
                u = s - first
                pe.wait_ge(K.s_lo, c + (first + 1))
                if u % 4 == 0:
                    pe.wait_ge(s_free, c + 4)
                for t in range(TT):
                    for k2 in range(2):
                        k = 2 * (u % 4) + k2
                        w = slice(k2 * 512, k2 * 512 + 512)
                        a = tok0 + t * P
                        out = K.ps[:, 4 * (u // 4 % 2) + t, :]
                        pe.matmul(out, x_hi[:, k, a:a + P], K.whi[:, s % HL, w], start=k == 0, stop=False)
                        pe.matmul(out, x_lo[:, k, a:a + P], K.whi[:, s % HL, w], start=False, stop=False)
                        mm = pe.matmul(out, x_hi[:, k, a:a + P], K.wlo[:, s % HL, w], start=False, stop=k == KT - 1)
                mm.then_inc(K.s_used, 1)
            over_chunks(pe, first, n, step, unroll)

        @block.scalar
        def _(act):
            act.nop().then_inc(s_free, 8)

            def step(c, s, turn):
                u = s - first
                guarded(K, first, split_hi)(act, c, s, turn)
                if u % 4 == 3:
                    act.wait_ge(K.s_used, c + (first + 1))
                    evac(act, c, u, K.ps[:, 4 * (u // 4 % 2):4 * (u // 4 % 2) + 4, :]).then_inc(s_free, 4)
            over_chunks(act, first, n, step, unroll)

        @block.vector
        def _(dve):
            def step(c, s, turn):
                guarded(K, first, split_lo)(dve, c, s, turn)
            over_chunks(dve, first, n, step, unroll)


def product_rows(K, first, n, x_hi, x_lo, finish, unroll=2):
    s_added, = sems(K, "rows_added")

    with K.nc.Block() as block:
        @block.tensor
        def _(pe):
            for c in range(n):
                pe.wait_ge(K.s_lo, first + c + 1)
                w = (first + c) % HL
                for t in range(TT):
                    for half in range(2):
                        out = K.ps[:, 2 * t + half, :]
                        wc = slice(half * 512, half * 512 + 512)
                        xh, xl = x_hi[:, c, t * P:(t + 1) * P], x_lo[:, c, t * P:(t + 1) * P]
                        pe.matmul(out, xh, K.whi[:, w, wc], start=c == 0, stop=False)
                        pe.matmul(out, xl, K.whi[:, w, wc], start=False, stop=False)
                        mm = pe.matmul(out, xh, K.wlo[:, w, wc], start=False, stop=c == n - 1)
                mm.then_inc(K.s_used, 1)

        @block.scalar
        def _(act):
            over_chunks(act, first, n, lambda c, s, turn: guarded(K, first, split_hi)(act, c, s, turn))

        @block.vector
        def _(dve):
            over_chunks(dve, first, n, lambda c, s, turn: guarded(K, first, split_lo)(dve, c, s, turn))
            dve.wait_ge(K.s_used, first + n)
            for t in range(TT):
                dve.tensor_tensor(K.h[:, t, :], K.h[:, t, :],
                                  K.ps[:, 2 * t:2 * t + 2, :].rearrange("p a b -> p (a b)"), ALU.add).then_inc(s_added, 1)

        @block.sync
        def _(sp):
            load_chunks(K, sp, first, n)
            if finish:
                finish(sp, s_added)



def norm_rows(K, gain, meta):
    meta_in, meta = meta, 0 if meta is None else 1
    ss, rs, xn, gb = K.t_ss, K.t_rs, K.t_xn, K.t_gain
    s_gain, s_sum, s_xn, s_tr, s_hi, s_ev, s_mt = sems(
        K, "gain_in", "sums", "xn", "transposed", "hi", "evacuated", "meta")
    tiles = [(K.h[:, t, :], P, META * meta + t * P) for t in range(TT)]
    if meta:
        tiles.append((K.hm[0:META, :], META, 0))
    nt = len(tiles)

    with K.nc.Block() as block:
        @block.sync
        def _(sp):
            if meta:
                sp.dma_start(K.hm[:], meta_in).then_inc(s_mt, 16)
            sp.dma_start(gb[:], gain).then_inc(s_gain, 16)

        @block.scalar
        def _(act):
            ch = K.act_chain
            for t, (h, rows, _) in enumerate(tiles):
                if t == TT:
                    act.wait_ge(s_mt, 16)
                act.activation(xn[0:rows, t, :], h, ACT.Square, accum_out=ss[0:rows, t:t + 1]).then_inc(s_sum, 1)
            act.wait_ge(s_sum, nt + 1)
            act.activation(rs[:, 0:nt], ss[:, 0:nt], ACT.Sqrt).then_inc(s_sum, 1)
            for k in range(KT):
                act.wait_ge(s_tr, k + 1)
                act.activation(K.nx_hi[:, k, META * meta:META * meta + SEQ], K.ps[:, k, :], ACT.Copy).then_inc(s_hi, 1)

        @block.vector
        def _(dve):
            ch = K.dve_chain
            dve.wait_ge(s_sum, nt)
            dve.tensor_scalar(ss[:, 0:nt], ss[:, 0:nt], 1.0 / D, EPS, ALU.mult, ALU.add).then_inc(s_sum, 1)
            dve.wait_ge(s_sum, nt + 2)
            ch.link(dve, dve.reciprocal(rs[:, 0:nt], rs[:, 0:nt]))
            dve.wait_ge(s_gain, 16)
            for t, (h, rows, _) in enumerate(tiles):
                dve.scalar_tensor_tensor(xn[0:rows, t, :], h, rs[0:rows, t:t + 1], gb[0:rows, :],
                                         ALU.mult, ALU.mult).then_inc(s_xn, 1)
            for k in range(KT):
                dve.wait_ge(s_hi, k + 1)
                dve.tensor_tensor(K.nx_lo[:, k, META * meta:META * meta + SEQ], K.ps[:, k, :],
                                  K.nx_hi[:, k, META * meta:META * meta + SEQ].bitcast(F32), ALU.subtract).then_inc(s_ev, 1)
            if meta:
                dve.wait_ge(s_mt, 17)
                pm = K.ps[:, 0, 0:KT * META].rearrange("p (k m) -> p k m", m=META)
                ch.link(dve, dve.tensor_copy(K.nx_hi[:, :, 0:META], pm))
                dve.tensor_tensor(K.nx_lo[:, :, 0:META], pm, K.nx_hi[:, :, 0:META].bitcast(F32), ALU.subtract)

        @block.tensor
        def _(pe):
            for k in range(KT):
                for t in range(TT):
                    if k == 0:
                        pe.wait_ge(s_xn, t + 1)
                    tr = pe.transpose(K.ps[:, k, t * P:(t + 1) * P], xn[:, t, k * P:(k + 1) * P], cst(K, "ident"))
                tr.then_inc(s_tr, 1)
            if meta:
                pe.wait_ge(s_xn, nt)
                pe.wait_ge(s_ev, 1)
                for k in range(KT):
                    tr = pe.transpose(K.ps[:, 0, k * META:(k + 1) * META], xn[0:META, TT, k * P:(k + 1) * P],
                                      cst(K, "ident", META)[:, 0:META])
                tr.then_inc(s_mt, 1)



def start(K, v, wait_x=True):
    s_in, = sems(K, "inputs_in")
    with K.nc.Block() as block:
        @block.sync
        def _(sp):
            sp.dma_start(K.h[:], v["x"].rearrange("b (t p) d -> p (b t) d", p=P)).then_inc(s_in, 16)
            for g in range(RAW):
                sp.dma_start(K.raw[:, g], K.stream[g]).then_inc(K.s_raw[g], 16)
            sp.dma_start(K.const[:], v["const"][:, 0:K.const.shape[1]]).then_inc(s_in, 16)
            sp.dma_start(K.param[:], v["param"]).then_inc(s_in, 16)
            sp.wait_ge(s_in, 48)

        @block.scalar
        def _(act):
            for g in range(HL):
                act.wait_ge(K.s_raw[g], 16)
                act.activation(K.whi[:, g], K.raw[:, g], ACT.Copy).then_inc(K.s_hi, 1)

        @block.vector
        def _(dve):
            dve.memset(K.t_ss[:], 1.0)
            for g in range(HL):
                dve.wait_ge(K.s_hi, g + 1)
                dve.tensor_tensor(K.wlo[:, g], K.raw[:, g], K.whi[:, g].bitcast(F32), ALU.subtract).then_inc(K.s_lo, 1)



def project1(K, R, v):
    product_rows512(K, K.at, 4, K.nx_hi, K.nx_lo, 0,
                    lambda act, c, u, banks: act.activation(
                        R.rows[:, ds(c * 512 - 3 * 512, 2048)], banks.rearrange("p a b -> p (a b)"), ACT.Copy),
                    load=(K.const1[:], v["const"][:, K.const.shape[1]:]))
    K.at += 16
    product_cols(K, K.at, 8, None, None, [(K.nx_hi, K.nx_lo, [(0, SEQ)])], {
        "frees": "act",
        "act": lambda act, c, u, turn, b, s_free: act.activation(
            R.cols[:, ds(c * 512, 512)], K.ps[:, b, :], ACT.Copy).then_inc(s_free, 1)})
    K.at += 8



def rope(K, dve, x, cos, sin, t):
    ch = K.dve_chain
    x1, x2 = x
    dve.tensor_tensor(t[0], x1, cos, ALU.mult)
    dve.tensor_tensor(t[1], x2, sin, ALU.mult)
    dve.tensor_tensor(t[2], x2, cos, ALU.mult)
    ch.link(dve, dve.tensor_tensor(t[3], x1, sin, ALU.mult))
    dve.tensor_tensor(x1, t[0], t[1], ALU.subtract)
    ch.link(dve, dve.tensor_tensor(x2, t[2], t[3], ALU.add))


def nsa_prepare(K, R, v):
    s_ss, s_rt, s_q, s_kd, s_tr, s_ev, s_x2, s_w1, s_w1b, s_wu, s_tb, s_g, s_gt, s_gc, s_o2, s_kt, s_gate = sems(
        K, "square_sums", "roots", "q_rows", "k_rows", "transposed", "evacuated", "pairs_in", "w1_even_in",
        "w1_odd_in", "w1_used", "blocks", "gelu", "gelu_t", "gelu_tc", "cmp_out", "cmp_k_t", "gates_t")
    rows = R.rows.rearrange("p (g t c) -> p g t c", g=4, t=TT)
    cols = R.cols.rearrange("p (f t) -> p f t", f=8)
    q = rows[:, 0].rearrange("p t (h d) -> p (t h) d", d=64)
    ks = [rows[:, 1, :, b * 256:b * 256 + 128].rearrange("p t (g d) -> p t g d", d=64) for b in range(2)]
    with ExitStack() as c:
        ss = scratch(K, c, "ss", [P, 48])
        rt = scratch(K, c, "rt", [P, 48])
        tmp = scratch(K, c, "rope_t", [P, 4, 256])
        kd = scratch(K, c, "k_dup", [P, TT, 4, 2, 64])
        x2 = scratch(K, c, "x_pairs", [P, 4, SEQ])
        tb = scratch(K, c, "x_blocks", [P, 2, CMP_J, 64])
        sq = tb.rearrange("p a b c -> p (a b c)")
        w1 = scratch(K, c, "cmp_w1", [P, 2, 4, 256])
        gl = scratch(K, c, "gelu", [64, 2, 256])
        glt = scratch(K, c, "gelu_t", [P, 2, 2, 64])
        kc = scratch(K, c, "k_cmp", [64, 2, 64])
        s64 = scratch(K, c, "s64", [64, 4])
        t64 = scratch(K, c, "t64", [64, 64 + 32])
        n_ss = 3

        with K.nc.Block() as block:
            @block.sync
            def _(sp):
                for kind in range(2):
                    for g in range(NSA_G):
                        src = cols[g * 64:g * 64 + 64, kind]
                        sp.dma_start(x2[0:64, 2 * kind + g, :], src).then_inc(s_x2, 16)
                        sp.dma_start(x2[64:128, 2 * kind + g, 0:SEQ - 1], src[:, 1:SEQ]).then_inc(s_x2, 16)
                for i in range(8):
                    w = (v["cmp_w1_k"], v["cmp_w1_v"])[i // 4].rearrange("(j p) n -> p j n", p=P)
                    if i >= 2:
                        sp.wait_ge(s_wu, i - 1)
                    sp.dma_start(w1[:, i % 2], w[:, 4 * (i % 4):4 * (i % 4) + 4]).then_inc((s_w1, s_w1b)[i % 2], 16)

            @block.vector
            def _(dve):
                ch = K.dve_chain
                eps_q = 64 * EPS
                ch.link(dve, dve.tensor_tensor(sq[:], rows[:, 0].rearrange("p t c -> p (t c)"),
                                               rows[:, 0].rearrange("p t c -> p (t c)"), ALU.mult))
                ch.link(dve, dve.tensor_reduce(ss[:, 0:32], sq.rearrange("p (a d) -> p a d", d=64), AX.X, ALU.add))
                ch.link(dve, dve.tensor_scalar(ss[:, 0:32], ss[:, 0:32], eps_q, None, ALU.add))
                for b in range(2):
                    sqk = sq[:, 0:512].rearrange("p (t g d) -> p t g d", t=TT, g=2)
                    ch.link(dve, dve.tensor_tensor(sqk, ks[b], ks[b], ALU.mult))
                    ch.link(dve, dve.tensor_reduce(ss[:, 32 + 8 * b:40 + 8 * b],
                                                   sq[:, 0:512].rearrange("p (a d) -> p a d", d=64), AX.X, ALU.add))
                dve.tensor_scalar(ss[:, 32:48], ss[:, 32:48], 1.0 / 64, EPS, ALU.mult, ALU.add).then_inc(s_ss, 1)
                dve.wait_ge(s_rt, 1)
                ch.link(dve, dve.reciprocal(rt[:], rt[:]))
                ch.link(dve, dve.tensor_tensor(q, q, bc(rt[:, 0:32], [P, 32, 64], 2), ALU.mult))
                ch.link(dve, dve.tensor_tensor(q, q, bc(par(K, "q_gain"), [P, 32, 64], 1), ALU.mult))
                cos = cst(K, "cos").rearrange("p (t d) -> p t d", d=8)
                sin = cst(K, "sin").rearrange("p (t d) -> p t d", d=8)
                q4 = rows[:, 0].rearrange("p t (h d) -> p t h d", d=64)
                tq = [tmp[:, i].rearrange("p (t h d) -> p t h d", t=TT, h=8) for i in range(4)]
                rope(K, dve, (q4[:, :, :, 0:8], q4[:, :, :, 8:16]), bc(cos, [P, TT, 8, 8], 2),
                     bc(sin, [P, TT, 8, 8], 2), tq)
                dve.nop().then_inc(s_q, 1)
                for b in range(2):
                    r = rt[:, 32 + 8 * b:40 + 8 * b].rearrange("p (t g) -> p t g", t=TT)
                    ch.link(dve, dve.tensor_tensor(ks[b], ks[b], bc(r, [P, TT, 2, 64], 3), ALU.mult))
                    gain = par(K, f"k_gain{b + 1}").unsqueeze(1).unsqueeze(1).to_broadcast([P, TT, 2, 64])
                    ch.link(dve, dve.tensor_tensor(ks[b], ks[b], gain, ALU.mult))
                    tk = [tmp[:, i, 0:64].rearrange("p (t g d) -> p t g d", t=TT, g=2) for i in range(4)]
                    rope(K, dve, (ks[b][:, :, :, 0:8], ks[b][:, :, :, 8:16]), bc(cos, [P, TT, 2, 8], 2),
                         bc(sin, [P, TT, 2, 8], 2), tk)
                    for copy in range(2):
                        dve.tensor_copy(kd[:, :, 2 * b:2 * b + 2, copy, :], ks[b]).then_inc(s_kd, 1)
                ch.link(dve, dve.memset(tb[:], 0.0))
                dve.wait_ge(s_x2, 16 * 8)
                for kind in range(2):
                    pe_ = par(K, ("pe_k", "pe_v")[kind])
                    for g in range(NSA_G):
                        xs = x2[:, 2 * kind + g, :].rearrange("p (n s) -> p s n", s=16)
                        for hf in range(2):
                            dst = tb[:, kind, 8 * hf:8 * hf + 8, 32 * g:32 * g + N_CMP]
                            dve.tensor_tensor(dst, xs[:, 0:16:2, hf:hf + N_CMP],
                                              bc(pe_[:, 8 * hf:8 * hf + 8], [P, 8, N_CMP], 2), ALU.add).then_inc(s_tb, 1)
                dve.wait_ge(s_gt, 1)
                dve.tensor_copy(glt.rearrange("p a b c -> p (a b c)"), K.ps[:, 2, 0:256]).then_inc(s_gc, 1)
                dve.wait_ge(s_o2, 1)
                dve.tensor_copy(R.vcmp[:], K.ps[0:64, 3, 64:128])
                ch.link(dve, dve.tensor_copy(kc[:, 0], K.ps[0:64, 3, 0:64]))
                ch.link(dve, dve.tensor_tensor(t64[:, 0:64], kc[:, 0], kc[:, 0], ALU.mult))
                ch.link(dve, dve.tensor_reduce(s64[:, 0:1], t64[:, 0:64], AX.X, ALU.add))
                dve.tensor_scalar(s64[:, 1:2], s64[:, 0:1], 1.0 / 64, EPS, ALU.mult, ALU.add).then_inc(s_ss, 1)
                dve.wait_ge(s_rt, 2)
                ch.link(dve, dve.reciprocal(s64[:, 2:3], s64[:, 2:3]))
                ch.link(dve, dve.scalar_tensor_tensor(kc[:, 0], kc[:, 0], s64[:, 2:3], par(K, "k_gain0", 64), ALU.mult, ALU.mult))
                rope(K, dve, (kc[:, 0, 0:8], kc[:, 0, 8:16]), cst(K, "cos_cmp", 64), cst(K, "sin_cmp", 64),
                     [t64[:, 64 + 8 * i:72 + 8 * i] for i in range(4)])
                dve.tensor_copy(kc[:, 1], kc[:, 0]).then_inc(s_kt, 1)
                dve.wait_ge(s_kt, 2)
                dve.tensor_copy(R.kcT[:], K.ps[:, 3, 128:192])

            @block.scalar
            def _(act):
                act.wait_ge(s_ss, 1)
                act.activation(rt[:], ss[:], ACT.Sqrt).then_inc(s_rt, 1)
                for i in range(8):
                    act.wait_ge(s_tr, i + 1)
                    dst = R.qT[:, i, :] if i < 4 else R.kT[:, i - 4, :]
                    act.activation(dst, K.ps[:, 4 + i % 4, :], ACT.Copy).then_inc(s_ev, 1)
                act.wait_ge(s_gate, 1)
                act.activation(R.gates[:], K.ps[:, 2, 0:96], ACT.Sigmoid)
                for kind in range(2):
                    act.wait_ge(s_wu, 4 * kind + 4)
                    act.activation(gl[:, kind], K.ps[0:64, kind, 0:256], ACT.Gelu_apprx_tanh).then_inc(s_g, 1)
                act.wait_ge(s_ss, 2)
                act.activation(s64[:, 2:3], s64[:, 1:2], ACT.Sqrt).then_inc(s_rt, 1)

            @block.tensor
            def _(pe):
                ident = cst(K, "ident")
                for t in range(TT):
                    tr = pe.transpose(K.ps[:, 2, 24 * t:24 * t + 24], cols[0:24, 2, t * P:(t + 1) * P],
                                      cst(K, "ident", 24)[:, 0:24])
                tr.then_inc(s_gate, 1)
                pe.wait_ge(s_q, 1)
                for i in range(4):
                    for t in range(TT):
                        tr = pe.transpose(K.ps[:, 4 + i, t * P:(t + 1) * P], rows[:, 0, t, i * P:(i + 1) * P], ident)
                    tr.then_inc(s_tr, 1)
                pe.wait_ge(s_kd, 4)
                for i in range(4):
                    pe.wait_ge(s_ev, i + 1)
                    for t in range(TT):
                        tr = pe.transpose(K.ps[:, 4 + i, t * P:(t + 1) * P],
                                          kd[:, t, i].rearrange("p c d -> p (c d)"), ident)
                    tr.then_inc(s_tr, 1)
                for kind in range(2):
                    pe.wait_ge(s_tb, 4 * kind + 4)
                    for j in range(CMP_J):
                        i = 4 * kind + j // 4
                        if j % 4 == 0:
                            pe.wait_ge((s_w1, s_w1b)[i % 2], 16 * (i // 2 + 1))
                        mm = pe.matmul(K.ps[0:64, kind, 0:256], tb[:, kind, j], w1[:, i % 2, j % 4], start=j == 0, stop=j == CMP_J - 1)
                        if j % 4 == 3:
                            mm.then_inc(s_wu, 1)
                for kind in range(2):
                    pe.wait_ge(s_g, kind + 1)
                    for f in range(2):
                        tr = pe.transpose(K.ps[:, 2, (2 * kind + f) * 64:(2 * kind + f + 1) * 64],
                                          gl[:, kind, f * P:(f + 1) * P], cst(K, "ident", 64)[:, 0:64])
                tr.then_inc(s_gt, 1)
                pe.wait_ge(s_gc, 1)
                for kind in range(2):
                    w2 = par(K, ("cmp_w2_k", "cmp_w2_v")[kind])
                    for f in range(2):
                        mm = pe.matmul(K.ps[0:64, 3, 64 * kind:64 * kind + 64], glt[:, kind, f], w2[:, f * 64:f * 64 + 64],
                                       start=f == 0, stop=f == 1)
                mm.then_inc(s_o2, 1)
                pe.wait_ge(s_kt, 1)
                pe.transpose(K.ps[:, 3, 128:192], kc.rearrange("p c d -> p (c d)"), cst(K, "ident", 64)[:, 0:64]).then_inc(s_kt, 1)


def nsa_compressed(K, R):
    s_sc, s_mx, s_ex, s_w, s_tr, s_cp = sems(K, "scores", "maxima", "probs", "weighted", "transposed", "copied")
    keep = cst(K, "cmp_keep").rearrange("p (t g n) -> p t g n", t=TT, g=2)
    cbias = cst(K, "cmp_bias").rearrange("p (t g n) -> p t g n", t=TT, g=2)
    gates = R.gates.rearrange("p (t i a b) -> p t a i b", t=TT, i=4, a=2)
    with ExitStack() as c:
        sc = scratch(K, c, "scores", [P, TT, 2, 4, 64])
        mx, sm, fc = [scratch(K, c, n, [P, TT, 2, 4]) for n in ("max", "sum", "factor")]
        with K.nc.Block() as block:
            @block.tensor
            def _(pe):
                for t in range(TT):
                    for a in range(2):
                        for i in range(4):
                            mm = pe.matmul(K.ps[:, 4 * a + t, 64 * i:64 * i + 64], R.qT[64 * a:64 * a + 64, i, t * P:(t + 1) * P],
                                           R.kcT[64 * a:64 * a + 64, :], start=True, stop=True)
                        mm.then_inc(s_sc, 1)
                for t in range(TT):
                    pe.wait_ge(s_w, t + 1)
                    for a in range(2):
                        for i in range(4):
                            tr = pe.transpose(K.ps[0:64, 4 * a + t, i * P:(i + 1) * P], sc[:, t, a, i], cst(K, "ident"))
                    tr.then_inc(s_tr, 1)

            @block.vector
            def _(dve):
                ch = K.dve_chain

                def maxima(t):
                    for a in range(2):
                        dve.wait_ge(s_sc, 2 * t + a + 1)
                        for g in range(2):
                            last = dve.tensor_tensor(sc[:, t, a, 2 * g:2 * g + 2],
                                                     K.ps[:, 4 * a + t, P * g:P * g + P].rearrange("p (i n) -> p i n", n=64),
                                                     bc(cbias[:, t, g], [P, 2, 64], 1), ALU.add)
                    ch.link(dve, last)
                    dve.tensor_reduce(mx[:, t], sc[:, t], AX.X, ALU.max, negate=True).then_inc(s_mx, 1)

                def weights(t):
                    dve.wait_ge(s_ex, t + 1)
                    ch.link(dve, dve.reciprocal(fc[:, t], sm[:, t]))
                    ch.link(dve, dve.scalar_tensor_tensor(fc[:, t], fc[:, t], keep[:, t, 0, 0:1], gates[:, t, :, :, 0],
                                                          ALU.mult, ALU.mult))
                    dve.tensor_tensor(sc[:, t], sc[:, t], fc[:, t].unsqueeze(3).to_broadcast([P, 2, 4, 64]),
                                      ALU.mult).then_inc(s_w, 1)
                maxima(0)
                for t in range(TT):
                    if t + 1 < TT:
                        maxima(t + 1)
                    weights(t)
                for t in range(TT):
                    dve.wait_ge(s_tr, t + 1)
                    dve.tensor_copy(R.ptc[:, :, 1, t * P:(t + 1) * P], K.ps[0:64, 4 + t, :].rearrange("p (i q) -> p i q", q=P))

            @block.scalar
            def _(act):
                for t in range(TT):
                    act.wait_ge(s_mx, t + 1)
                    for a in range(2):
                        for i in range(4):
                            last = act.activation(sc[:, t, a, i], sc[:, t, a, i], ACT.Exp, bias=mx[:, t, a, i:i + 1],
                                                  accum_out=sm[:, t, a, i:i + 1])
                    last.then_inc(s_ex, 1)
                for t in range(TT):
                    act.wait_ge(s_tr, t + 1)
                    act.activation(R.ptc[:, :, 0, t * P:(t + 1) * P], K.ps[0:64, t, :].rearrange("p (i q) -> p i q", q=P), ACT.Copy)


def nsa_attend(K, R):
    s_sc, s_mx, s_ex, s_w, s_tr, s_pt0, s_pt1, s_pv, s_oh, s_oc = sems(
        K, "scores", "maxima", "probs", "weighted", "transposed", "selected_t", "window_t", "pv", "o_hi", "o_copied")
    rows = R.rows.rearrange("p (g t c) -> p g t c", g=4, t=TT)
    units = [(h, t) for h in range(NSA_H) for t in range(TT)]
    NU = len(units)

    def pair_done(u):
        return 0 <= u < NU and units[u][0] % 2 == 1 and units[u][1] == TT - 1
    with ExitStack() as c:
        pr = scratch(K, c, "probs", [P, 2, 2, SEQ])
        pt = scratch(K, c, "probs_t", [P, 2, 2, SEQ])
        mx, sm, fc = [scratch(K, c, n, [P, 2, 2]) for n in ("max", "sum", "factor")]

        with K.nc.Block() as block:
            @block.tensor
            def _(pe):
                ident, causal = cst(K, "ident"), cst(K, "causal")

                def scores(u, b):
                    if u >= NU:
                        return
                    h, t = units[u]
                    g, b0, ext = h // 4, 64 * (h % 2), (t + 1) * P
                    if u >= 2:
                        pe.wait_ge(s_ex, 2 * (u - 2) + b + 1)
                    out = K.ps[:, 2 * (u % 2) + b, 0:ext]
                    pe.matmul(out, R.qT[b0:b0 + 64, h // 2, t * P:(t + 1) * P], R.kT[b0:b0 + 64, 2 * b + g, 0:ext],
                              start=True, stop=False, skip_group_check=True)
                    pe.matmul(out[:, t * P:ext], ident, causal, start=False, stop=True, skip_group_check=True).then_inc(s_sc, 1)

                def transposed(u, b):
                    h, t = units[u]
                    pe.wait_ge(s_w, 2 * u + b + 1)
                    if u >= 1:
                        pe.wait_ge((s_pt0, s_pt1)[b], u)
                    for kt in range(t + 1):
                        tr = pe.transpose(K.ps[:, 4 + b, kt * P:(kt + 1) * P], pr[:, u % 2, b, kt * P:(kt + 1) * P], ident)
                    tr.then_inc(s_tr, 1)

                def values(u, b):
                    if u < 0:
                        return
                    h, t = units[u]
                    g, b0 = h // 4, 64 * (h % 2)
                    out = K.ps[b0:b0 + 64, 6 + h // 2 % 2, t * P:(t + 1) * P]
                    if b == 0 and h % 2 == 0 and t == 0 and h >= 4:
                        pe.wait_ge(s_oc, h // 2 - 1)
                    pe.wait_ge((s_pt0, s_pt1)[b], u + 1)
                    for kt in range(t + 1):
                        vv = rows[:, 1, kt, 256 * b + 128 + g * 64:256 * b + 192 + g * 64]
                        mm = pe.matmul(out, vv, pt[:, u % 2, b, kt * P:(kt + 1) * P], start=b == 0 and kt == 0,
                                       stop=b == 1 and kt == t, skip_group_check=True)
                    if b == 0:
                        pe.matmul(out, R.vcmp[:], R.ptc[:, h // 2, h % 2, t * P:(t + 1) * P], start=False, stop=False,
                                  skip_group_check=True)
                    else:
                        mm.then_inc(s_pv, 1)
                for u in range(2):
                    for b in range(2):
                        scores(u, b)
                for u in range(NU):
                    for b in range(2):
                        transposed(u, b)
                        scores(u + 2, b)
                        values(u - 1, b)
                for b in range(2):
                    values(NU - 1, b)

            @block.vector
            def _(dve):
                ch = K.dve_chain

                def maximum(u, b):
                    if u < NU:
                        dve.wait_ge(s_sc, 2 * u + b + 1)
                        dve.tensor_reduce(mx[:, u % 2, b:b + 1], K.ps[:, 2 * (u % 2) + b, 0:(units[u][1] + 1) * P], AX.X, ALU.max,
                                          negate=True).then_inc(s_mx, 1)

                def weights(u):
                    if u >= NU:
                        return
                    h, t = units[u]
                    dve.wait_ge(s_ex, 2 * u + 2)
                    ch.link(dve, dve.reciprocal(fc[:, u % 2], sm[:, u % 2]))
                    ch.link(dve, dve.tensor_tensor(fc[:, u % 2], fc[:, u % 2],
                                                   R.gates[:, t * 24 + h * 3 + 1:t * 24 + h * 3 + 3], ALU.mult))
                    for b in range(2):
                        p = pr[:, u % 2, b, 0:(t + 1) * P]
                        dve.tensor_scalar(p, p, fc[:, u % 2, b:b + 1], None, ALU.mult).then_inc(s_w, 1)

                def o_lo(u):
                    if pair_done(u):
                        i = units[u][0] // 2
                        dve.wait_ge(s_oh, i + 1)
                        dve.tensor_tensor(K.nx_lo[:, i, 0:SEQ], K.ps[:, 6 + i % 2, :], K.nx_hi[:, i, 0:SEQ].bitcast(F32),
                                          ALU.subtract).then_inc(s_oc, 1)
                for u in range(2):
                    for b in range(2):
                        maximum(u, b)
                weights(0)
                for u in range(NU):
                    weights(u + 1)
                    maximum(u + 2, 0)
                    dve.wait_ge(s_tr, 2 * u + 2)
                    dve.tensor_copy(pt[:, u % 2, 1, 0:(units[u][1] + 1) * P],
                                    K.ps[:, 5, 0:(units[u][1] + 1) * P]).then_inc(s_pt1, 1)
                    maximum(u + 2, 1)
                    o_lo(u - 2)
                o_lo(NU - 1)

            @block.scalar
            def _(act):
                def exps(u):
                    if u >= NU:
                        return
                    h, t = units[u]
                    for b in range(2):
                        act.wait_ge(s_mx, 2 * u + b + 1)
                        act.activation(pr[:, u % 2, b, 0:(t + 1) * P], K.ps[:, 2 * (u % 2) + b, 0:(t + 1) * P], ACT.Exp,
                                       bias=mx[:, u % 2, b:b + 1], accum_out=sm[:, u % 2, b:b + 1]).then_inc(s_ex, 1)

                def o_hi(u):
                    if pair_done(u):
                        i = units[u][0] // 2
                        act.wait_ge(s_pv, u + 1)
                        act.activation(K.nx_hi[:, i, 0:SEQ], K.ps[:, 6 + i % 2, :], ACT.Copy).then_inc(s_oh, 1)
                exps(0)
                exps(1)
                for u in range(NU):
                    act.wait_ge(s_tr, 2 * u + 1)
                    act.activation(pt[:, u % 2, 0, 0:(units[u][1] + 1) * P], K.ps[:, 4, 0:(units[u][1] + 1) * P],
                                   ACT.Copy).then_inc(s_pt0, 1)
                    exps(u + 2)
                    o_hi(u - 1)
                o_hi(NU - 1)



def gla(K, R):
    (s_x, s_xb, s_ab, s_la, s_b, s_eb, s_bl, s_kd, s_kt, s_kc, s_at, s_am, s_ds, s_st, s_o, s_of, s_ss, s_rt,
     s_on, s_tr, s_hi, s_lo) = sems(
        K, "gate_logits", "biased", "log_parts", "log_a", "cum", "exps", "last", "k_decayed", "kd_t", "kd_rows",
        "scores_t", "masked_t", "states_in", "states", "o_sums", "o_free", "squares", "roots", "normed", "o_t", "o_hi", "o_lo")
    rows = R.rows.rearrange("p (g t c) -> p g t c", g=4, t=TT)
    cols = R.cols.rearrange("p (f t) -> p f t", f=8)
    gv, gout, glr = rows[:, 2], rows[:, 3], cols[0:16, 7]
    with ExitStack() as c:
        la = scratch(K, c, "log_a", [P, TT, 256])
        e1 = scratch(K, c, "exp1", [P, TT, 256])
        eb = scratch(K, c, "exp_b", [P, 2, SEQ])
        enb = scratch(K, c, "exp_nb", [P, 2, SEQ])
        ekd = scratch(K, c, "exp_kd", [P, 2, SEQ])
        bl = scratch(K, c, "b_last", [P, 2, 8])
        dec = scratch(K, c, "decay", [P, 2, 8])
        kd = scratch(K, c, "kd_rows", [P, TT, 256])
        am = scratch(K, c, "scores_m", [P, 2, GLA_H, P])
        st = scratch(K, c, "states", [P, 8, 2, P])
        o, sil = rows[:, 0], gout
        sq = scratch(K, c, "sq", [P, 512])
        ss = scratch(K, c, "ss", [P, 32])
        qt, kt, kdt = eb, enb, ekd

        with K.nc.Block() as block:
            @block.tensor
            def _(pe):
                ident, tri = cst(K, "ident"), cst(K, "tri_incl")
                for t in range(TT):
                    mm = pe.matmul(K.ps[:, t // 2, 256 * (t % 2):256 * (t % 2) + 256], glr[:, t * P:(t + 1) * P],
                                   par(K, "w_gate2", 16), start=True, stop=True)
                mm.then_inc(s_x, 1)
                pe.wait_ge(s_la, 1)
                for f in range(2):
                    for t in range(TT):
                        mm = pe.matmul(K.ps[:, 2 + f, t * P:(t + 1) * P], la[:, t, f * P:(f + 1) * P], tri, start=True, stop=True)
                mm.then_inc(s_b, 1)
                pe.wait_ge(s_kd, 1)
                for f in range(2):
                    for t in range(TT):
                        tr = pe.transpose(K.ps[:, 4 + t // 2, 256 * (t % 2) + f * P:256 * (t % 2) + (f + 1) * P],
                                          kdt[:, f, t * P:(t + 1) * P], ident)
                tr.then_inc(s_kt, 1)
                pe.wait_ge(s_kc, 1)
                for ck in range(8):
                    t, r0 = ck // 2, CH * (ck % 2)
                    for hh in range(GLA_H):
                        b0, at = 64 * (hh % 2), 256 * (ck // 2 % 2) + P * (hh // 2)
                        mm = pe.matmul(K.ps[b0:b0 + 64, 2 * (ck % 2) + ck // 4, at:at + P],
                                       kd[r0:r0 + 64, t, hh * 64:hh * 64 + 64], gv[r0:r0 + 64, t, hh * P:(hh + 1) * P],
                                       start=True, stop=True, skip_group_check=True)
                    mm.then_inc(s_ds, 1)

                def scores(t):
                    if t >= 1:
                        pe.wait_ge(s_am, t)
                    for hh in range(GLA_H):
                        b0, f = 64 * (hh % 2), hh // 2
                        mm = pe.matmul(K.ps[:, 4 + hh % 2, f * P:(f + 1) * P], kt[b0:b0 + 64, f, t * P:(t + 1) * P],
                                       qt[b0:b0 + 64, f, t * P:(t + 1) * P], start=True, stop=True)
                    mm.then_inc(s_at, 1)
                scores(0)
                for t in range(TT):
                    if t + 1 < TT:
                        scores(t + 1)
                    pe.wait_ge(s_am, t + 1)
                    pe.wait_ge(s_st, min(2 * t + 1, 7))
                    if t >= 1:
                        pe.wait_ge(s_of, t)
                    for hh in range(GLA_H):
                        b0, f = 64 * (hh % 2), hh // 2
                        pe.matmul(K.ps[:, 6 + hh % 2, f * P:(f + 1) * P], am[:, t % 2, hh], gv[:, t, hh * P:(hh + 1) * P],
                                  start=True, stop=False, skip_group_check=True)
                        for c2 in range(2):
                            mm = pe.matmul(K.ps[64 * c2:64 * c2 + 64, 6 + hh % 2, f * P:(f + 1) * P],
                                           qt[b0:b0 + 64, f, t * P + 64 * c2:t * P + 64 * c2 + 64],
                                           st[b0:b0 + 64, 2 * t + c2, f], start=False, stop=c2 == 1, skip_group_check=True)
                    mm.then_inc(s_o, 1)
                pe.wait_ge(s_on, 1)
                for hh in range(GLA_H):
                    for t in range(TT):
                        tr = pe.transpose(K.ps[:, hh, t * P:(t + 1) * P], o[:, t, hh * P:(hh + 1) * P], ident)
                    tr.then_inc(s_tr, 1)

            @block.vector
            def _(dve):
                ch = K.dve_chain
                dve.wait_ge(s_x, 1)
                x4 = K.ps[:, 0:2, :].rearrange("p a (b c) -> p (a b) c", b=2)
                dve.tensor_tensor(la[:], x4, bc(par(K, "b_gate"), [P, TT, 256], 1), ALU.add).then_inc(s_xb, 1)
                dve.wait_ge(s_ab, 1)
                dve.scalar_tensor_tensor(la.rearrange("p t c -> p (t c)"), la.rearrange("p t c -> p (t c)"), 0.0,
                                         e1.rearrange("p t c -> p (t c)"), ALU.min, ALU.subtract).then_inc(s_la, 1)
                dve.wait_ge(s_b, 1)
                for f in range(2):
                    last = dve.tensor_scalar(bl[:, f, :], K.ps[:, 2 + f, CH - 1::CH], 1.0 / 16, None, ALU.mult)
                last.then_inc(s_bl, 1)
                dve.wait_ge(s_eb, 1)
                for f in range(2):
                    last = dve.tensor_tensor(kdt[:, f], kdt[:, f], cols[:, 5 + f], ALU.mult)
                last.then_inc(s_kd, 1)
                for f in range(2):
                    dve.scalar_tensor_tensor(qt[:, f], qt[:, f], GLA_SCALE, cols[:, 3 + f], ALU.mult, ALU.mult)
                    last = dve.tensor_tensor(kt[:, f], kt[:, f], cols[:, 5 + f], ALU.mult)
                last.then_inc(s_kd, 1)
                dve.wait_ge(s_kt, 1)
                dve.tensor_copy(kd.rearrange("p t c -> p (t c)"), K.ps[:, 4:6, :].rearrange("p a b -> p (a b)")).then_inc(s_kc, 1)

                def mask(t):
                    dve.wait_ge(s_at, t + 1)
                    if t >= 2:
                        dve.wait_ge(s_o, t - 1)
                    dve.tensor_tensor(am[:, t % 2].rearrange("p (f b) c -> p b f c", b=2),
                                      K.ps[:, 4:6, 0:256].rearrange("p b (f c) -> p b f c", f=2),
                                      cst(K, "tri_incl").unsqueeze(1).unsqueeze(1).to_broadcast([P, 2, 2, P]),
                                      ALU.mult).then_inc(s_am, 1)

                def evac(t):
                    dve.wait_ge(s_o, t + 1)
                    dve.tensor_copy(o[:, t, :].rearrange("p (f b c) -> p b f c", f=2, b=2),
                                    K.ps[:, 6:8, 0:256].rearrange("p b (f c) -> p b f c", f=2)).then_inc(s_of, 1)
                mask(0)
                ch.link(dve, dve.memset(st[:, 0], 0.0))
                for ck in range(7):
                    dve.wait_ge(s_ds, 4 * (ck // 4) + 4)
                    at = 256 * (ck // 2 % 2)
                    for f in range(2):
                        last = dve.scalar_tensor_tensor(st[:, ck + 1, f], st[:, ck, f], dec[:, f, ck:ck + 1],
                                                        K.ps[:, 2 * (ck % 2) + ck // 4, at + f * P:at + (f + 1) * P],
                                                        ALU.mult, ALU.add)
                    last.then_inc(s_st, 1)
                    dve.wait_ge(s_st, ck + 1)
                for t in range(1, TT):
                    mask(t)
                    evac(t - 1)
                evac(TT - 1)
                for t in range(TT):
                    dve.wait_ge(s_of, t + 1)
                    ch.link(dve, dve.tensor_tensor(sq[:], o[:, t], o[:, t], ALU.mult))
                    ch.link(dve, dve.tensor_reduce(ss[:, 4 * t:4 * t + 4], sq.rearrange("p (h c) -> p h c", h=4), AX.X, ALU.add))
                dve.tensor_scalar(ss[:, 0:16], ss[:, 0:16], 1.0 / P, EPS, ALU.mult, ALU.add).then_inc(s_ss, 1)
                dve.wait_ge(s_rt, 1)
                ch.link(dve, dve.reciprocal(ss[:, 16:32], ss[:, 16:32]))
                o16 = o.rearrange("p t (h c) -> p (t h) c", h=4)
                ch.link(dve, dve.tensor_tensor(o16, o16, bc(ss[:, 16:32], [P, 16, P], 2), ALU.mult))
                ch.link(dve, dve.tensor_tensor(o16, o16, bc(par(K, "gla_gain"), [P, 16, P], 1), ALU.mult))
                dve.tensor_tensor(o, o, sil, ALU.mult).then_inc(s_on, 1)
                for hh in range(GLA_H):
                    dve.wait_ge(s_hi, hh + 1)
                    dve.tensor_tensor(K.nx_lo[:, 4 + hh, 0:SEQ], K.ps[:, hh, :], K.nx_hi[:, 4 + hh, 0:SEQ].bitcast(F32), ALU.subtract)

            @block.scalar
            def _(act):
                ch = K.act_chain
                act.wait_ge(s_xb, 1)
                ch.link(act, act.activation(e1[:], la[:], ACT.Abs))
                ch.link(act, act.activation(e1[:], e1[:], ACT.Exp, scale=-1.0))
                act.activation(e1[:], e1[:], ACT.Ln, bias=1.0).then_inc(s_ab, 1)
                act.wait_ge(s_bl, 1)
                act.activation(eb[:], K.ps[:, 2:4, :], ACT.Exp, scale=1.0 / 16)
                act.activation(enb[:], K.ps[:, 2:4, :], ACT.Exp, scale=-1.0 / 16)
                act.activation(dec[:], bl[:], ACT.Exp)
                for f in range(2):
                    for ck in range(8):
                        last = act.activation(ekd[:, f, ck * CH:(ck + 1) * CH], K.ps[:, 2 + f, ck * CH:(ck + 1) * CH], ACT.Exp,
                                              bias=bl[:, f, ck:ck + 1], scale=-1.0 / 16)
                last.then_inc(s_eb, 1)
                act.activation(sil, gout, ACT.Silu)
                act.wait_ge(s_ss, 1)
                act.activation(ss[:, 16:32], ss[:, 0:16], ACT.Sqrt).then_inc(s_rt, 1)
                for hh in range(GLA_H):
                    act.wait_ge(s_tr, hh + 1)
                    act.activation(K.nx_hi[:, 4 + hh, 0:SEQ], K.ps[:, hh, :], ACT.Copy).then_inc(s_hi, 1)


GLA_SCALE = 64 ** -0.5



def ffn_up(K, act_hi, act_lo, conv, tok0):
    with ExitStack() as c:
        g = scratch(K, c, "gate", [P, 2, SEQ])
        up = scratch(K, c, "up", [P, 2, SEQ])
        w1 = par(K, "conv1_w").rearrange("p (k f t) -> p k f t", k=2, t=3)
        b1 = par(K, "conv1_b").rearrange("p (k f) -> p k f", k=2)

        def evac_act(act, ch, u, turn, b, s_free):
            s_first, s_silu, s_full, s_hi = evac["signals"]
            kind, pb, pair = u % 2, u // 2 % 2, turn * 2 + u // 2
            if conv:
                act.activation((g, up)[kind][:, pb], K.ps[:, b, :], ACT.Identity,
                               scale=w1[:, kind, ds(pair, 1), 2], bias=b1[:, kind, ds(pair, 1)]).then_inc(s_first, 1)
                if kind == 1:
                    act.wait_ge(s_free, ch + 2)
                    act.activation(g[:, pb], g[:, pb], ACT.Silu).then_inc(s_silu, 1)
            elif kind == 0:
                act.activation(g[:, pb], K.ps[:, b, :], ACT.Silu).then_inc(s_silu, 1)
            if kind == 1:
                act.wait_ge(s_full, pair + 1)
                act.activation(act_hi[:, ds(pair, 1), :], up[:, pb].unsqueeze(1), ACT.Copy).then_inc(s_hi, 1)

        def evac_dve(dve, ch, u, turn, b, s_free):
            s_first, s_silu, s_full, s_hi = evac["signals"]
            kind, pb, pair = u % 2, u // 2 % 2, turn * 2 + u // 2
            y = (g, up)[kind][:, pb]
            if conv:
                dve.wait_ge(s_first, ch + 1)
                K.dve_chain.link(dve, dve.scalar_tensor_tensor(
                    y[:, 1:SEQ], K.ps[:, b, 0:SEQ - 1], w1[:, kind, ds(pair, 1), 1], y[:, 1:SEQ], ALU.mult, ALU.add))
                dve.scalar_tensor_tensor(y[:, 2:SEQ], K.ps[:, b, 0:SEQ - 2], w1[:, kind, ds(pair, 1), 0], y[:, 2:SEQ],
                                         ALU.mult, ALU.add).then_inc(s_free, 1)
                if kind == 1:
                    dve.wait_ge(s_free, ch + 3)
            elif kind == 0:
                dve.wait_ge(s_silu, pair + 1)
                dve.nop().then_inc(s_free, 1)
            if kind == 1:
                dve.wait_ge(s_silu, pair + 1)
                if conv:
                    dve.tensor_tensor(y, y, g[:, pb], ALU.mult).then_inc(s_full, 1)
                else:
                    dve.tensor_tensor(y, K.ps[:, b, :], g[:, pb], ALU.mult).then_inc(s_full, 1)
                    dve.wait_ge(s_full, pair + 1)
                    dve.nop().then_inc(s_free, 1)
                dve.wait_ge(s_hi, pair + 1)
                dve.tensor_tensor(act_lo[:, ds(pair, 1), :], up[:, pb].unsqueeze(1),
                                  act_hi[:, ds(pair, 1), :].bitcast(F32), ALU.subtract)
        evac = {"frees": "dve", "act": evac_act, "dve": evac_dve, "table": ACT.Silu,
                "sems": ("first_tap", "silu", "act_full", "act_hi")}
        product_cols(K, K.at, 2 * FT, None, None, [(K.nx_hi, K.nx_lo, [(tok0, tok0 + SEQ)])], evac,
                     dve_links=1 if conv else 0)
    K.at += 2 * FT


def block1(K, v):
    norm_stage(K, v["attn_gain"], None)
    with ExitStack() as c:
        R = Core()
        R.rows, R.cols = scratch(K, c, "rows", [P, 4 * 2048]), scratch(K, c, "cols", [P, 8 * 512])
        K.const1 = scratch(K, c, "const_1", [P, v["const"].shape[1] - K.const.shape[1]])
        project1(K, R, v)
        with ExitStack() as c2:
            R.qT, R.kT = scratch(K, c2, "qT", [P, 4, SEQ]), scratch(K, c2, "kT", [P, 4, SEQ])
            R.kcT, R.vcmp = scratch(K, c2, "kcT", [P, 64]), scratch(K, c2, "vcmp", [64, 64])
            R.gates = scratch(K, c2, "gates", [P, TT * 24])
            nsa_prepare(K, R, v)
            with ExitStack() as c3:
                R.ptc = scratch(K, c3, "probs_c_t", [64, 4, 2, SEQ])
                nsa_compressed(K, R)
                nsa_attend(K, R)
        gla(K, R)
    product_rows(K, K.at, KT, K.nx_hi, K.nx_lo, None)
    K.at += KT
    norm_stage(K, v["ffn_gain"], None)
    with ExitStack() as c:
        act_hi, act_lo = scratch(K, c, "act_hi", [P, FT, SEQ], F32R), scratch(K, c, "act_lo", [P, FT, SEQ], F32R)
        ffn_up(K, act_hi, act_lo, True, 0)
        product_rows(K, K.at, FT, act_hi, act_lo, None)
        K.at += FT



FULL = [(0, HALF), (HALF, T2)]


def norm_cols(K, tiles, bias, scales):
    s_sq, s_ss, s_rt, s_r, s_bc, s_out = sems(K, "squares", "sums", "roots", "factors", "spread", "normed")
    n = len(tiles)
    with ExitStack() as c:
        sq, rt = scratch(K, c, "sq", [P, 2, T2]), scratch(K, c, "rt", [16, T2])
        with K.nc.Block() as block:
            @block.tensor
            def _(pe):
                for i in range(n):
                    pe.wait_ge(s_sq, i + 1)
                    for h, (a, e) in enumerate(FULL):
                        mm = pe.matmul(K.ps[0:16, h, 0:HALF], cst(K, "pick")[:, 15 - i:31 - i], sq[:, i % 2, a:e],
                                       start=i == 0, stop=i == n - 1, skip_group_check=True)
                    mm.then_inc(s_ss, 1)
                pe.wait_ge(s_r, 1)
                for i in range(n):
                    if i >= 3:
                        pe.wait_ge(s_out, i - 2)
                    for h, (a, e) in enumerate(FULL):
                        mm = pe.matmul(K.ps[:, 2 + 2 * (i % 3) + h, 0:HALF], cst(K, "ident", 16)[:, i:i + 1].broadcast_to([16, P]),
                                       rt[:, a:e], start=True, stop=True)
                    mm.then_inc(s_bc, 1)

            @block.scalar
            def _(act):
                act.preload_act_table(ACT.Sqrt)
                for i in range(n):
                    if i >= 2:
                        act.wait_ge(s_ss, i - 1)
                    act.activation(sq[:, i % 2], tiles[i][0], ACT.Square).then_inc(s_sq, 1)
                act.wait_ge(s_ss, n)
                act.activation(rt.rearrange("p (a b) -> p a b", a=2), K.ps[0:16, 0:2, 0:HALF], ACT.Sqrt, bias=bias).then_inc(s_rt, 1)

            @block.vector
            def _(dve):
                dve.wait_ge(s_rt, 1)
                K.dve_chain.link(dve, dve.reciprocal(rt[0:n], rt[0:n]))
                dve.tensor_scalar(rt[0:n], rt[0:n], cst(K, scales, n), None, ALU.mult).then_inc(s_r, 1)
                for i, (x, gain) in enumerate(tiles):
                    dve.wait_ge(s_bc, i + 1)
                    x2 = x.rearrange("p (a b) -> p a b", a=2)
                    f = K.ps[:, 2 + 2 * (i % 3):4 + 2 * (i % 3), 0:HALF]
                    if gain is None:
                        dve.tensor_tensor(x2, f, x2, ALU.mult).then_inc(s_out, 1)
                    else:
                        dve.scalar_tensor_tensor(x2, f, gain, x2, ALU.mult, ALU.mult).then_inc(s_out, 1)


def transpose_units(K, units):
    s_tr, s_act, s_dve = sems(K, "transposed", "even_copied", "odd_copied")
    with K.nc.Block() as block:
        @block.tensor
        def _(pe):
            for u, (dst, srcs) in enumerate(units):
                if u >= 8:
                    pe.wait_ge((s_act, s_dve)[u % 2], (u - 8) // 2 + 1)
                for j, src in enumerate(srcs):
                    k, m = src.shape
                    tr = pe.transpose(K.ps[0:m, u % 8, j * k:(j + 1) * k], src, cst(K, "ident", k)[:, 0:k])
                tr.then_inc(s_tr, 1)

        @block.scalar
        def _(act):
            for u, (dst, srcs) in enumerate(units):
                if u % 2 == 0:
                    act.wait_ge(s_tr, u + 1)
                    act.activation(dst, K.ps[0:dst.shape[0], u % 8, 0:dst.shape[1]], ACT.Copy).then_inc(s_act, 1)

        @block.vector
        def _(dve):
            for u, (dst, srcs) in enumerate(units):
                if u % 2 == 1:
                    dve.wait_ge(s_tr, u + 1)
                    dve.tensor_copy(dst, K.ps[0:dst.shape[0], u % 8, 0:dst.shape[1]]).then_inc(s_dve, 1)


def token_ranges():
    return [(t, P, META + t * P) for t in range(TT)] + [(TT, META, 0)]


def project_conv(K, dst, taps):
    with ExitStack() as c:
        z = scratch(K, c, "z", [P, 2, T2 + 3])
        y = scratch(K, c, "y", [P, 2, T2])

        def head(dve):
            K.dve_chain.link(dve, dve.memset(z[:, :, 0:3], 0.0))

        def evac_act(act, ch, u, turn, b, s_free):
            s_conv, = evac["signals"]
            act.activation(z[:, u % 2, 3:].rearrange("p (a b) -> p a b", a=2), K.ps[:, b:b + 2, 0:HALF], ACT.Copy).then_inc(s_free, 1)
            act.wait_ge(s_conv, ch + 1)
            act.activation(dst[:, ds(ch, 1), :], y[:, u % 2].unsqueeze(1), ACT.Silu)

        def evac_dve(dve, ch, u, turn, b, s_free):
            s_conv, = evac["signals"]
            dve.wait_ge(s_free, ch + 3)
            yy, zz = y[:, u % 2], z[:, u % 2]
            K.dve_chain.link(dve, dve.tensor_scalar(yy, zz[:, 3:], taps[:, ds(ch, 1), 3], None, ALU.mult))
            for j in (2, 1):
                K.dve_chain.link(dve, dve.scalar_tensor_tensor(yy, zz[:, j:j + T2], taps[:, ds(ch, 1), j], yy, ALU.mult, ALU.add))
            dve.scalar_tensor_tensor(yy, zz[:, 0:T2], taps[:, ds(ch, 1), 0], yy, ALU.mult, ALU.add).then_inc(s_conv, 1)
        evac = {"frees": "act", "act": evac_act, "dve": evac_dve, "sems": ("convolved",), "head_dve": head,
                "table": ACT.Silu}
        product_cols(K, K.at, 8, None, None, [(K.nx_hi, K.nx_lo, FULL)], evac, dve_links=3)
    K.at += 8


def project_plain(K, n, dst):
    def evac_act(act, ch, u, turn, b, s_free):
        act.activation(dst[:, ds(ch, 1), :].rearrange("p o (a b) -> p (o a) b", a=2), K.ps[:, b:b + 2, 0:HALF],
                       ACT.Copy).then_inc(s_free, 1)
    product_cols(K, K.at, n, None, None, [(K.nx_hi, K.nx_lo, FULL)], {"frees": "act", "act": evac_act})
    K.at += n



def delta_gates(K, S):
    with ExitStack() as c:
        abT = scratch(K, c, "ab_cols", [P, 1, T2])
        ab = scratch(K, c, "ab_rows", [P, 5, 16])
        xa = scratch(K, c, "xa", [P, 5, 8])
        e1 = scratch(K, c, "e1", [P, 5, 8])
        ea = scratch(K, c, "exp_a_log", [P, 8])
        project_plain(K, 1, abT)
        s_tr, s_x, s_ln, s_ea, s_g, s_cum, s_e = sems(K, "transposed", "logits", "ln", "betas", "g", "cums", "exps")
        with K.nc.Block() as block:
            @block.tensor
            def _(pe):
                for t, rows, a in token_ranges():
                    tr = pe.transpose(K.ps[0:rows, 0, 16 * t:16 * t + 16], abT[0:16, 0, a:a + rows], cst(K, "ident", 16)[:, 0:16])
                tr.then_inc(s_tr, 1)
                pe.wait_ge(s_g, 1)
                for t, rows, a in token_ranges():
                    g = S.g[0:rows, t, :]
                    pe.matmul(K.ps[0:rows, 1, 8 * t:8 * t + 8], cst(K, "tri_incl", rows)[:, 0:rows], g, start=True, stop=True)
                    pe.matmul(K.ps[0:rows, 2, 8 * t:8 * t + 8], cst(K, "tri_after", rows)[:, 0:rows], g, start=True, stop=True)
                    for ck in range(2 if rows == P else 1):
                        mm = pe.matmul(K.ps[:, 3, 16 * t + 8 * ck:16 * t + 8 * ck + 8],
                                       cst(K, "chunk_ones", rows)[:, P * ck:P * ck + P], g, start=True, stop=True)
                mm.then_inc(s_cum, 1)

            @block.vector
            def _(dve):
                ch = K.dve_chain
                ch.link(dve, dve.memset(ab[:], 0.0))
                dve.memset(S.eg[:], 0.0)
                dve.memset(S.beg[:], 0.0)
                ch.link(dve, dve.memset(S.g_cum[:], 0.0))
                dve.wait_ge(s_tr, 1)
                dve.tensor_copy(ab[:, 0:4].rearrange("p a b -> p (a b)"), K.ps[:, 0, 0:64])
                ch.link(dve, dve.tensor_copy(ab[0:META, 4], K.ps[0:META, 0, 64:80]))
                dve.tensor_tensor(xa[:], ab[:, :, 0:8], bc(par(K, "dt_bias"), [P, 5, 8], 1), ALU.add).then_inc(s_x, 1)
                dve.wait_ge(s_ln, 1)
                ch.link(dve, dve.scalar_tensor_tensor(xa.rearrange("p a b -> p (a b)"), xa.rearrange("p a b -> p (a b)"), 0.0,
                                                      e1.rearrange("p a b -> p (a b)"), ALU.max, ALU.add))
                dve.scalar_tensor_tensor(S.g[:], xa[:], -1.0, bc(ea[:], [P, 5, 8], 1), ALU.mult, ALU.mult).then_inc(s_g, 1)
                dve.wait_ge(s_cum, 1)
                dve.tensor_copy(S.g_cum[:, 0:4].rearrange("p a b -> p (a b)"), K.ps[:, 1, 0:32])
                dve.tensor_copy(S.g_cum[0:META, 4], K.ps[0:META, 1, 32:40]).then_inc(s_x, 1)
                dve.wait_ge(s_e, 1)
                dve.tensor_tensor(S.beg[:], S.eg[:], S.beta[:], ALU.mult)

            @block.scalar
            def _(act):
                ch = K.act_chain
                act.wait_ge(s_x, 1)
                ch.link(act, act.activation(e1[:], xa[:], ACT.Abs))
                ch.link(act, act.activation(e1[:], e1[:], ACT.Exp, scale=-1.0))
                act.activation(e1[:], e1[:], ACT.Ln, bias=1.0)
                act.activation(ea[:], par(K, "a_log"), ACT.Exp).then_inc(s_ln, 1)
                act.activation(S.beta[:], ab[:, :, 8:16], ACT.Sigmoid)
                act.wait_ge(s_x, 2)
                act.activation(S.eg[:], S.g_cum[:], ACT.Exp)
                act.activation(S.ea[:, 0:4].rearrange("p a b -> p (a b)"), K.ps[:, 2, 0:32], ACT.Exp)
                act.activation(S.ea[0:META, 4], K.ps[0:META, 2, 32:40], ACT.Exp)
                act.activation(S.egl[:, 0:4].rearrange("p a b c -> p (a b c)"), K.ps[:, 3, 0:64], ACT.Exp)
                act.activation(S.egl[:, 4, 0], K.ps[:, 3, 64:72], ACT.Exp).then_inc(s_e, 1)


DS_BANK = (5, 5, 0, 0)
SIDE_META = {"ug": 4, "lower": 20, "a_sb": 6, "x2_sb": 6, "a4_sb": 6, "x8_sb": 6, "r_sb": 8, "u_sb": 8}
SIDE_X = {"ug": 4, "lower": 20, "a_sb": 5, "x2_sb": 5, "a4_sb": 5, "x8_sb": 5, "r_sb": 4, "k_sb": 4, "k2_sb": 3, "y_sb": 4,
          "w_sb": 3, "u_sb": 4, "state 0": 3, "vn 0": 4, "state 1": 3, "vn 1": 4}
SIDE_POINTS = list(SIDE_META.items()) + TT * list(SIDE_X.items())
SIDE_CHUNK = 3 * KT


class Side:

    def __init__(self, first, n, dst, s_out):
        self.first, self.n, self.dst, self.s_out = first, n, dst, s_out
        total = sum(w for _, w in SIDE_POINTS)
        ends = np.cumsum([w for _, w in SIDE_POINTS]) * (n * SIDE_CHUNK) // total
        self.ends = [0] + [int(e) for e in ends]
        self.at = {"pe": 0, "act": 0, "dve": 0}

    def advance(self, engine, point):
        i = self.at[engine]
        assert SIDE_POINTS[i][0] == point, (engine, point, SIDE_POINTS[i])
        self.at[engine] += 1
        return self.ends[i], self.ends[i + 1]

    def chunks(self, a, b):
        return range(a // SIDE_CHUNK, b // SIDE_CHUNK)


def side_matmuls(K, pe, side, a, b):
    for i in range(a, b):
        c, j = divmod(i, SIDE_CHUNK)
        kt, which = divmod(j, 3)
        s = side.first + c
        if j == 0:
            pe.wait_ge(K.s_lo, s + 1)
            if c >= 2:
                pe.wait_ge(side.s_out, c - 1)
        w = (K.whi, K.whi, K.wlo)[which][:, s % HL, kt * P:(kt + 1) * P]
        x = (K.nx_hi, K.nx_lo, K.nx_hi)[which][:, kt, META:T2]
        mm = pe.matmul(K.ps[:, 6 + c % 2, :], w, x, start=j == 0, stop=j == SIDE_CHUNK - 1, skip_group_check=True)
        if j == SIDE_CHUNK - 1:
            mm.then_inc(K.s_used, 1)
    assert b - a < SIDE_CHUNK


def delta_rule(K, S, grp, n_side, dst):
    first = K.at
    names = ("tile_done", "ug", "gb", "kk", "caps", "exps", "lower", "pooled", "a_t", "a_sb", "r1", "p2", "a2_sb", "x2_sb",
             "p4", "a4_sb", "x4_sb", "p8", "x8_sb", "r3", "p16", "r_sb", "k_t", "k_sb", "kt_sb", "k2", "k2_sb", "y_t", "y_sb",
             "w", "w_sb", "u", "u_sb", "nw", "vs", "vn", "ds", "state", "o", "o_sb", "side_out")
    z = dict(zip(names, sems(K, *names)))
    fill = Side(first, n_side, dst, z["side_out"])
    tiles = [token_ranges()[-1]] + token_ranges()[:-1]
    H4 = range(HG)
    hd = slice(HG * grp, HG * grp + HG)
    with ExitStack() as c:
        def buf(name, n=P):
            return scratch(K, c, name, [P, HG, n])
        ug, dt, qd, lw, x1, a1, rr, x2, a2, x4, a4, at, kd, nw = [buf(n) for n in (
            "ug", "decay_t", "q_dec", "lower", "x1", "a1", "r", "x2", "a2", "x4", "a4", "attn_t", "k_dec", "neg_w")]
        st = S.state

        def bank(b, rows, n):
            return K.ps[0:rows, b, 0:HG * n].rearrange("p (h c) -> p h c", h=HG)

        def wide(b, p0, p1):
            return K.ps[p0:p1, b:b + 2, :].rearrange("p a (h c) -> p (a h) c", h=2)

        def k_rows(s, t):
            return S.k[s, t].rearrange("p (h c) -> p h c", h=HG)

        def v_rows(s, t):
            return S.v[s, t].rearrange("p (h c) -> p h c", h=HG)

        def tb(ap, rows, n):
            return bc(ap, [rows, HG, n], 2)

        with K.nc.Block() as block:
            @block.sync
            def _(sp):
                load_chunks(K, sp, first, n_side)

            @block.tensor
            def _(pe):
                def side(*points):
                    for p in points:
                        side_matmuls(K, pe, fill, *fill.advance("pe", p))

                for n, (t, r, a) in enumerate(tiles):
                    x = n - 1
                    s = slice(0, r)

                    def four(b, lhs, rhs, w=r, **kw):
                        for h in H4:
                            mm = pe.matmul(bank(b, w, r)[:, h], lhs(h), rhs(h), start=True, stop=True)
                        return mm
                    side("ug")
                    pe.wait_ge(z["ug"], n + 1)
                    pe.matmul(K.ps[:, 0, 0:HG * r], cst(K, "ones", r), ug[s, :, 0:r], start=True, stop=True).then_inc(z["gb"], 1)
                    q, k = (lambda h: S.qk[:, h, a:a + r]), (lambda h: S.qk[:, HG + h, a:a + r])
                    if x >= 1:
                        pe.wait_ge(z["o_sb"], 2 * x)
                    mm = four(1, k, k)
                    if x >= 0:
                        mm = four(2, k, q)
                    mm.then_inc(z["kk"], 1)
                    side("lower")
                    pe.wait_ge(z["lower"], n + 1)
                    for h in H4:
                        mm = pe.transpose(bank(3, r, r)[:, h], x1[s, h, 0:r], cst(K, "ident", r)[:, 0:r])
                    mm.then_inc(z["a_t"], 1)
                    A, X, A2, X2, A4, X4, R = [(lambda h, v=v: v[s, h, 0:r]) for v in (a1, x1, a2, x2, a4, x4, rr)]
                    side("a_sb")
                    pe.wait_ge(z["a_sb"], n + 1)
                    four(4, X, A)
                    four(5, A, X).then_inc(z["p2"], 1)
                    side("x2_sb")
                    pe.wait_ge(z["a2_sb"], n + 1)
                    pe.wait_ge(z["x2_sb"], n + 1)
                    four(0, X2, A2)
                    four(1, A2, X2)
                    pe.wait_ge(z["r1"], n + 1)
                    four(3, X2, R).then_inc(z["p4"], 1)
                    side("a4_sb")
                    pe.wait_ge(z["a4_sb"], n + 1)
                    pe.wait_ge(z["x4_sb"], n + 1)
                    four(4, A4, X4)
                    four(5, X4, R).then_inc(z["p8"], 1)
                    side("x8_sb")
                    pe.wait_ge(z["x8_sb"], n + 1)
                    pe.wait_ge(z["r3"], n + 1)
                    four(0, A, R).then_inc(z["p16"], 1)
                    side("r_sb")
                    pe.wait_ge(z["r_sb"], n + 1)
                    W = R
                    if x >= 0:
                        N = lambda h: lw[s, h, 0:r]
                        four(1, R, N)
                        four(3, N, R)
                        for h in H4:
                            mm = pe.transpose(bank(4, r, r)[:, h], R(h), cst(K, "ident", r)[:, 0:r])
                        mm.then_inc(z["k_t"], 1)
                        side("k_sb")
                        pe.wait_ge(z["k_sb"], x + 1)
                        pe.wait_ge(z["kt_sb"], x + 1)
                        four(5, X2, A2).then_inc(z["k2"], 1)
                        side("k2_sb")
                        pe.wait_ge(z["k2_sb"], x + 1)
                        four(0, A4, X4).then_inc(z["y_t"], 1)
                        side("y_sb")
                        pe.wait_ge(z["y_sb"], x + 1)
                        four(1, X, X4).then_inc(z["w"], 1)
                        side("w_sb")
                        pe.wait_ge(z["w_sb"], x + 1)
                        W = A
                    pe.wait_ge(z["pooled"], n + 1)
                    for h in H4:
                        mm = pe.matmul(wide(0, 0, r)[:, h], W(h), v_rows(s, t)[:, h], start=True, stop=True)
                    if x >= 0:
                        mm = four(2, lambda h: k_rows(s, t)[:, h], W, w=P)
                    mm.then_inc(z["u"], 1)
                    side("u_sb")
                    pe.wait_ge(z["u_sb"], n + 1)
                    if x < 0:
                        for h in H4:
                            mm = pe.matmul(wide(3, 0, P)[:, h], kd[s, h], v_rows(s, t)[:, h], start=True, stop=True)
                        mm.then_inc(z["ds"], 1)
                        continue
                    pe.wait_ge(z["nw"], x + 1)
                    for ck in range(2):
                        m, r0 = 2 * x + ck, CH * ck
                        c0 = slice(r0, r0 + CH)
                        side(f"state {ck}")
                        pe.wait_ge(z["state"], m + 1)
                        for h in H4:
                            mm = pe.matmul(wide(3, r0, r0 + CH)[:, h], nw[:, h, c0], st[:, h], start=True, stop=True)
                        mm.then_inc(z["vs"], 1)
                        if m >= 1:
                            pe.wait_ge(z["o_sb"], m)
                        for h in H4:
                            pe.matmul(wide(1, r0, r0 + CH)[:, h], qd[:, h, c0], st[:, h], start=h % 2 == 0, stop=False,
                                      skip_group_check=True)
                        side(f"vn {ck}")
                        pe.wait_ge(z["vn"], m + 1)
                        for h in H4:
                            mm = pe.matmul(K.ps[:, DS_BANK[h], 256 * (h % 2):256 * (h % 2) + 256], kd[c0, h], v_rows(c0, t)[:, h],
                                           start=True, stop=True)
                        mm.then_inc(z["ds"], 1)
                        for h in H4:
                            mm = pe.matmul(wide(1, r0, r0 + CH)[:, h], at[c0, h, c0], v_rows(c0, t)[:, h], start=False, stop=True,
                                           skip_group_check=True)
                        mm.then_inc(z["o"], 1)

            @block.vector
            def _(dve):
                ch = K.dve_chain

                def side(*points):
                    for p in points:
                        for c in fill.chunks(*fill.advance("dve", p)):
                            guarded(K, first, split_lo)(dve, c, first + c, 0)

                for n, (t, r, a) in enumerate(tiles):
                    x, s = n - 1, slice(0, r)
                    ident4 = bc(cst(K, "ident", r)[:, 0:r], [r, HG, r], 1)

                    def v4(b):
                        return b[s, :, 0:r]
                    if x >= 1:
                        dve.wait_ge(z["o"], 2 * x)
                    tri = bc(cst(K, "tri_incl", r)[:, 0:r], [r, HG, r], 1)
                    dve.tensor_tensor(v4(ug), tri, tb(S.g[s, t, hd], r, r), ALU.mult).then_inc(z["ug"], 1)
                    dve.wait_ge(z["gb"], n + 1)
                    ch.link(dve, dve.tensor_tensor(v4(ug), bank(0, r, r), tb(S.g_cum[s, t, hd], r, r), ALU.subtract))
                    cap = bc(cst(K, "cap_incl", r)[:, 0:r], [r, HG, r], 1)
                    ch.link(dve, dve.tensor_tensor(v4(dt), v4(ug), cap, ALU.min))
                    cap = bc(cst(K, "cap_strict", r)[:, 0:r], [r, HG, r], 1)
                    dve.scalar_tensor_tensor(v4(ug), v4(ug), -1.0, cap, ALU.mult, ALU.min).then_inc(z["caps"], 1)
                    dve.wait_ge(z["exps"], n + 1)
                    dve.wait_ge(z["kk"], n + 1)
                    for h in H4:
                        hh = HG * grp + h
                        last = dve.scalar_tensor_tensor(lw[s, h, 0:r], bank(1, r, r)[:, h], S.beta[s, t, hh:hh + 1], ug[s, h, 0:r],
                                                        ALU.mult, ALU.mult)
                    ch.link(dve, last)
                    same = bc(cst(K, "same16", r)[:, 0:r], [r, HG, r], 1)
                    dve.tensor_tensor(v4(x1), v4(lw), same, ALU.mult).then_inc(z["lower"], 1)
                    if x >= 0:
                        dve.wait_ge(z["lower"], n + 1)
                        dve.tensor_tensor(v4(lw), v4(lw), v4(x1), ALU.subtract)
                        dve.tensor_tensor(v4(at), bank(2, r, r), v4(dt), ALU.mult)
                    if x == 0:
                        side("u_sb")
                    side("ug")
                    dve.wait_ge(z["a_sb"], n + 1)
                    dve.scalar_tensor_tensor(v4(rr), v4(a1), -1.0, ident4, ALU.mult, ALU.add).then_inc(z["r1"], 1)
                    dve.wait_ge(z["p2"], n + 1)
                    dve.tensor_copy(v4(x2), bank(5, r, r)).then_inc(z["x2_sb"], 1)
                    side("lower", "a_sb")
                    dve.wait_ge(z["p4"], n + 1)
                    dve.tensor_tensor(v4(rr), v4(rr), bank(3, r, r), ALU.add)
                    dve.tensor_copy(v4(x4), bank(1, r, r)).then_inc(z["x4_sb"], 1)
                    side("x2_sb")
                    dve.wait_ge(z["p8"], n + 1)
                    dve.tensor_tensor(v4(rr), v4(rr), bank(5, r, r), ALU.add).then_inc(z["r3"], 1)
                    side("a4_sb")
                    dve.wait_ge(z["p16"], n + 1)
                    dve.tensor_tensor(v4(rr), v4(rr), bank(0, r, r), ALU.add).then_inc(z["r_sb"], 1)
                    if x >= 0:
                        dve.wait_ge(z["k_t"], x + 1)
                        ch.link(dve, dve.tensor_copy(v4(x2), bank(3, r, r)))
                        dve.scalar_tensor_tensor(v4(x4), v4(x2), -1.0, ident4, ALU.mult, ALU.add).then_inc(z["kt_sb"], 1)
                        side("x8_sb", "r_sb")
                        dve.wait_ge(z["y_t"], x + 1)
                        dve.tensor_tensor(v4(x4), v4(x4), bank(0, r, r), ALU.add).then_inc(z["y_sb"], 1)
                        side("k_sb")
                        dve.wait_ge(z["u"], n + 1)
                        dve.tensor_scalar(nw[:], bank(2, P, r), -1.0, None, ALU.mult).then_inc(z["nw"], 1)
                        side("k2_sb", "y_sb", "w_sb")
                        for ck in range(2):
                            m, r0 = 2 * x + ck, CH * ck
                            c0 = slice(r0, r0 + CH)
                            dve.wait_ge(z["vs"], m + 1)
                            dve.wait_ge(z["u_sb"], n + 1)
                            dve.tensor_tensor(v_rows(c0, t), wide(3, r0, r0 + CH), v_rows(c0, t), ALU.add).then_inc(z["vn"], 1)
                            dve.wait_ge(z["ds"], m + 2)
                            for h in H4:
                                hh = HG * grp + h
                                last = dve.scalar_tensor_tensor(
                                    st[:, h], st[:, h], S.egl[:, t, ck, hh:hh + 1],
                                    K.ps[:, DS_BANK[h], 256 * (h % 2):256 * (h % 2) + 256], ALU.mult, ALU.add)
                            last.then_inc(z["state"], 1)
                            dve.wait_ge(z["state"], m + 2)
                            side(*(("u_sb",) if ck == 0 else ()), f"state {ck}", f"vn {ck}")
                    else:
                        dve.wait_ge(z["ds"], 1)
                        dve.tensor_copy(st[:], wide(3, 0, P)).then_inc(z["state"], 1)
                        dve.wait_ge(z["state"], 1)
                        side("x8_sb", "r_sb")

            @block.scalar
            def _(act):
                def side(*points):
                    for p in points:
                        for c in fill.chunks(*fill.advance("act", p)):
                            guarded(K, first, split_hi)(act, c, first + c, 0)
                            act.wait_ge(K.s_used, first + c + 1)
                            act.activation(fill.dst[:, c], K.ps[:, 6 + c % 2, :], ACT.Copy).then_inc(fill.s_out, 1)

                for n, (t, r, a) in enumerate(tiles):
                    x, s = n - 1, slice(0, r)

                    def v4(b):
                        return b[s, :, 0:r]
                    act.wait_ge(z["caps"], n + 1)
                    act.activation(v4(dt), v4(dt), ACT.Exp)
                    act.activation(qd[:, :, 0:r], bank(0, P, r), ACT.Exp)
                    act.activation(v4(ug), v4(ug), ACT.Exp).then_inc(z["exps"], 1)
                    if x == 0:
                        side("u_sb")
                    side("ug")
                    for sig, dst, b, done, points in (
                            ("a_t", a1, 3, "a_sb", ("lower",)), ("p2", a2, 4, "a2_sb", ("a_sb",)),
                            ("p4", a4, 0, "a4_sb", ("x2_sb",)), ("p8", a1, 4, "x8_sb", ("a4_sb",))):
                        act.wait_ge(z[sig], n + 1)
                        act.activation(v4(dst), bank(b, r, r), ACT.Copy).then_inc(z[done], 1)
                        side(*points)
                    if x >= 0:
                        act.wait_ge(z["k_t"], x + 1)
                        act.activation(v4(a2), bank(1, r, r), ACT.Copy)
                        act.activation(v4(x1), bank(4, r, r), ACT.Copy).then_inc(z["k_sb"], 1)
                        side("x8_sb", "r_sb")
                        act.wait_ge(z["k2"], x + 1)
                        act.activation(v4(a4), bank(5, r, r), ACT.Copy).then_inc(z["k2_sb"], 1)
                        side("k_sb")
                        act.wait_ge(z["w"], x + 1)
                        act.activation(v4(a1), bank(1, r, r), ACT.Copy).then_inc(z["w_sb"], 1)
                        side("k2_sb", "y_sb")
                    act.wait_ge(z["u"], n + 1)
                    act.activation(v_rows(s, t), wide(0, 0, r), ACT.Copy).then_inc(z["u_sb"], 1)
                    if x >= 0:
                        side("w_sb")
                        for ck in range(2):
                            m, c0 = 2 * x + ck, slice(CH * ck, CH * ck + CH)
                            act.wait_ge(z["o"], m + 1)
                            act.activation(v_rows(c0, t), wide(1, CH * ck, CH * ck + CH), ACT.Copy).then_inc(z["o_sb"], 1)
                            side(*(("u_sb",) if ck == 0 else ()), f"state {ck}", f"vn {ck}")
                    else:
                        side("x8_sb", "r_sb")

            @block.gpsimd
            def _(pool):
                for n, (t, r, a) in enumerate(tiles):
                    x, s = n - 1, slice(0, r)
                    if x == 0:
                        pool.wait_ge(z["ds"], 1)
                    if x >= 1:
                        pool.wait_ge(z["o"], 2 * x)
                    k4, v4_ = k_rows(s, t), v_rows(s, t)
                    K.pool_chain.link(pool, pool.tensor_tensor(kd[s], k4, tb(S.ea[s, t, hd], r, P), ALU.mult))
                    pool.tensor_tensor(k4, k4, tb(S.beg[s, t, hd], r, P), ALU.mult)
                    last = pool.tensor_tensor(v4_, v4_, tb(S.beta[s, t, hd], r, DN_V), ALU.mult)
                    if x >= 0:
                        pool.wait_ge(z["exps"], n + 1)
                        last = pool.tensor_tensor(qd[:], qd[:], S.qk[:, 0:HG, a:a + r], ALU.mult)
                    last.then_inc(z["pooled"], 1)
    K.at += n_side


def delta_output(K, S, o_hi, o_lo, dz):
    s_sq, s_ss, s_rt, s_on, s_tr, s_y, s_hi = sems(K, "squares", "sums", "roots", "normed", "transposed", "gated", "hi")
    o = S.v
    with ExitStack() as c:
        sq = scratch(K, c, "sq", [P, TT, 1024])
        ss = scratch(K, c, "ss", [P, 32])
        y = scratch(K, c, "gated", [P, 2, SEQ])
        with K.nc.Block() as block:
            @block.vector
            def _(dve):
                ch = K.dve_chain
                for t in range(TT):
                    dve.wait_ge(s_sq, t + 1)
                    last = dve.tensor_reduce(ss[:, 4 * t:4 * t + 4], sq[:, t].rearrange("p (h c) -> p h c", c=DN_V), AX.X, ALU.add)
                ch.link(dve, last)
                dve.tensor_scalar(ss[:, 0:16], ss[:, 0:16], 1.0 / DN_V, EPS, ALU.mult, ALU.add).then_inc(s_ss, 1)
                dve.wait_ge(s_rt, 1)
                ch.link(dve, dve.reciprocal(ss[:, 16:32], ss[:, 16:32]))
                for t in range(TT):
                    ot = o[:, t].rearrange("p (h c) -> p h c", c=DN_V)
                    dve.tensor_tensor(ot, ot, bc(ss[:, 16 + 4 * t:20 + 4 * t], [P, 4, DN_V], 2), ALU.mult).then_inc(s_on, 1)
                for f in range(9):
                    if f < 8:
                        dve.wait_ge(s_tr, f + 1)
                        dve.scalar_tensor_tensor(y[:, f % 2], K.ps[:, f], par(K, "dn_gain")[:, f % 2:f % 2 + 1], dz[:, f],
                                                 ALU.mult, ALU.mult).then_inc(s_y, 1)
                    if f >= 1:
                        dve.wait_ge(s_hi, f)
                        ch.link(dve, dve.tensor_tensor(o_lo[:, f - 1], y[:, (f - 1) % 2], o_hi[:, f - 1].bitcast(F32), ALU.subtract))

            @block.scalar
            def _(act):
                for t in range(TT):
                    act.activation(sq[:, t], o[:, t], ACT.Square).then_inc(s_sq, 1)
                act.activation(dz[:], dz[:], ACT.Silu)
                act.preload_act_table(ACT.Sqrt)
                act.wait_ge(s_ss, 1)
                act.activation(ss[:, 16:32], ss[:, 0:16], ACT.Sqrt).then_inc(s_rt, 1)
                for f in range(8):
                    act.wait_ge(s_y, f + 1)
                    act.activation(o_hi[:, f], y[:, f % 2], ACT.Copy).then_inc(s_hi, 1)

            @block.tensor
            def _(pe):
                for f in range(8):
                    for t in range(TT):
                        if f == 0:
                            pe.wait_ge(s_on, t + 1)
                        tr = pe.transpose(K.ps[:, f, t * P:(t + 1) * P], o[:, t, f * P:(f + 1) * P], cst(K, "ident"))
                    tr.then_inc(s_tr, 1)



def merge_pairs(K, o_hi, o_lo, pre, out_hi=None, out_lo=None):
    with ExitStack() as c:
        g = scratch(K, c, "gate", [P, 2, SEQ])
        y = scratch(K, c, "y", [P, 2, SEQ])

        def evac_act(act, ch, u, turn, b, s_free):
            s_sig, s_sum, s_hi = evac["signals"]
            kind, pb, pair = u % 2, u // 2 % 2, turn * 2 + u // 2
            if kind == 0:
                act.activation(g[:, pb], K.ps[:, b, :], ACT.Sigmoid).then_inc(s_sig, 1)
            elif out_hi is not None:
                act.wait_ge(s_sum, pair + 1)
                act.activation(out_hi[:, ds(pair, 1), :], y[:, pb].unsqueeze(1), ACT.Copy).then_inc(s_hi, 1)

        def evac_dve(dve, ch, u, turn, b, s_free):
            s_sig, s_sum, s_hi = evac["signals"]
            kind, pb, pair = u % 2, u // 2 % 2, turn * 2 + u // 2
            yy, p1 = y[:, pb].unsqueeze(1), pre[:, ds(pair, 1), :]
            if kind == 0:
                dve.wait_ge(s_sig, pair + 1)
                dve.nop().then_inc(s_free, 1)
                return
            ps = K.ps[:, b:b + 1, :]
            if out_hi is None:
                dve.tensor_tensor(yy, ps, p1, ALU.add).then_inc(s_free, 1)
                dve.wait_ge(s_free, ch + 3)
                dve.tensor_tensor(p1, yy, g[:, pb].unsqueeze(1), ALU.mult).then_inc(s_sum, 1)
            else:
                dve.tensor_tensor(yy, ps, g[:, pb].unsqueeze(1), ALU.mult).then_inc(s_free, 1)
                dve.wait_ge(s_free, ch + 3)
                dve.tensor_tensor(yy, yy, p1, ALU.add).then_inc(s_sum, 1)
                dve.wait_ge(s_hi, pair + 1)
                dve.tensor_tensor(out_lo[:, ds(pair, 1), :], yy, out_hi[:, ds(pair, 1), :].bitcast(F32), ALU.subtract)
        evac = {"frees": "dve", "act": evac_act, "dve": evac_dve, "table": ACT.Sigmoid,
                "sems": ("sigmoid", "summed", "hi")}
        product_cols(K, K.at, 16, None, None, [(K.nx_hi, K.nx_lo, [(META, T2)]), (o_hi, o_lo, [(0, SEQ)])], evac)
    K.at += 16



def stick_breaking(K, qT, kT, v):
    s_z, s_ln, s_sp, s_r, s_c, s_w, s_pv, s_o = sems(
        K, "z", "ln", "softplus", "later", "log_w", "w", "pv", "o")
    units = [(h, a) for h in range(SB_H) for a in (3, 2, 1, 0, 4)]
    NU = len(units)

    def geo(u):
        h, a = units[u]
        return (h, a, P, a * P, META + a * P, SEQ - a * P) if a < TT else (h, a, META, 0, 0, SEQ)
    with ExitStack() as c:
        az, sp, w = [scratch(K, c, n, [P, 3, SEQ]) for n in ("abs_z", "softplus", "w")]
        rs = scratch(K, c, "later_sum", [P, 2, SEQ])
        with K.nc.Block() as block:
            @block.tensor
            def _(pe):
                def z_product(u):
                    h, a, r, q0, k0, n = geo(u)
                    if u >= 6:
                        pe.wait_ge(s_w, u - 5)
                    out = K.ps[0:r, u % 6, 0:n]
                    if a == 3 and h >= 1:
                        pass
                    mm = pe.matmul(out, kT[:, h, k0:k0 + r], qT[:, h, META + q0:T2], start=True, stop=a == TT, skip_group_check=True)
                    if a < TT:
                        mm = pe.matmul(out[:, 0:P], cst(K, "ident"), cst(K, "sb_mask"), start=False, stop=True, skip_group_check=True)
                    mm.then_inc(s_z, 1)

                def later_sums(u):
                    h, a, r, q0, k0, n = geo(u)
                    pe.wait_ge(s_sp, u + 1)
                    mm = pe.matmul(K.ps[0:r, u % 6, 0:n], cst(K, "neg_from", r)[:, 0:r], sp[0:r, u % 3, 0:n],
                                   start=False, stop=a == 3, skip_group_check=True)
                    if a != 3:
                        pe.wait_ge(s_r, u - u // 5)
                        off = P if a < TT else 0
                        mm = pe.matmul(K.ps[0:r, u % 6, off:n], cst(K, "neg_ones")[:, 0:r], rs[:, u % 5 % 2, q0 + off:SEQ],
                                       start=False, stop=True, skip_group_check=True)
                    mm.then_inc(s_c, 1)

                def values(u):
                    h, a, r, q0, k0, n = geo(u)
                    pe.wait_ge(s_w, u + 1)
                    if a == 3 and h >= 2:
                        pe.wait_ge(s_o, h - 1)
                    pe.matmul(K.ps[:, 6 + h % 2, q0:SEQ], v[0:r, a, h * P:(h + 1) * P], w[0:r, u % 3, 0:n], start=a == 3,
                              stop=a == TT, skip_group_check=True).then_inc(s_pv, 1)
                for u in range(3):
                    z_product(u)
                for u in range(NU):
                    if u + 3 < NU:
                        z_product(u + 3)
                    later_sums(u)
                    if u >= 1:
                        values(u - 1)
                values(NU - 1)

            @block.vector
            def _(dve):
                def softplus(u):
                    h, a, r, q0, k0, n = geo(u)
                    dve.wait_ge(s_ln, u + 1)
                    if u >= 3:
                        dve.wait_ge(s_c, u - 2)
                        k = u - 3
                        dve.wait_ge(s_r, (k // 5) * 4 + min(k % 5, 3) + 1)
                    dve.scalar_tensor_tensor(sp[0:r, u % 3, 0:n], K.ps[0:r, u % 6, 0:n], 0.0, az[0:r, u % 3, 0:n],
                                             ALU.max, ALU.add).then_inc(s_sp, 1)
                for u in range(NU):
                    softplus(u)

            @block.scalar
            def _(act):
                def logs(u):
                    h, a, r, q0, k0, n = geo(u)
                    act.wait_ge(s_z, u + 1)
                    if u >= 3:
                        act.wait_ge(s_sp, u - 2)
                    b = az[0:r, u % 3, 0:n]
                    K.act_chain.link(act, act.activation(b, K.ps[0:r, u % 6, 0:n], ACT.Abs))
                    K.act_chain.link(act, act.activation(b, b, ACT.Exp, scale=-1.0))
                    act.activation(b, b, ACT.Ln, bias=1.0).then_inc(s_ln, 1)

                def weights(u):
                    h, a, r, q0, k0, n = geo(u)
                    act.wait_ge(s_c, u + 1)
                    if u >= 3:
                        act.wait_ge(s_pv, u - 2)
                    act.activation(w[0:r, u % 3, 0:n], K.ps[0:r, u % 6, 0:n], ACT.Exp).then_inc(s_w, 1)

                def copy_out(h):
                    act.wait_ge(s_pv, 5 * h + 5)
                    act.activation(qT[:, h, 0:SEQ], K.ps[:, 6 + h % 2, :], ACT.Copy).then_inc(s_o, 1)
                act.preload_act_table_set("natural_log_exp_and_others")
                logs(0)
                for u in range(NU):
                    if u + 1 < NU:
                        logs(u + 1)
                    weights(u)
                    if u >= 6 and u % 5 == 1:
                        copy_out(u // 5 - 1)
                copy_out(SB_H - 1)

            @block.gpsimd
            def _(pool):
                for u in range(NU):
                    h, a, r, q0, k0, n = geo(u)
                    if a == TT:
                        continue
                    i = u % 5
                    pool.wait_ge(s_sp, u + 1)
                    if u >= 1:
                        pool.wait_ge(s_c, u if i else u)
                    last = pool.tensor_copy(rs[:, (i + 1) % 2, q0:q0 + P], sp[:, u % 3, 0:P])
                    if a < 3:
                        last = pool.tensor_tensor(rs[:, (i + 1) % 2, q0 + P:SEQ], rs[:, i % 2, q0 + P:SEQ], sp[:, u % 3, P:n], ALU.add)
                    last.then_inc(s_r, 1)
                    pool.wait_ge(s_r, u - u // 5 + 1)


def split_stage(K, src, hi, lo, n):
    s_hi, = sems(K, "hi")
    with K.nc.Block() as block:
        @block.scalar
        def _(act):
            for i in range(n):
                act.activation(hi[:, i], src[:, i, 0:SEQ], ACT.Copy).then_inc(s_hi, 1)

        @block.vector
        def _(dve):
            for i in range(n):
                dve.wait_ge(s_hi, i + 1)
                dve.tensor_tensor(lo[:, i], src[:, i, 0:SEQ], hi[:, i].bitcast(F32), ALU.subtract)


def block2(K, v):
    norm_stage(K, v["mix_gain"], v["meta"])
    with ExitStack() as c:
        pre = scratch(K, c, "merged", [P, 8, SEQ])
        with ExitStack() as c2:
            S = Core()
            S.g, S.g_cum, S.eg, S.beg, S.ea, S.beta = [
                scratch(K, c2, n, [P, 5, 8]) for n in ("g", "g_cum", "exp_g", "beta_exp_g", "exp_after", "beta")]
            S.egl = scratch(K, c2, "egl", [P, 5, 2, 8])
            delta_gates(K, S)
            taps = par(K, "conv2").rearrange("p (g f t) -> p g f t", g=2, t=4)
            for grp in range(2):
                with ExitStack() as c3:
                    dz = pre if grp == 0 else scratch(K, c3, "dz", [P, 8, SEQ])
                    S.v = scratch(K, c3, "v_rows", [P, 5, 1024])
                    with ExitStack() as c4:
                        S.k = scratch(K, c4, "k_rows", [P, 5, 512])
                        S.qk = scratch(K, c4, "qk_cols", [P, 8, T2])
                        S.state = scratch(K, c4, "state", [P, HG, DN_V])
                        project_conv(K, S.qk, taps[:, grp, 0:8])
                        with ExitStack() as c5:
                            vT = scratch(K, c5, "v_cols", [P, 8, T2])
                            project_conv(K, vT, taps[:, grp, 8:16])
                            norm_cols(K, [(S.qk[:, i], None) for i in range(8)], EPS, "dn_scales")
                            units = []
                            for t, r, a in token_ranges():
                                for f in range(2):
                                    units.append((S.v[0:r, t, 512 * f:512 * f + 512], [vT[:, 4 * f + j, a:a + r] for j in range(4)]))
                                units.append((S.k[0:r, t, :], [S.qk[:, 4 + j, a:a + r] for j in range(4)]))
                            transpose_units(K, units)
                        delta_rule(K, S, grp, 8, dz)
                    with ExitStack() as c4:
                        o_hi, o_lo = [scratch(K, c4, n, [P, 8, SEQ], F32R) for n in ("o_hi", "o_lo")]
                        delta_output(K, S, o_hi, o_lo, dz)
                        if grp == 0:
                            product_cols(K, K.at, 8, None, None, [(o_hi, o_lo, [(0, SEQ)])], {
                                "frees": "act",
                                "act": lambda act, ch, u, turn, b, s_free: act.activation(
                                    pre[:, ds(ch, 1), :], K.ps[:, b:b + 1, :], ACT.Copy).then_inc(s_free, 1)})
                            K.at += 8
                        else:
                            merge_pairs(K, o_hi, o_lo, pre)
        with ExitStack() as c2:
            qT = scratch(K, c2, "sb_q", [P, SB_H, T2])
            with ExitStack() as c3:
                kT = scratch(K, c3, "sb_k", [P, SB_H, T2])
                v_rows = scratch(K, c3, "sb_v", [P, 5, 1024])
                project_plain(K, 8, qT)
                project_plain(K, 8, kT)
                with ExitStack() as c4:
                    vT = scratch(K, c4, "sb_vT", [P, SB_H, T2])
                    project_plain(K, 8, vT)
                    transpose_units(K, [(v_rows[0:r, t, 512 * f:512 * f + 512], [vT[:, 4 * f + j, a:a + r] for j in range(4)])
                                        for t, r, a in token_ranges() for f in range(2)])
                norm_cols(K, [(qT[:, i], par(K, "sbq_gain")) for i in range(8)]
                          + [(kT[:, i], par(K, "sbk_gain")) for i in range(8)], 128 * EPS, "sb_scales")
                stick_breaking(K, qT, kT, v_rows)
            o_hi, o_lo = [scratch(K, c2, n, [P, 8, SEQ], F32R) for n in ("o_hi", "o_lo")]
            split_stage(K, qT, o_hi, o_lo, 8)
            with ExitStack() as c3:
                m_hi, m_lo = [scratch(K, c3, n, [P, 8, SEQ], F32R) for n in ("m_hi", "m_lo")]
                merge_pairs(K, o_hi, o_lo, pre, m_hi, m_lo)
                product_rows(K, K.at, KT, m_hi, m_lo, None)
                K.at += KT
    norm_stage(K, v["ffn_gain_2"], None)
    with ExitStack() as c:
        act_hi, act_lo = scratch(K, c, "act_hi", [P, FT, SEQ], F32R), scratch(K, c, "act_lo", [P, FT, SEQ], F32R)
        ffn_up(K, act_hi, act_lo, False, 0)

        def finish(sp, s_added):
            out = v["out"].rearrange("b (t p) d -> p (b t) d", p=P)
            for t in range(TT):
                sp.wait_ge(s_added, t + 1)
                sp.dma_start(out[:, t], K.h[:, t]).then_inc(K.s_out, 16)
            sp.wait_ge(K.s_out, 16 * TT)
        product_rows(K, K.at, FT, act_hi, act_lo, finish)
        K.at += FT



def core_setup(nc, ctx, v, n_stream):
    K = Core()
    K.live, K.cleared, K.uid = [], [], 0
    K.nc, K.stage, K.at, K.stream, K.n_stream = nc, 0, 0, v["stream"], n_stream

    def sb(name, shape, dt=F32):
        return ctx.enter_context(nc.sbuf_tensor(name, shape, dt))

    K.ps = ctx.enter_context(nc.psum_tensor("ps", [P, 8, 512], F32))
    K.raw = sb("raw", [P, RAW, 1024])
    K.whi, K.wlo = sb("whi", [P, HL, 1024], F32R), sb("wlo", [P, HL, 1024], F32R)
    K.h = sb("h_sb", [P, TT, D])
    K.const, K.param = sb("const_sb", [P, CONST_COLS["of block 1"][0]]), sb("param_sb", [P, PARAM_N])
    K.nx_hi, K.nx_lo = sb("nx_hi", [P, KT, T2], F32R), sb("nx_lo", [P, KT, T2], F32R)
    K.s_out = ctx.enter_context(nc.semaphore("out_written"))
    K.t_ss, K.t_rs = sb("t_ss", [P, 8]), sb("t_rs", [P, 8])
    K.s_raw = [ctx.enter_context(nc.semaphore(f"raw_in_{i}")) for i in range(RAW)]
    K.s_hi, K.s_lo, K.s_used = [ctx.enter_context(nc.semaphore(n)) for n in ("hi_made", "lo_made", "chunk_used")]
    K.act_chain = Chain(ctx.enter_context(nc.semaphore("act_step")))
    K.dve_chain = Chain(ctx.enter_context(nc.semaphore("dve_step")))
    K.pool_chain = Chain(ctx.enter_context(nc.semaphore("pool_step")))
    return K


def scratch(K, ctx, name, shape, dt=F32):
    K.uid += 1
    return ctx.enter_context(K.nc.sbuf_tensor(f"{name}_{K.uid}", shape, dt))


def norm_stage(K, gain, meta):
    with ExitStack() as c:
        K.t_xn = scratch(K, c, "xn", [P, TT + 1, D])
        K.t_gain = scratch(K, c, "gain", [P, D])
        if meta is not None:
            K.hm = scratch(K, c, "h_meta", [META, D])
        norm_rows(K, gain, meta)


def program(nc, v):
    with ExitStack() as ctx:
        K = core_setup(nc, ctx, v, N_STREAM1 + N_STREAM2)
        start(K, v)
        block1(K, v)
        block2(K, v)



def kernel(**inputs):
    import concourse.bacc as bacc
    from concourse.bass_utils import run_bass_kernel_spmd

    v = {n: np.asarray(a) for n, a in inputs.items()}

    def rows(a):
        return np.ascontiguousarray(np.broadcast_to(a.reshape(1, -1), (P, a.size)))

    arrays = dict(
        x=v["x"], meta=v["meta_tokens_2"], stream=np.concatenate(stream1(v) + stream2(v)),
        const=const_array(), param=param_array(v),
        attn_gain=rows(v["attn_norm"][0]), ffn_gain=rows(v["ffn_norm"][0]),
        mix_gain=rows(v["norm_mix_gain_2"][0]), ffn_gain_2=rows(v["norm_ffn_gain_2"][0]),
        cmp_w1_k=v["cmp_w1_k"][0], cmp_w1_v=v["cmp_w1_v"][0],
    )
    arrays = {f"{n}_dram": np.ascontiguousarray(a) for n, a in arrays.items()}
    nc = bacc.Bacc("TRN2", target_bir_lowering=False, num_devices=1)
    args = {n.removesuffix("_dram"): nc.dram_tensor(n, a.shape, mybir.dt.from_np(a.dtype), kind="ExternalInput").ap()
            for n, a in arrays.items()}
    args["out"] = nc.dram_tensor("out_dram", (1, SEQ, D), F32, kind="ExternalOutput").ap()
    program(nc, args)
    result = run_bass_kernel_spmd(nc, [arrays], core_ids=[0])
    return result.results[0]["out_dram"]
```
